# Optimizing a Trainium2 kernel written in Bass

```python
import math
import jax, jax.numpy as jnp
from jax import lax
import numpy as np

D_MODEL = 1024
BATCH = 1
SEQ = 2048
DEPTH = 1
DEC_BATCH = 8
DEC_SEQ = 8
PAST_LEN = 16384
PAGE_SIZE = 128

D_MIX = D_MODEL
D_A = D_MIX // 2
D_B = D_MIX - D_A
HEAD_DIM_A = 128
N_HEADS_A = D_A // HEAD_DIM_A
CHUNK = 128
SSM_GROUP = 16
N_SSM_GROUPS = D_B // SSM_GROUP
SSM_STATE = 64
N_EXPERT_GROUPS = 4
EXPERTS_PER_GROUP = 8
N_EXPERTS = N_EXPERT_GROUPS * EXPERTS_PER_GROUP
TOP_K_INNER = 2
D_EXPERT = D_MODEL // 4
EXPERT_BLOCK = 128
EPS = 1e-6

kernel_name = 'hymba_gmlp_s5_hmoe_step'

def rms_norm(x, g):
    xf = x.astype(jnp.float32)
    y = xf * lax.rsqrt(jnp.mean(xf * xf, axis=-1, keepdims=True) + EPS)
    return (y * g.astype(jnp.float32)).astype(x.dtype)

def modulate(x, g, shift, scale):
    return rms_norm(x, g) * (1 + scale) + shift

def head_layer_norm(v, g, b):
    vf = v.astype(jnp.float32)
    mu = jnp.mean(vf, axis=-1, keepdims=True)
    var = jnp.mean(jnp.square(vf - mu), axis=-1, keepdims=True)
    y = (vf - mu) * lax.rsqrt(var + EPS)
    return (y * g.astype(jnp.float32) + b.astype(jnp.float32)).astype(v.dtype)

def chunk_spatial_mix(v, w_s, b_s):
    Bn, L, H, dh = v.shape
    n_chunks = -(-L // CHUNK)
    pad = n_chunks * CHUNK - L
    vp = jnp.pad(v, ((0, 0), (0, pad), (0, 0), (0, 0))).reshape(Bn, n_chunks, CHUNK, H, dh)
    mask = jnp.tril(jnp.ones((CHUNK, CHUNK), dtype=bool))[None]
    w = jnp.where(mask, w_s, jnp.zeros_like(w_s)).astype(v.dtype)
    out = jnp.einsum('hts,bcshd->bcthd', w, vp) + b_s.T.astype(v.dtype)[None, None, :, :, None]
    return out.reshape(Bn, n_chunks * CHUNK, H, dh)[:, :L]

def ssm_discretize(lam_re, lam_im, log_dt, b_re, b_im):
    dt = jnp.exp(log_dt.astype(jnp.float32))[:, None]
    lr = lam_re.astype(jnp.float32)
    li = lam_im.astype(jnp.float32)
    mag = jnp.exp(lr * dt)
    ar = mag * jnp.cos(li * dt)
    ai = mag * jnp.sin(li * dt)
    den = lr * lr + li * li
    cr = ((ar - 1) * lr + ai * li) / den
    ci = (ai * lr - (ar - 1) * li) / den
    br_, bi_ = b_re.astype(jnp.float32), b_im.astype(jnp.float32)
    br = cr[..., None] * br_ - ci[..., None] * bi_
    bi = cr[..., None] * bi_ + ci[..., None] * br_
    return ar, ai, br, bi

def ssm_combine(left, right):
    a1r, a1i, b1r, b1i = left
    a2r, a2i, b2r, b2i = right
    ar = a2r * a1r - a2i * a1i
    ai = a2r * a1i + a2i * a1r
    br = a2r * b1r - a2i * b1i + b2r
    bi = a2r * b1i + a2i * b1r + b2i
    return ar, ai, br, bi

def s5_mixer(xs, h0_re, h0_im, lam_re, lam_im, log_dt, b_re, b_im, c_re, c_im, d_skip, w_glu, b_glu):
    Bn, L, _ = xs.shape
    u = xs.astype(jnp.float32).reshape(Bn, L, N_SSM_GROUPS, SSM_GROUP)
    ar, ai, br, bi = ssm_discretize(lam_re, lam_im, log_dt, b_re, b_im)
    bu_re = jnp.einsum('blgh,gph->blgp', u, br)
    bu_im = jnp.einsum('blgh,gph->blgp', u, bi)
    h0r = h0_re.astype(jnp.float32)
    h0i = h0_im.astype(jnp.float32)
    bu_re = bu_re.at[:, 0].add(ar * h0r - ai * h0i)
    bu_im = bu_im.at[:, 0].add(ar * h0i + ai * h0r)
    a_re = jnp.broadcast_to(ar, bu_re.shape)
    a_im = jnp.broadcast_to(ai, bu_im.shape)
    _, _, h_re, h_im = lax.associative_scan(ssm_combine, (a_re, a_im, bu_re, bu_im), axis=1)
    y = (jnp.einsum('blgp,ghp->blgh', h_re, c_re.astype(jnp.float32))
         - jnp.einsum('blgp,ghp->blgh', h_im, c_im.astype(jnp.float32))
         + d_skip.astype(jnp.float32) * u)
    y = jax.nn.gelu(y.reshape(Bn, L, D_B))
    y = y * jax.nn.sigmoid(y @ w_glu.astype(jnp.float32) + b_glu.astype(jnp.float32))
    return y.astype(xs.dtype), h_re[:, -1].astype(h0_re.dtype), h_im[:, -1].astype(h0_im.dtype)

def hier_moe(x, w_group, b_group, w_expert, b_expert, w1, w3, w2):
    Bn, L, D = x.shape
    xt = x.reshape(-1, D)
    T = xt.shape[0]
    g_prob = jax.nn.softmax((xt @ w_group + b_group).astype(jnp.float32), axis=-1)
    g_w, g_idx = lax.top_k(g_prob, 1)
    e_logits = (xt @ w_expert + b_expert).astype(jnp.float32).reshape(T, N_EXPERT_GROUPS, EXPERTS_PER_GROUP)
    e_in = jnp.take_along_axis(e_logits, g_idx[:, :, None], axis=1)[:, 0]
    e_top, e_idx = lax.top_k(e_in, TOP_K_INNER)
    gate = g_w * jax.nn.softmax(e_top, axis=-1)
    expert = g_idx * EXPERTS_PER_GROUP + e_idx
    n_assign = T * TOP_K_INNER
    flat_e = expert.reshape(-1)
    flat_tok = jnp.repeat(jnp.arange(T), TOP_K_INNER)
    flat_g = gate.reshape(-1)
    order = jnp.argsort(flat_e)
    e_s, tok_s, g_s = flat_e[order], flat_tok[order], flat_g[order]
    counts = jnp.bincount(flat_e, length=N_EXPERTS)
    starts = jnp.cumsum(counts) - counts
    padded = (counts + EXPERT_BLOCK - 1) // EXPERT_BLOCK * EXPERT_BLOCK
    pend = jnp.cumsum(padded)
    pstarts = pend - padded
    dest = pstarts[e_s] + (jnp.arange(n_assign) - starts[e_s])
    n_blocks = (n_assign + N_EXPERTS * (EXPERT_BLOCK - 1) + EXPERT_BLOCK - 1) // EXPERT_BLOCK
    buf = jnp.zeros((n_blocks * EXPERT_BLOCK, D), x.dtype).at[dest].set(xt[tok_s])
    block_expert = jnp.clip(jnp.searchsorted(pend, jnp.arange(n_blocks) * EXPERT_BLOCK, side='right'), 0, N_EXPERTS - 1)

    def run_block(args):
        xb, e = args
        h = jax.nn.silu(xb @ w1[e]) * (xb @ w3[e])
        return h @ w2[e]

    yb = lax.map(run_block, (buf.reshape(n_blocks, EXPERT_BLOCK, D), block_expert))
    y_s = yb.reshape(-1, D)[dest].astype(jnp.float32)
    out = jnp.zeros((T, D), jnp.float32).at[tok_s].add(g_s[:, None] * y_s)
    return out.astype(x.dtype).reshape(Bn, L, D)

def trunk_layer(x, c, h0_re, h0_im, w_ada, b_ada, g_norm1, g_norm2, w_in, ln_g, ln_b, w_s, b_s,
                lam_re, lam_im, log_dt, ssm_b_re, ssm_b_im, ssm_c_re, ssm_c_im, ssm_d, w_glu, b_glu,
                w_out, w_group, b_group, w_expert, b_expert, w1, w3, w2):
    Bn, L, _ = x.shape
    ada = jax.nn.silu(c) @ w_ada + b_ada
    sh1, sc1, gt1, sh2, sc2, gt2 = jnp.split(ada[:, None, :], 6, axis=-1)
    h = modulate(x, g_norm1, sh1, sc1)
    proj = h @ w_in
    u = jax.nn.gelu(proj[..., :D_A])
    v = jax.nn.gelu(proj[..., D_A:2 * D_A]).reshape(Bn, L, N_HEADS_A, HEAD_DIM_A)
    s_in = proj[..., 2 * D_A:]
    v = head_layer_norm(v, ln_g, ln_b)
    a_out = u * chunk_spatial_mix(v, w_s, b_s).reshape(Bn, L, D_A)
    b_out, h_re, h_im = s5_mixer(s_in, h0_re, h0_im, lam_re, lam_im, log_dt, ssm_b_re, ssm_b_im,
                                 ssm_c_re, ssm_c_im, ssm_d, w_glu, b_glu)
    mix = jnp.concatenate([a_out, b_out], axis=-1) @ w_out
    x = x + gt1 * mix
    h = modulate(x, g_norm2, sh2, sc2)
    x = x + gt2 * hier_moe(h, w_group, b_group, w_expert, b_expert, w1, w3, w2)
    return x, h_re, h_im, v.reshape(Bn, L, D_A)

def setup_inputs(seed: int = 0) -> dict:
    key = jax.random.key(seed)
    ks = iter(jax.random.split(key, 40))
    f32 = jnp.float32

    def nrm(shape, scale):
        return jax.random.normal(next(ks), shape, f32) * scale

    x_prompt = nrm((BATCH, SEQ, D_MODEL), 1.0)
    x_sample = nrm((DEC_BATCH, DEC_SEQ, D_MODEL), 1.0)
    state_ssm_re = nrm((DEPTH, DEC_BATCH, N_SSM_GROUPS, SSM_STATE), 0.5)
    state_ssm_im = nrm((DEPTH, DEC_BATCH, N_SSM_GROUPS, SSM_STATE), 0.5)
    c_prompt = nrm((BATCH, D_MODEL), 1.0)
    c_sample = nrm((DEC_BATCH, D_MODEL), 1.0)
    w_ada = nrm((DEPTH, D_MODEL, 6 * D_MODEL), 0.5 * D_MODEL ** -0.5)
    b_ada = nrm((DEPTH, 6 * D_MODEL), 0.01)
    g_norm1 = 1.0 + nrm((DEPTH, D_MODEL), 0.02)
    g_norm2 = 1.0 + nrm((DEPTH, D_MODEL), 0.02)
    w_in = nrm((DEPTH, D_MODEL, 2 * D_A + D_B), D_MODEL ** -0.5)
    ln_g = 1.0 + nrm((DEPTH, N_HEADS_A, HEAD_DIM_A), 0.02)
    ln_b = nrm((DEPTH, N_HEADS_A, HEAD_DIM_A), 0.02)
    row_scale = (1.0 / jnp.sqrt(jnp.arange(1, CHUNK + 1, dtype=f32)))[:, None]
    w_s = nrm((DEPTH, N_HEADS_A, CHUNK, CHUNK), 1.0) * row_scale
    b_s = 1.0 + nrm((DEPTH, N_HEADS_A, CHUNK), 0.02)
    lam_re = -0.5 + nrm((DEPTH, N_SSM_GROUPS, SSM_STATE), 0.01)
    lam_im = jnp.pi * jnp.arange(SSM_STATE, dtype=f32) + nrm((DEPTH, N_SSM_GROUPS, SSM_STATE), 0.01)
    log_dt = jax.random.uniform(next(ks), (DEPTH, N_SSM_GROUPS), f32, math.log(0.001), math.log(0.1))
    ssm_b_re = nrm((DEPTH, N_SSM_GROUPS, SSM_STATE, SSM_GROUP), (2 * SSM_GROUP) ** -0.5)
    ssm_b_im = nrm((DEPTH, N_SSM_GROUPS, SSM_STATE, SSM_GROUP), (2 * SSM_GROUP) ** -0.5)
    ssm_c_re = nrm((DEPTH, N_SSM_GROUPS, SSM_GROUP, SSM_STATE), (2 * SSM_STATE) ** -0.5)
    ssm_c_im = nrm((DEPTH, N_SSM_GROUPS, SSM_GROUP, SSM_STATE), (2 * SSM_STATE) ** -0.5)
    ssm_d = nrm((DEPTH, N_SSM_GROUPS, SSM_GROUP), 1.0)
    w_glu = nrm((DEPTH, D_B, D_B), D_B ** -0.5)
    b_glu = nrm((DEPTH, D_B), 0.01)
    w_out = nrm((DEPTH, D_MIX, D_MODEL), D_MIX ** -0.5)
    w_group = nrm((DEPTH, D_MODEL, N_EXPERT_GROUPS), D_MODEL ** -0.5)
    b_group = nrm((DEPTH, N_EXPERT_GROUPS), 0.01)
    w_expert = nrm((DEPTH, D_MODEL, N_EXPERTS), D_MODEL ** -0.5)
    b_expert = nrm((DEPTH, N_EXPERTS), 0.01)
    w1 = nrm((DEPTH, N_EXPERTS, D_MODEL, D_EXPERT), D_MODEL ** -0.5)
    w3 = nrm((DEPTH, N_EXPERTS, D_MODEL, D_EXPERT), D_MODEL ** -0.5)
    w2 = nrm((DEPTH, N_EXPERTS, D_EXPERT, D_MODEL), D_EXPERT ** -0.5)
    g_final = 1.0 + nrm((D_MODEL,), 0.02)
    return {'x_prompt': x_prompt, 'x_sample': x_sample, 'state_ssm_re': state_ssm_re, 'state_ssm_im': state_ssm_im,
            'c_prompt': c_prompt, 'c_sample': c_sample, 'w_ada': w_ada, 'b_ada': b_ada,
            'g_norm1': g_norm1, 'g_norm2': g_norm2, 'w_in': w_in, 'ln_g': ln_g, 'ln_b': ln_b,
            'w_s': w_s, 'b_s': b_s, 'lam_re': lam_re, 'lam_im': lam_im, 'log_dt': log_dt,
            'ssm_b_re': ssm_b_re, 'ssm_b_im': ssm_b_im, 'ssm_c_re': ssm_c_re, 'ssm_c_im': ssm_c_im,
            'ssm_d': ssm_d, 'w_glu': w_glu, 'b_glu': b_glu, 'w_out': w_out,
            'w_group': w_group, 'b_group': b_group, 'w_expert': w_expert, 'b_expert': b_expert,
            'w1': w1, 'w3': w3, 'w2': w2, 'g_final': g_final}

def reference(x_prompt, x_sample, state_ssm_re, state_ssm_im, c_prompt, c_sample, w_ada, b_ada,
              g_norm1, g_norm2, w_in, ln_g, ln_b, w_s, b_s, lam_re, lam_im, log_dt,
              ssm_b_re, ssm_b_im, ssm_c_re, ssm_c_im, ssm_d, w_glu, b_glu, w_out,
              w_group, b_group, w_expert, b_expert, w1, w3, w2, g_final):
    xp, xs = x_prompt, x_sample
    p_re, p_im, s_re, s_im, s_v = [], [], [], [], []
    for l in range(DEPTH):
        lw = (w_ada[l], b_ada[l], g_norm1[l], g_norm2[l], w_in[l], ln_g[l], ln_b[l], w_s[l], b_s[l],
              lam_re[l], lam_im[l], log_dt[l], ssm_b_re[l], ssm_b_im[l], ssm_c_re[l], ssm_c_im[l], ssm_d[l],
              w_glu[l], b_glu[l], w_out[l], w_group[l], b_group[l], w_expert[l], b_expert[l],
              w1[l], w3[l], w2[l])
        h0 = jnp.zeros((xp.shape[0], N_SSM_GROUPS, SSM_STATE), state_ssm_re.dtype)
        xp, hr, hi, _ = trunk_layer(xp, c_prompt, h0, h0, *lw)
        p_re.append(hr)
        p_im.append(hi)
        xs, hr, hi, v = trunk_layer(xs, c_sample, state_ssm_re[l], state_ssm_im[l], *lw)
        s_re.append(hr)
        s_im.append(hi)
        s_v.append(v)
    y_prompt = rms_norm(xp, g_final)
    y_sample = rms_norm(xs, g_final)
    return (y_prompt, y_sample, jnp.stack(p_re), jnp.stack(p_im), jnp.stack(s_re), jnp.stack(s_im), jnp.stack(s_v))


_drawn_inputs = setup_inputs


def setup_inputs(seed=0):
    import zlib

    import numpy as np

    out = dict(_drawn_inputs(seed))
    spreads = {}
    factors = {'g_norm2': 5.924,
     'ln_g': 2.748,
     'ln_b': 2.873,
     'b_s': 8.0,
     'lam_re': 3.638,
     'b_glu': 8.0,
     'b_group': 8.0,
     'b_expert': 8.0,
     'g_final': 2.842}
    for name, (base, spread) in spreads.items():
        noise = np.random.default_rng([zlib.crc32(name.encode()), seed]).standard_normal(out[name].shape)
        drawn = base * np.exp(spread * noise) if base else spread * noise
        out[name] = __import__('jax').numpy.asarray(drawn.astype(out[name].dtype))
    for name, factor in factors.items():
        out[name] = (out[name] * factor).astype(out[name].dtype)
    return out
```

```python
from contextlib import ExitStack

import numpy as np
import concourse.bass as bass
from concourse import mybir

F32 = mybir.dt.float32
I32 = mybir.dt.int32
U32 = mybir.dt.uint32
ACT = mybir.ActivationFunctionType
ALU = mybir.AluOpType
AX = mybir.AxisListType
ds = bass.ds

P = 128
D = 1024
KD = D // P
SEQ = 2048
NSEQ = 8
DSEQ = 8
TP = SEQ // P
NS = NSEQ * DSEQ
NT = TP + 1
TOK = SEQ + NS
DA = 512
HEADS = 4
HD = 128
G = 32
GC = 16
ST = 64
PAIRS = G // 2
Q = 8
NCH = SEQ // Q
CH = NCH + NSEQ
EG = 4
EPG = 8
NE = EG * EPG
DE = 256
NR = EG + NE
NBLK = TOK * 2 // P + NE - 1
FULL = TOK * 2 // P
EPS = 1e-6
BIG = 1e30
RING = 4
TWO_PI = 2 * np.pi
MAGIC = 1.5 * 2 ** 23
PI_HI = float(np.float32(6.28125))
PI_MID = float(np.float32(np.float64(TWO_PI) - 6.28125))
PI_LO = float(TWO_PI - 6.28125 - PI_MID)


class Inputs:

    def __init__(self, t):
        self.x_prompt = t["x_prompt"]
        self.x_sample = t["x_sample"]
        self.state_ssm_re = t["state_ssm_re"]
        self.state_ssm_im = t["state_ssm_im"]
        self.c_prompt = t["c_prompt"]
        self.c_sample = t["c_sample"]
        self.w_ada = t["w_ada"]
        self.b_ada = t["b_ada"]
        self.g_norm1 = t["g_norm1"]
        self.g_norm2 = t["g_norm2"]
        self.w_in = t["w_in"]
        self.ln_g = t["ln_g"]
        self.ln_b = t["ln_b"]
        self.w_s = t["w_s"]
        self.b_s = t["b_s"]
        self.lam_re = t["lam_re"]
        self.lam_im = t["lam_im"]
        self.log_dt = t["log_dt"]
        self.ssm_b_re = t["ssm_b_re"]
        self.ssm_b_im = t["ssm_b_im"]
        self.ssm_c_re = t["ssm_c_re"]
        self.ssm_c_im = t["ssm_c_im"]
        self.ssm_d = t["ssm_d"]
        self.w_glu = t["w_glu"]
        self.b_glu = t["b_glu"]
        self.w_out = t["w_out"]
        self.w_group = t["w_group"]
        self.b_group = t["b_group"]
        self.w_expert = t["w_expert"]
        self.b_expert = t["b_expert"]
        self.w1 = t["w1"]
        self.w3 = t["w3"]
        self.w2 = t["w2"]
        self.g_final = t["g_final"]


class Outputs:

    def __init__(self, t):
        self.y_prompt = t["y_prompt"]
        self.y_sample = t["y_sample"]
        self.ssm_re_prompt = t["ssm_re_prompt"]
        self.ssm_im_prompt = t["ssm_im_prompt"]
        self.ssm_re_sample = t["ssm_re_sample"]
        self.ssm_im_sample = t["ssm_im_sample"]
        self.v_sample = t["v_sample"]


class Shared:

    def __init__(self, sb, psum, sem):
        self.sb, self.psum, self.sem = sb, psum, sem


class Steps:

    def __init__(self, eng, sem, done=0):
        self.eng, self.sem, self.done, self.count = eng, sem, done, 0

    def did(self, ins):
        ins.then_inc(self.sem, 1)
        self.done = self.done + 1
        self.count += 1

    def link(self, ins):
        self.did(ins)
        self.eng.wait_ge(self.sem, self.done)

    def sync(self):
        self.eng.wait_ge(self.sem, self.done)


def fan(ap, shape):
    return ap.unsqueeze(len(shape) - 1).to_broadcast(shape)


def build(nc, a, o):
    ctx = ExitStack()
    with ctx:
        ctx.enter_context(nc.allow_non_contiguous_dma(reason="small parameter loads"))
        used = [0]

        def sb(stack, name, shape, dt=F32):
            return stack.enter_context(nc.sbuf_tensor(name, shape, dt))

        def psum(stack, name, shape):
            return stack.enter_context(nc.psum_tensor(name, shape, F32))

        def sem(name):
            used[0] += 1
            return ctx.enter_context(nc.semaphore(name))

        def dram(name, shape):
            return nc.dram_tensor(name, shape, F32, kind="Internal").ap()

        S = Shared(sb, psum, sem)
        S.ada_d = dram("ada_rows", (9, 6 * D))
        S.kpad_d = dram("toeplitz_rows", (GC, G, 2 * P))
        S.a_d = dram("gmlp_rows", (TOK, DA))
        S.s_d = dram("s5_in_rows", (TOK, DA))
        S.y_d = dram("s5_out_rows", (TOK, DA))
        S.h2_d = dram("moe_in_rows", (TOK, D))
        S.yb_d = dram("expert_rows", (NBLK * P, D))
        S.ident = sb(ctx, "ident", [P, P])
        with ExitStack() as early:
            tables(S, early)
            setup(nc, S, a)
            mixin(nc, S, a, o)
            s5(nc, S, a, o)
        S.x2 = sb(ctx, "x2", [P, NT, D])
        S.logits = sb(ctx, "logits", [P, NT, NR])
        mixout(nc, S, a)
        S.dest = sb(ctx, "dest", [P, NT * 2], I32)
        S.slot_tok = sb(ctx, "slot_tok", [P, NBLK + 3], I32)
        S.slot_gate = sb(ctx, "slot_gate", [P, NBLK + 3])
        S.n_blocks = sb(ctx, "n_blocks", [1, 2], I32)
        S.block_run = sb(ctx, "block_run", [1, NBLK + 3], I32)
        S.run_expert = sb(ctx, "run_expert", [1, NE], I32)
        S.run_free = sb(ctx, "run_free", [1, NE], I32)
        route(nc, S)
        experts(nc, S, a)
        final(nc, S, a, o)


def tables(S, stack):
    sb = S.sb
    S.m_re = sb(stack, "m_re", [P, PAIRS, 9, GC])
    S.m_im = sb(stack, "m_im", [P, PAIRS, 9, GC])
    S.wx = sb(stack, "wx", [P, PAIRS, 2, P])
    S.toep = sb(stack, "toep", [P, G, P])
    S.rot_c = sb(stack, "rot_c", [P, PAIRS, NCH])
    S.rot_s = sb(stack, "rot_s", [P, PAIRS, NCH])
    S.decay = sb(stack, "decay", [P, PAIRS])
    S.a8_re = sb(stack, "a8_re", [P, PAIRS])
    S.a8_im = sb(stack, "a8_im", [P, PAIRS])
    S.na8_im = sb(stack, "na8_im", [P, PAIRS])
    S.ws = sb(stack, "ws", [P, HEADS, P])
    S.ws_samp = sb(stack, "ws_samp", [NS, HEADS, NS])
    S.bs = sb(stack, "bs", [P, HEADS])
    S.bs_samp = sb(stack, "bs_samp", [NS, HEADS])


def setup(nc, S, a):
    with ExitStack() as st:
        sb, sem = S.sb, S.sem
        NW = 12
        WB = 2
        c9 = sb(st, "c9", [9, D])
        sc9 = c9
        rows = sb(st, "rows", [9, 6 * D])
        cT = sb(st, "cT", [P, KD, 9])
        wada = sb(st, "wada", [P, WB, KD, 512])
        bada = sb(st, "bada", [9, 6 * D])
        g12 = sb(st, "g12", [9, 2, D])
        lam = sb(st, "lam", [PAIRS, 2, P])
        lr = sb(st, "lr", [P, PAIRS])
        li = sb(st, "li", [P, PAIRS])
        dt = sb(st, "dt", [P, PAIRS])
        tmp = [sb(st, f"tmp{i}", [P, PAIRS]) for i in range(8)]
        pw_re = sb(st, "pw_re", [P, PAIRS, 9])
        pw_im = sb(st, "pw_im", [P, PAIRS, 9])
        pr_re = sb(st, "pr_re", [P, PAIRS, Q])
        pr_im = sb(st, "pr_im", [P, PAIRS, Q])
        b_in = sb(st, "b_in", [P, 2, PAIRS, GC])
        bb = sb(st, "bb", [P, 2, PAIRS, GC])
        c_in = sb(st, "c_in", [P, 2, 2, P])
        cc = sb(st, "cc", [P, 2, PAIRS, GC])
        big1 = sb(st, "big1", [P, PAIRS, 9, GC])
        zero = sb(st, "zero", [GC, P])
        k0 = S.toep[0:GC, :, :]
        dd = sb(st, "dd", [GC, G])
        dtmp = sb(st, "dtmp", [GC, G, GC])
        ws_in = sb(st, "ws_in", [P, HEADS, P])
        v = [S.toep[:, 0:PAIRS, :].rearrange("p a (s h) -> p a s h", s=Q),
             S.toep[:, PAIRS:G, :].rearrange("p a (s h) -> p a s h", s=Q)]
        pm = S.psum(st, "ps_misc", [P, 4, 512])
        pa = S.psum(st, "ps_ada", [P, WB, 512])
        ident = S.ident

        id_steps, z_k0, z_ws = sem("id_steps"), sem("z_k0"), sem("z_ws")
        c_in_s, small, w_s, bada_s = sem("c_loaded"), sem("small_loaded"), [sem(f"wada_loaded{i}") for i in range(WB)], sem("bada_loaded")
        ws_cp, ws_mask, ws_blk = sem("ws_copied"), sem("ws_masked"), sem("ws_blocks")
        ada_free = sem("ada_bank_free")
        act_s, pe_s, dve_s, ada_mm, ada_ev, rows_ok, rows_out = (sem("setup_act"), sem("setup_pe"), sem("setup_dve"), sem("ada_mm"), sem("ada_evac"), sem("ada_rows_ready"), sem("ada_rows_stored"))
        k_ok, k_out, toep_in, chan = sem("k0_ready"), sem("k0_stored"), sem("toep_loaded"), sem("dve_chain")
        w_view = a.w_ada[0].rearrange("(k p) n -> p k n", p=P)

        with nc.Block() as block:
            @block.sync
            def _(sp):
                sp.dma_start(c9[0:1, :], a.c_prompt).then_inc(c_in_s, 16)
                sp.dma_start(c9[1:9, :], a.c_sample).then_inc(c_in_s, 16)
                sp.dma_start(lam[:, 0, :], a.lam_re[0].rearrange("(a g) p -> a (g p)", g=2)).then_inc(small, 16)
                sp.dma_start(lam[:, 1, :], a.lam_im[0].rearrange("(a g) p -> a (g p)", g=2)).then_inc(small, 16)
                ldt = a.log_dt[0:1, :].rearrange("o (a g) -> o g a", g=2)
                for g in range(2):
                    sp.dma_start(dt[g * ST:(g + 1) * ST, :], ldt[:, g, :].to_broadcast([ST, PAIRS])).then_inc(small, 16)
                for i, t in enumerate((a.ssm_b_re, a.ssm_b_im)):
                    sp.dma_start(b_in[:, i, :, :], t[0].rearrange("(a g) p h -> (g p) a h", g=2)).then_inc(small, 16)
                for i, t in enumerate((a.ssm_c_re, a.ssm_c_im)):
                    cv = t[0].rearrange("(b a g) o p -> b a o g p", b=2, g=2)
                    for h in range(2):
                        for q in range(8):
                            sp.dma_start(c_in[q * GC:(q + 1) * GC, i, h, :].rearrange("o (g p) -> o g p", g=2),
                                         cv[h, q, :, :, :]).then_inc(small, 16)
                sp.dma_start(dd[:, :], a.ssm_d[0].rearrange("g h -> h g")).then_inc(small, 16)
                sp.dma_start(ws_in[:, :, :], a.w_s[0].rearrange("h t s -> t h s")).then_inc(small, 16)
                sp.dma_start(S.bs[:, :], a.b_s[0].rearrange("h t -> t h")).then_inc(small, 16)
                for q in range(NSEQ):
                    sp.dma_start(S.bs_samp[q * DSEQ:(q + 1) * DSEQ, :],
                                 a.b_s[0].rearrange("h t -> t h")[0:DSEQ, :]).then_inc(small, 16)
                sp.dma_start(bada[:, :], a.b_ada.to_broadcast([9, 6 * D])).then_inc(bada_s, 16)
                sp.dma_start(g12[:, 0, :], a.g_norm1.to_broadcast([9, D])).then_inc(bada_s, 16)
                sp.dma_start(g12[:, 1, :], a.g_norm2.to_broadcast([9, D])).then_inc(bada_s, 16)
                for n in range(NW):
                    if n >= WB:
                        sp.wait_ge(ada_mm, n - WB + 1)
                    sp.dma_start(wada[:, n % WB, :, :], w_view[:, :, n * 512:(n + 1) * 512]).then_inc(w_s[n % WB], 16)
                sp.wait_ge(ws_mask, 1)
                sp.wait_ge(z_ws, 1)
                for q in range(NSEQ):
                    r = slice(q * DSEQ, (q + 1) * DSEQ)
                    sp.dma_start(S.ws_samp[r, :, r], S.ws[0:DSEQ, :, 0:DSEQ]).then_inc(ws_blk, 16)
                sp.wait_ge(k_ok, 1)
                sp.wait_ge(z_k0, 1)
                sp.dma_start(S.kpad_d[:, :, 0:P], zero[:, :].unsqueeze(1).to_broadcast([GC, G, P])).then_inc(k_out, 16)
                sp.dma_start(S.kpad_d[:, :, P:2 * P], k0).then_inc(k_out, 16)
                sp.wait_ge(k_out, 32)
                for s in range(Q):
                    sp.dma_start(S.toep[s * GC:(s + 1) * GC, :, :],
                                 S.kpad_d[:, :, P - s * GC:2 * P - s * GC]).then_inc(toep_in, 16)
                sp.wait_ge(rows_ok, 5)
                sp.dma_start(S.ada_d, rows[:, :]).then_inc(rows_out, 16)
                sp.wait_ge(ws_blk, 16 * NSEQ)
                sp.wait_ge(toep_in, 16 * Q)
                sp.wait_ge(rows_out, 16)

            @block.gpsimd
            def _(pool):
                ids = Steps(pool, id_steps)
                ids.link(pool.memset(ident[:, :], 0.0))
                ids.did(pool.affine_select(out=ident[:, :], in_=ident[:, :], compare_op=ALU.not_equal, fill=1.0,
                                           base=0, pattern=[[-1, P]], channel_multiplier=1))
                pool.memset(zero[:, :], 0.0).then_inc(z_k0, 1)
                pool.memset(S.ws_samp[:, :, :], 0.0).then_inc(z_ws, 1)
                pool.wait_ge(ws_cp, 1)
                pool.affine_select(out=S.ws[:, :, :], in_=S.ws[:, :, :], compare_op=ALU.is_ge, fill=0.0, base=0,
                                   pattern=[[0, HEADS], [1, P]], channel_multiplier=-1).then_inc(ws_mask, 1)
                pool.wait_ge(bada_s, 48)
                pool.wait_ge(ada_ev, NW)
                rk = Steps(pool, rows_ok)
                rk.link(pool.tensor_tensor(rows[:, :], rows[:, :], bada[:, :], ALU.add))
                for at in (1, 4):
                    rk.did(pool.tensor_scalar(rows[:, at * D:(at + 1) * D], rows[:, at * D:(at + 1) * D], 1.0, None, ALU.add))
                rk.sync()
                for i, at in enumerate((1, 4)):
                    rk.did(pool.tensor_tensor(rows[:, at * D:(at + 1) * D], rows[:, at * D:(at + 1) * D], g12[:, i, :], ALU.mult))

            @block.scalar
            def _(act):
                act.wait_ge(c_in_s, 32)
                st_ = Steps(act, act_s)
                st_.did(act.activation(sc9[:, :], c9[:, :], ACT.Silu))
                act.wait_ge(small, 16 * N_SMALL)
                st_.link(act.activation(tmp[7][:, :], dt[:, :], ACT.Exp))
                act.wait_ge(dve_s, 2)
                st_.did(act.activation(tmp[2][:, :], tmp[0][:, :], ACT.Exp))
                st_.did(act.activation(S.decay[:, :], tmp[0][:, :], ACT.Exp, scale=float(Q)))
                st_.did(act.activation(tmp[3][:, :], tmp[1][:, :], ACT.Sin))
                st_.did(act.activation(tmp[4][:, :], tmp[1][:, :], ACT.Sin, scale=0.5))
                for i in range(2):
                    act.wait_ge(pe_s, 3 + i)
                    st_.did(act.activation(cc[:, i, :, :].rearrange("p a o -> p (a o)"), pm[:, i, 256:512], ACT.Copy))
                act.wait_ge(pe_s, 5)
                act.activation(S.ws[:, :, :].rearrange("p h t -> p (h t)"), pm[:, 2, :], ACT.Copy).then_inc(ws_cp, 1)
                act.sem_inc(ada_free, WB)
                with act.Fori(0, NW // WB) as j:
                    for b in range(WB):
                        act.wait_ge(ada_mm, WB * j + b + 1)
                        act.activation(rows[:, ds((WB * j + b) * 512, 512)], pa[0:9, b, :], ACT.Copy).then_inc(ada_free, 1)
                act.wait_ge(ada_free, WB + NW)
                act.sem_inc(ada_ev, NW)
                for n in range(8):
                    act.wait_ge(pe_s, 6 + n)
                    st_.did(act.activation(
                        S.wx[:, 2 * n:2 * n + 2, :, :].rearrange("p a r s -> p (a r s)"), pm[:, n % 2, :], ACT.Copy))

            @block.tensor
            def _(pe):
                ps = Steps(pe, pe_s)
                pe.wait_ge(id_steps, 2)
                pe.wait_ge(act_s, 1)
                for k in range(KD):
                    last = pe.transpose(pm[:, 0, k * 9:(k + 1) * 9], sc9[:, k * P:(k + 1) * P], ident[0:9, 0:9])
                ps.did(last)
                pe.wait_ge(small, 16 * N_SMALL)
                pe.transpose(pm[:, 1, 0:PAIRS], lam[:, 0, :], ident[0:PAIRS, 0:PAIRS])
                ps.did(pe.transpose(pm[:, 1, PAIRS:2 * PAIRS], lam[:, 1, :], ident[0:PAIRS, 0:PAIRS]))
                pe.wait_ge(chan, 3)
                for i in range(2):
                    for h in range(2):
                        last = pe.transpose(pm[:, i, 256 + h * P:256 + (h + 1) * P], c_in[:, i, h, :], ident[:, :])
                    ps.did(last)
                for h in range(HEADS):
                    last = pe.transpose(pm[:, 2, h * P:(h + 1) * P], ws_in[:, h, :], ident[:, :])
                ps.did(last)
                with pe.Fori(0, NW // WB) as j:
                    for b in range(WB):
                        pe.wait_ge(w_s[b], 16 * j + 16)
                        pe.wait_ge(ada_free, WB * j + b + 1)
                        for k in range(KD):
                            last = pe.matmul(pa[0:9, b, :], cT[:, k, :], wada[:, b, k, :], start=k == 0, stop=k == KD - 1)
                        last.then_inc(ada_mm, 1)
                for n in range(8):
                    if n == 0:
                        pe.wait_ge(dve_s, 4)
                        pe.wait_ge(act_s, 8)
                    if n >= 2:
                        pe.wait_ge(act_s, 9 + n - 2)
                    for q in range(4):
                        last = pe.transpose(pm[:, n % 2, q * P:(q + 1) * P],
                                            v[q % 2][:, 2 * n + q // 2, :, :].rearrange("p s h -> p (s h)"), ident[:, :])
                    ps.did(last)
                pe.wait_ge(dve_s, 5)
                for n in range(8):
                    if n >= 2:
                        pe.wait_ge(dve_s, 5 + n - 1)
                    for q in range(4):
                        g = 8 * (n // 2) + 2 * q + n % 2
                        r = slice((g % 2) * ST, (g % 2) * ST + ST)
                        for i, m in enumerate((S.m_re, S.m_im)):
                            last = pe.matmul(pm[0:GC, 2 + n % 2, q * P:(q + 1) * P], bb[r, i, g // 2, :],
                                             m[r, g // 2, 0:Q, :].rearrange("p k o -> p (k o)"),
                                             start=i == 0, stop=i == 1)
                    ps.did(last)

            @block.vector
            def _(dve):
                ch = Steps(dve, chan)
                dv = Steps(dve, dve_s)

                def tt(out, x, y, op):
                    ch.link(dve.tensor_tensor(out, x, y, op))

                def cmul(o_re, o_im, x_re, x_im, y_re, y_im, t, shape=None):
                    ch.did(dve.tensor_tensor(o_re, x_re, y_re, ALU.mult))
                    ch.did(dve.tensor_tensor(o_im, x_re, y_im, ALU.mult))
                    tt(t, x_im, y_im, ALU.mult)
                    tt(o_re, o_re, t, ALU.subtract)
                    tt(t, x_im, y_re, ALU.mult)
                    tt(o_im, o_im, t, ALU.add)

                dve.wait_ge(pe_s, 1)
                ch.link(dve.tensor_copy(cT[:, :, :].rearrange("p k n -> p (k n)"), pm[:, 0, 0:9 * KD]))
                dve.wait_ge(pe_s, 2)
                ch.did(dve.tensor_copy(lr[:, :], pm[:, 1, 0:PAIRS]))
                ch.link(dve.tensor_copy(li[:, :], pm[:, 1, PAIRS:2 * PAIRS]))
                dve.wait_ge(act_s, 2)
                T = [t[:, :] for t in tmp]
                dv.did(dve.tensor_tensor(T[0], lr[:, :], T[7], ALU.mult))
                tt(T[1], li[:, :], T[7], ALU.mult)
                ch.link(dve.tensor_scalar(T[5], T[1], 1.0 / TWO_PI, MAGIC, ALU.mult, ALU.add))
                ch.link(dve.tensor_scalar(T[5], T[5], MAGIC, None, ALU.subtract))
                for part in (PI_HI, PI_MID):
                    ch.link(dve.scalar_tensor_tensor(out=T[1], in0=T[5], scalar=-part, in1=T[1], op0=ALU.mult, op1=ALU.add))
                dv.did(dve.scalar_tensor_tensor(out=T[1], in0=T[5], scalar=-PI_LO, in1=T[1], op0=ALU.mult, op1=ALU.add))
                dve.wait_ge(act_s, 6)
                tt(T[5], T[4], T[4], ALU.mult)
                ch.link(dve.tensor_scalar(T[5], T[5], -2.0, 1.0, ALU.mult, ALU.add))
                ch.did(dve.memset(pw_re[:, :, 0], 1.0))
                ch.did(dve.memset(pw_im[:, :, 0], 0.0))
                tt(pw_re[:, :, 1], T[2], T[5], ALU.mult)
                tt(pw_im[:, :, 1], T[2], T[3], ALU.mult)
                for k in range(2, 9):
                    cmul(pw_re[:, :, k], pw_im[:, :, k], pw_re[:, :, k - 1], pw_im[:, :, k - 1],
                         pw_re[:, :, 1], pw_im[:, :, 1], T[6])
                for s in range(Q):
                    ch.did(dve.tensor_copy(pr_re[:, :, s], pw_re[:, :, Q - 1 - s]))
                    ch.did(dve.tensor_copy(pr_im[:, :, s], pw_im[:, :, Q - 1 - s]))
                ch.did(dve.tensor_copy(S.a8_re[:, :], pw_re[:, :, 8]))
                ch.did(dve.tensor_copy(S.a8_im[:, :], pw_im[:, :, 8]))
                ch.link(dve.tensor_scalar(S.na8_im[:, :], pw_im[:, :, 8], -1.0, None, ALU.mult))
                ch.link(dve.tensor_scalar(T[0], pw_re[:, :, 1], -1.0, None, ALU.add))
                ch.did(dve.tensor_tensor(T[1], lr[:, :], lr[:, :], ALU.mult))
                tt(T[2], li[:, :], li[:, :], ALU.mult)
                tt(T[1], T[1], T[2], ALU.add)
                ch.link(dve.reciprocal(T[1], T[1]))
                ch.did(dve.tensor_tensor(T[2], T[0], lr[:, :], ALU.mult))
                tt(T[4], pw_im[:, :, 1], li[:, :], ALU.mult)
                tt(T[2], T[2], T[4], ALU.add)
                tt(T[2], T[2], T[1], ALU.mult)
                ch.did(dve.tensor_tensor(T[6], pw_im[:, :, 1], lr[:, :], ALU.mult))
                tt(T[4], T[0], li[:, :], ALU.mult)
                tt(T[6], T[6], T[4], ALU.subtract)
                tt(T[6], T[6], T[1], ALU.mult)
                s3 = [P, PAIRS, GC]
                t256 = big1[:, :, 0, :]
                cmul(bb[:, 0, :, :], bb[:, 1, :, :], fan(T[2], s3), fan(T[6], s3), b_in[:, 0, :, :], b_in[:, 1, :, :], t256)
                s4 = [P, PAIRS, Q, GC]
                pr, pi = fan(pr_re[:, :, :], s4), fan(pr_im[:, :, :], s4)
                b_re = bb[:, 0, :, :].unsqueeze(2).to_broadcast(s4)
                b_im = bb[:, 1, :, :].unsqueeze(2).to_broadcast(s4)
                t4 = big1[:, :, 0:Q, :]
                ch.did(dve.tensor_tensor(v[0], pr, b_re, ALU.mult))
                ch.did(dve.tensor_tensor(v[1], pr, b_im, ALU.mult))
                tt(t4, pi, b_im, ALU.mult)
                dv.did(dve.tensor_tensor(v[0], v[0], t4, ALU.subtract))
                dv.sync()
                tt(t4, pi, b_re, ALU.mult)
                dv.did(dve.tensor_tensor(v[1], v[1], t4, ALU.add))
                dv.sync()
                dve.wait_ge(act_s, 8)
                s9 = [P, PAIRS, 9, GC]
                q_re, q_im = fan(pw_re[:, :, :], s9), fan(pw_im[:, :, :], s9)
                c_re = cc[:, 0, :, :].unsqueeze(2).to_broadcast(s9)
                c_im = cc[:, 1, :, :].unsqueeze(2).to_broadcast(s9)
                m_re, m_im, t9 = S.m_re[:, :, :, :], S.m_im[:, :, :, :], big1[:, :, :, :]
                ch.did(dve.tensor_tensor(m_re, q_re, c_re, ALU.mult))
                ch.did(dve.tensor_tensor(m_im, q_im, c_re, ALU.mult))
                tt(t9, q_im, c_im, ALU.mult)
                tt(m_re, m_re, t9, ALU.subtract)
                tt(t9, q_re, c_im, ALU.mult)
                tt(m_im, m_im, t9, ALU.add)
                dv.did(dve.tensor_scalar(m_im, m_im, -1.0, None, ALU.mult))
                ch.link(dve.tensor_tensor(dtmp[:, :, :], ident[0:GC, 0:GC].unsqueeze(1).to_broadcast([GC, G, GC]),
                                          fan(dd[:, :], [GC, G, GC]), ALU.mult))
                rc, rs = S.rot_c, S.rot_s
                sq = [(T[5], T[3]), (T[0], T[1])]
                for i in range(3):
                    (x, y), (u, w) = sq[i % 2], sq[(i + 1) % 2]
                    cmul(u, w, x, y, x, y, T[2])
                ch.did(dve.memset(rc[:, :, 0:1], 1.0))
                ch.link(dve.memset(rs[:, :, 0:1], 0.0))
                n, i = 1, 1
                while n < NCH:
                    (x, y), (u, w) = sq[i % 2], sq[(i + 1) % 2]
                    sh = [P, PAIRS, n]
                    half = big1[:, :, :, :].rearrange("p a k o -> p a (k o)")[:, :, 0:n]
                    cmul(rc[:, :, n:2 * n], rs[:, :, n:2 * n], rc[:, :, 0:n], rs[:, :, 0:n], fan(x, sh), fan(y, sh), half)
                    cmul(u, w, x, y, x, y, T[2])
                    n, i = 2 * n, i + 1
                for n in range(8):
                    dve.wait_ge(pe_s, 14 + n)
                    dv.did(dve.tensor_copy(k0[:, 8 * (n // 2) + n % 2:8 * (n // 2) + 8:2, :],
                                           pm[0:GC, 2 + n % 2, :].rearrange("h (g k) -> h g k", g=4)))
                dv.sync()
                dve.tensor_tensor(k0[:, :, 0:GC], k0[:, :, 0:GC], dtmp[:, :, :], ALU.add).then_inc(k_ok, 1)



N_SMALL = 2 + 2 + 2 + 32 + 1 + 1 + 1 + NSEQ


def prompt_loop(eng, first, body):
    with eng.Fori(0, 7) as j:
        for b in range(2):
            t = first + b
            body(2 * j + t, j + t // 2, t % 2)


def inv_sqrt(eng, c, y, total, share, x, t):
    c.link(eng.tensor_scalar(x, total, share, EPS, ALU.mult, ALU.add))
    c.link(eng.tensor_scalar(y.bitcast(I32), x.bitcast(I32), -0.5, float(0x5F3759DF), ALU.mult, ALU.add))
    for _ in range(4):
        c.link(eng.tensor_tensor(t, y, y, ALU.mult))
        c.link(eng.tensor_tensor(t, t, x, ALU.mult))
        c.link(eng.tensor_scalar(t, t, -0.5, 1.5, ALU.mult, ALU.add))
        c.link(eng.tensor_tensor(y, y, t, ALU.mult))


INV = 2 + 4 * 4


def mixin(nc, S, a, o):
    with ExitStack() as st:
        sb, sem = S.sb, S.sem
        win = sb(st, "win", [P, KD, 3 * DA])
        x = sb(st, "x", [P, 2, D])
        hT = sb(st, "hT", [P, 2, KD, P])
        gain = sb(st, "gain1", [P, D])
        shift = sb(st, "shift1", [P, D])
        lng = sb(st, "lng", [P, DA])
        lnb = sb(st, "lnb", [P, DA])
        junk = sb(st, "junk1", [P, D])
        junk2 = sb(st, "junk2", [P, DA])
        ssq = sb(st, "ssq1", [P, 2])
        rstd = sb(st, "rstd1", [P, 2])
        v = sb(st, "v", [P, DA])
        u = sb(st, "u", [P, DA])
        a_row = sb(st, "a_row", [P, DA])
        s_row = sb(st, "s_row", [P, DA])
        mean = sb(st, "mean", [P, HEADS])
        var = sb(st, "var", [P, HEADS])
        newton = sb(st, "newton1", [P, 2, HEADS])
        pT = S.psum(st, "ps_hT", [P, 2, 512])
        pV = S.psum(st, "ps_v", [P, 512])
        pU = S.psum(st, "ps_u", [P, 512])
        pS = S.psum(st, "ps_s", [P, 512])
        pM = S.psum(st, "ps_mix", [P, 512])
        ident = S.ident
        blank = sb(st, "blank", [P, D])
        blank_ok, blank_out = sem("blank_ready"), sem("blank_stored")

        mod_in, mod_samp, win_in = sem("mod1_loaded"), sem("mod1_sample_loaded"), [sem(f"win_loaded{i}") for i in range(3)]
        x_in = [sem("x_loaded0"), sem("x_loaded1")]
        ssq_ok, ch, h_ok, hT_mm, hT_a, hT_d = sem("ssq1_ready"), sem("dve_chain1"), sem("h_ready"), sem("hT_transposed"), sem("hT_evac_act"), sem("hT_evac_dve")
        v_mm, v_ok, cen_ok, var_ok, vhat_ok, vn_ok = sem("v_mm"), sem("v_gelu"), sem("v_centred"), sem("v_var"), sem("v_scaled"), sem("v_normed")
        u_mm, u_ok, s_mm, s_ok, m_mm, a_ok = sem("u_mm"), sem("u_gelu"), sem("s_mm"), sem("s_copied"), sem("mix_mm"), sem("a_ready")
        xn_ok, s_out, a_out, v_out = sem("x_scaled"), sem("s_stored"), sem("a_stored"), sem("v_stored")
        w_view = a.w_in[0].rearrange("(k p) n -> p k n", p=P)
        x_rows = a.x_prompt[0]
        samp_rows = a.x_sample.rearrange("b t d -> (b t) d")

        def rows_of(i):
            return NS if isinstance(i, int) and i == TP else P

        def dr(t, i):
            return t[TP * P:TOK, :] if isinstance(i, int) and i == TP else t[ds(i * P, P), :]

        with nc.Block() as block:
            @block.sync
            def _(sp):
                sp.dma_start(x[:, 0, :], x_rows[0:P, :]).then_inc(x_in[0], 16)
                sp.dma_start(gain[:, :], S.ada_d[0:1, D:2 * D].to_broadcast([P, D])).then_inc(mod_in, 16)
                sp.dma_start(shift[:, :], S.ada_d[0:1, 0:D].to_broadcast([P, D])).then_inc(mod_in, 16)
                for n, c in enumerate((1, 0, 2)):
                    sp.dma_start(win[:, :, c * DA:(c + 1) * DA], w_view[:, :, c * DA:(c + 1) * DA]).then_inc(win_in[n], 16)
                sp.dma_start(lng[:, :], a.ln_g.rearrange("o h d -> o (h d)").to_broadcast([P, DA])).then_inc(mod_in, 16)
                sp.dma_start(lnb[:, :], a.ln_b.rearrange("o h d -> o (h d)").to_broadcast([P, DA])).then_inc(mod_in, 16)
                sp.dma_start(x[:, 1, :], x_rows[P:2 * P, :]).then_inc(x_in[1], 16)

                def stores(i, n, b):
                    r = rows_of(i)
                    if not isinstance(i, int) or i < TP - 1:
                        for k in range(2):
                            sp.dma_start(S.yb_d[ds((FULL + 2 * i + k) * P, P), :], blank[:, :]).then_inc(blank_out, 16)
                    elif i == TP - 1:
                        sp.dma_start(S.yb_d[(NBLK - 1) * P:NBLK * P, :], blank[:, :]).then_inc(blank_out, 16)
                    sp.wait_ge(s_ok, i + 1)
                    sp.dma_start(dr(S.s_d, i), s_row[0:r, :]).then_inc(s_out, 16)
                    sp.wait_ge(a_ok, i + 1)
                    sp.dma_start(dr(S.a_d, i), a_row[0:r, :]).then_inc(a_out, 16)

                sp.wait_ge(blank_ok, 1)

                def step(i, n, b):
                    sp.wait_ge(hT_mm, i + 1)
                    sp.dma_start(x[:, b, :], x_rows[ds((i + 2) * P, P), :]).then_inc(x_in[b], 16)
                    stores(i, n, b)

                prompt_loop(sp, 0, step)
                sp.wait_ge(hT_mm, 15)
                sp.dma_start(x[0:NS, 0, :], samp_rows).then_inc(x_in[0], 16)
                stores(14, 7, 0)
                sp.wait_ge(h_ok, TP)
                for k, t in enumerate((gain, shift)):
                    for q in range(NSEQ):
                        sp.dma_start(t[q * DSEQ:(q + 1) * DSEQ, :],
                                     S.ada_d[1 + q:2 + q, (1 - k) * D:(2 - k) * D].to_broadcast([DSEQ, D])).then_inc(mod_samp, 16)
                stores(15, 7, 1)
                stores(16, 8, 0)
                sp.wait_ge(vn_ok, 2 * NT)
                sp.dma_start(o.v_sample[0].rearrange("b t d -> (b t) d"), v[0:NS, :]).then_inc(v_out, 16)
                sp.wait_ge(v_out, 16)
                sp.wait_ge(blank_out, 16 * (NBLK - FULL))
                sp.wait_ge(s_out, 16 * NT)
                sp.wait_ge(a_out, 16 * NT)

            @block.gpsimd
            def _(pool):
                pool.memset(blank[:, :], 0.0).then_inc(blank_ok, 1)

                def shift_h(i, n, b):
                    r = rows_of(i)
                    pool.wait_ge(xn_ok, i + 1)
                    pool.tensor_tensor(x[0:r, b, :], x[0:r, b, :], shift[0:r, :], ALU.add).then_inc(h_ok, 1)

                def affine_v(i):
                    r = rows_of(i)
                    pool.wait_ge(vhat_ok, i + 1)
                    pool.tensor_tensor(v[0:r, :], v[0:r, :], lng[0:r, :], ALU.mult).then_inc(vn_ok, 1)
                    pool.wait_ge(vn_ok, 2 * i + 1)
                    pool.tensor_tensor(v[0:r, :], v[0:r, :], lnb[0:r, :], ALU.add).then_inc(vn_ok, 1)

                pool.wait_ge(mod_in, 64)
                shift_h(0, 0, 0)

                def step(i, n, b):
                    if not (isinstance(i, int) and i == TP):
                        shift_h(i + 1, n + b, 1 - b)
                    affine_v(i)

                prompt_loop(pool, 0, step)
                for i in (14, 15, 16):
                    step(i, i // 2, i % 2)

            @block.scalar
            def _(act):
                def square(i, n, b):
                    r = rows_of(i)
                    act.wait_ge(x_in[b], 16 * n + 16)
                    act.wait_ge(xn_ok, i)
                    act.activation(junk[0:r, :], x[0:r, b, :], ACT.Square, accum_out=ssq[0:r, b:b + 1]).then_inc(ssq_ok, 1)

                def evac(i, n, b):
                    r = rows_of(i)
                    act.wait_ge(hT_mm, i + 1)
                    act.activation(hT[:, b, 0:4, 0:r], pT[:, 0, :].rearrange("p (k t) -> p k t", k=4)[:, :, 0:r],
                                   ACT.Copy).then_inc(hT_a, 1)

                def step(i, n, b):
                    r = rows_of(i)
                    last = isinstance(i, int) and i == TP
                    if not last:
                        square(i + 1, n + b, 1 - b)
                    act.wait_ge(v_mm, i + 1)
                    act.activation(v[0:r, :], pV[0:r, :], ACT.Gelu_apprx_tanh).then_inc(v_ok, 1)
                    if not last:
                        evac(i + 1, n + b, 1 - b)
                    act.wait_ge(cen_ok, i + 1)
                    for h in range(HEADS):
                        s = act.activation(junk2[0:r, h * HD:(h + 1) * HD], v[0:r, h * HD:(h + 1) * HD], ACT.Square,
                                           accum_out=var[0:r, h:h + 1])
                    s.then_inc(var_ok, 1)
                    act.wait_ge(u_mm, i + 1)
                    act.wait_ge(a_ok, i)
                    act.activation(u[0:r, :], pU[0:r, :], ACT.Gelu_apprx_tanh).then_inc(u_ok, 1)
                    act.wait_ge(s_mm, i + 1)
                    act.wait_ge(s_out, 16 * i)
                    act.activation(s_row[0:r, :], pS[0:r, :], ACT.Copy).then_inc(s_ok, 1)

                square(0, 0, 0)
                evac(0, 0, 0)
                prompt_loop(act, 0, step)
                for i in (14, 15, 16):
                    step(i, i // 2, i % 2)

            @block.tensor
            def _(pe):
                def transposes(i, n, b):
                    r = rows_of(i)
                    pe.wait_ge(h_ok, i + 1)
                    pe.wait_ge(hT_a, i)
                    pe.wait_ge(hT_d, i)
                    for k in range(KD):
                        last = pe.transpose(pT[:, k // 4, k % 4 * P:k % 4 * P + r], x[0:r, b, k * P:(k + 1) * P],
                                            ident[0:r, 0:r])
                    last.then_inc(hT_mm, 1)

                def project(out, i, b, c, free, done):
                    r = rows_of(i)
                    pe.wait_ge(free, i)
                    for k in range(KD):
                        last = pe.matmul(out[0:r, :], hT[:, b, k, 0:r], win[:, k, c * DA:(c + 1) * DA],
                                         start=k == 0, stop=k == KD - 1)
                    last.then_inc(done, 1)

                def step(i, n, b):
                    r = rows_of(i)
                    samp = isinstance(i, int) and i == TP
                    pe.wait_ge(hT_a, i + 1)
                    pe.wait_ge(hT_d, i + 1)
                    pe.wait_ge(win_in[0], 16)
                    project(pV, i, b, 1, v_ok, v_mm)
                    if not samp:
                        transposes(i + 1, n + b, 1 - b)
                    pe.wait_ge(win_in[1], 16)
                    project(pU, i, b, 0, u_ok, u_mm)
                    pe.wait_ge(win_in[2], 16)
                    project(pS, i, b, 2, s_ok, s_mm)
                    pe.wait_ge(vn_ok, 2 * i + 2)
                    pe.wait_ge(a_ok, i)
                    w = S.ws_samp if samp else S.ws
                    for h in range(HEADS):
                        last = pe.matmul(pM[0:r, h * HD:(h + 1) * HD], w[:, h, :], v[0:r, h * HD:(h + 1) * HD],
                                         start=True, stop=True)
                    last.then_inc(m_mm, 1)

                transposes(0, 0, 0)
                prompt_loop(pe, 0, step)
                for i in (14, 15, 16):
                    step(i, i // 2, i % 2)

            @block.vector
            def _(dve):
                c = Steps(dve, ch)

                def scale_x(i, n, b):
                    r = rows_of(i)
                    dve.wait_ge(ssq_ok, i + 1)
                    inv_sqrt(dve, c, rstd[0:r, 0:1], ssq[0:r, b:b + 1], 1.0 / D, newton[0:r, 0, 0:1], newton[0:r, 1, 0:1])
                    dve.scalar_tensor_tensor(out=x[0:r, b, :], in0=x[0:r, b, :], scalar=rstd[0:r, 0:1],
                                             in1=gain[0:r, :], op0=ALU.mult, op1=ALU.mult).then_inc(xn_ok, 1)

                def step(i, n, b):
                    r = rows_of(i)
                    samp = isinstance(i, int) and i == TP
                    if not samp:
                        if isinstance(i, int) and i == TP - 1:
                            dve.wait_ge(mod_samp, 16 * 2 * NSEQ)
                        scale_x(i + 1, n + b, 1 - b)
                    v3 = v[0:r, :].rearrange("p (h d) -> p h d", h=HEADS)
                    s3 = [r, HEADS, HD]
                    dve.wait_ge(v_ok, i + 1)
                    c.link(dve.tensor_reduce(mean[0:r, :], v3, AX.X, ALU.add))
                    c.link(dve.tensor_scalar(mean[0:r, :], mean[0:r, :], 1.0 / HD, None, ALU.mult))
                    dve.tensor_tensor(v3, v3, fan(mean[0:r, :], s3), ALU.subtract).then_inc(cen_ok, 1)
                    if not samp:
                        rn = rows_of(i + 1) if isinstance(i, int) else P
                        dve.wait_ge(hT_mm, i + 2)
                        dve.tensor_copy(hT[:, 1 - b, 4:8, 0:rn],
                                        pT[:, 1, :].rearrange("p (k t) -> p k t", k=4)[:, :, 0:rn]).then_inc(hT_d, 1)
                    dve.wait_ge(var_ok, i + 1)
                    inv_sqrt(dve, c, mean[0:r, :], var[0:r, :], 1.0 / HD, newton[0:r, 0, :], newton[0:r, 1, :])
                    dve.tensor_tensor(v3, v3, fan(mean[0:r, :], s3), ALU.mult).then_inc(vhat_ok, 1)
                    dve.wait_ge(m_mm, i + 1)
                    dve.wait_ge(u_ok, i + 1)
                    dve.wait_ge(a_out, 16 * i)
                    bs = S.bs_samp if samp else S.bs
                    for h in range(HEADS):
                        hs = slice(h * HD, (h + 1) * HD)
                        last = dve.scalar_tensor_tensor(out=a_row[0:r, hs], in0=pM[0:r, hs], scalar=bs[0:r, h:h + 1],
                                                        in1=u[0:r, hs], op0=ALU.add, op1=ALU.mult)
                    last.then_inc(a_ok, 1)

                dve.wait_ge(mod_in, 64)
                scale_x(0, 0, 0)
                dve.wait_ge(hT_mm, 1)
                dve.tensor_copy(hT[:, 0, 4:8, :], pT[:, 1, :].rearrange("p (k t) -> p k t", k=4)).then_inc(hT_d, 1)
                k0 = c.count
                with dve.Fori(0, 7) as j:
                    c.done = INV + CH1 * j
                    step(2 * j, j, 0)
                    step(2 * j + 1, j, 1)
                assert c.count - k0 == CH1, c.count - k0
                c.done = INV + CH1 * 7
                for i in (14, 15, 16):
                    step(i, i // 2, i % 2)


CH1 = 2 * (2 * INV + 2)


def s5(nc, S, a, o):
    with ExitStack() as st:
        sb, sem = S.sb, S.sem
        rows = sb(st, "chunk_rows", [P, 2, Q, DA])
        uT = sb(st, "uT", [P, G, CH])
        h_re = sb(st, "h_re", [P, PAIRS, CH + 1])
        h_im = sb(st, "h_im", [P, PAIRS, CH + 1])
        h0_in = sb(st, "h0_in", [P, 2, P])
        fin = sb(st, "fin", [P, 2, NSEQ, PAIRS])
        f1 = sb(st, "f1", [P, 2, NSEQ])
        rot = sb(st, "rot", [P, 2, 4, NCH])
        scan = sb(st, "scan", [P, 2, 2, NCH])
        back = sb(st, "back", [P, 2, NCH])
        fo = sb(st, "fo", [P, 2, P])
        po = sb(st, "po", [PAIRS, 2, P])
        pX = S.psum(st, "ps_x", [P, 4, 512])
        pB = S.psum(st, "ps_b", [P, 4, 512])
        ident = S.ident

        rows_in, u_mm, u_a, u_d, h0_l, h0_mm, h0_ok = [sem("chunks_loaded0"), sem("chunks_loaded1")], sem("uT_mm"), sem("uT_evac_act"), sem("uT_evac_dve"), sem("h0_loaded"), sem("h0_mm"), sem("h0_ready")
        x_mm, x_free, scan_ok, h_ok, ch, ph = sem("state_mm"), sem("state_free"), sem("scan_ready"), sem("state_ready"), sem("dve_chain2"), sem("pool_chain2")
        y_mm, y_ok, y_out, f_mm, f_ok, f_out, fin_ok = sem("y_mm"), sem("y_gelu"), [sem("y_stored0"), sem("y_stored1")], sem("final_mm"), sem("final_copied"), sem("final_stored"), sem("sample_state")
        h_free = sem("scan_free")
        WIDTH = (P, P, NSEQ)
        at = (0, P, NCH)
        s_rows = S.s_d.rearrange("(c s) n -> c s n", s=Q)
        y_rows = S.y_d.rearrange("(c s) n -> c s n", s=Q)

        by_group = [h[:, :, :].rearrange("p a c -> p (a c)")[:, 0:Q * DA] for h in (h_re, h_im, h_re)]
        perm_a, perm_d = sem("regrouped_act"), sem("regrouped_dve")

        def regroup(eng, t, half):
            w = WIDTH[t]
            gs = slice(half * G // 2, (half + 1) * G // 2)
            eng.wait_ge(rows_in[t % 2], 16 * (t // 2 + 1))
            if t == 2:
                eng.wait_ge(u_mm, 8)
            dst = by_group[t][0:w, :].rearrange("p (g s h) -> p g s h", g=G, s=Q)[:, gs, :, :]
            src = rows[0:w, t % 2, :, :].rearrange("p s (g h) -> p g s h", g=G)[:, gs, :, :]
            if half == 0:
                eng.activation(dst, src, ACT.Copy).then_inc(perm_a, 1)
            else:
                eng.tensor_copy(dst, src).then_inc(perm_d, 1)

        with nc.Block() as block:
            @block.sync
            def _(sp):
                for t in range(2):
                    sp.dma_start(rows[:, t, :, :], s_rows[at[t]:at[t] + P, :, :]).then_inc(rows_in[t], 16)
                for i, x in enumerate((a.state_ssm_re, a.state_ssm_im)):
                    sp.dma_start(h0_in[:, i, :], x[0].rearrange("q (a g) p -> (q a) (g p)", g=2)).then_inc(h0_l, 16)
                sp.wait_ge(perm_a, 1)
                sp.wait_ge(perm_d, 1)
                sp.dma_start(rows[0:NSEQ, 0, :, :], s_rows[NCH:CH, :, :]).then_inc(rows_in[0], 16)
                for t in range(3):
                    sp.wait_ge(y_ok, 8 * (t + 1))
                    sp.dma_start(y_rows[at[t]:at[t] + WIDTH[t], :, :], rows[0:WIDTH[t], t % 2, :, :]).then_inc(y_out[t % 2], 16)
                sp.wait_ge(f_ok, 4)
                for i, (x, y) in enumerate(((o.ssm_re_prompt, o.ssm_re_sample), (o.ssm_im_prompt, o.ssm_im_sample))):
                    sp.dma_start(x[0, 0].rearrange("(a g) p -> a (g p)", g=2), po[:, i, :]).then_inc(f_out, 16)
                    sp.dma_start(y[0].rearrange("q (a g) p -> (q a) (g p)", g=2), fo[:, i, :]).then_inc(f_out, 16)
                sp.wait_ge(f_out, 64)
                sp.wait_ge(y_out[0], 32)
                sp.wait_ge(y_out[1], 16)

            @block.tensor
            def _(pe):
                for n in range(24):
                    t, m = n // 8, n % 8
                    w = WIDTH[t]
                    if m % 4 == 0:
                        pe.wait_ge((perm_a, perm_d)[m // 4], t + 1)
                    if n >= 2:
                        pe.wait_ge((u_a, u_d)[n % 2], n // 2)
                    for q in range(4):
                        g = 4 * m + q
                        last = pe.transpose(pB[:, n % 2, q * P:q * P + w], by_group[t][0:w, g * P:(g + 1) * P],
                                            ident[0:w, 0:w])
                    last.then_inc(u_mm, 1)
                pe.wait_ge(h0_l, 32)
                for i in range(2):
                    last = pe.transpose(pB[:, 2, i * P:(i + 1) * P], h0_in[:, i, :], ident[:, :])
                last.then_inc(h0_mm, 1)
                pe.wait_ge(u_a, 12)
                pe.wait_ge(u_d, 12)
                for k in range(PAIRS):
                    if k >= 2:
                        pe.wait_ge(x_free, k - 1)
                    for i in range(2):
                        for g in range(2):
                            r = slice(g * ST, (g + 1) * ST)
                            last = pe.matmul(pX[r, 2 * (k % 2) + i, 0:CH], S.wx[:, k, i, r], uT[:, 2 * k + g, :],
                                             start=True, stop=True)
                    last.then_inc(x_mm, 1)
                pe.wait_ge(x_free, PAIRS)
                for n in range(24):
                    t, m, r2 = n // 8, n % 8 // 2, n % 2
                    w = WIDTH[t]
                    r = slice(r2 * ST, (r2 + 1) * ST)
                    if n >= 4:
                        pe.wait_ge(y_ok, n - 3)
                    for q in range(4):
                        k = 4 * m + q
                        g = 2 * k + r2
                        if t == 0:
                            pe.wait_ge(h_ok, 2 * (k + 1))
                        c0 = at[t] + (1 if t == 2 else 0)
                        out = pX[0:w, n % 4, q * P:(q + 1) * P]
                        pe.matmul(out, uT[:, g, at[t]:at[t] + w], S.toep[:, g, :], start=True, stop=False)
                        pe.matmul(out, h_re[r, k, c0:c0 + w], S.m_re[r, k, 1:9, :].rearrange("p k o -> p (k o)"),
                                  start=False, stop=False)
                        last = pe.matmul(out, h_im[r, k, c0:c0 + w], S.m_im[r, k, 1:9, :].rearrange("p k o -> p (k o)"),
                                         start=False, stop=True)
                    last.then_inc(y_mm, 1)
                pe.wait_ge(fin_ok, 2 * PAIRS)
                for i, h in enumerate((h_re, h_im)):
                    pe.transpose(pB[0:PAIRS, 3, i * P:(i + 1) * P], h[:, :, NCH], ident[:, :])
                for i in range(2):
                    last = pe.transpose(pB[:, 2, i * P:(i + 1) * P], fin[:, i, :, :].rearrange("p q a -> p (q a)"), ident[:, :])
                last.then_inc(f_mm, 1)

            @block.scalar
            def _(act):
                for n in range(0, 24, 2):
                    t, m = n // 8, n % 8
                    w = WIDTH[t]
                    if m == 0:
                        regroup(act, t, 0)
                    act.wait_ge(u_mm, n + 1)
                    act.activation(uT[:, 4 * m:4 * m + 4, at[t]:at[t] + w],
                                   pB[:, 0, :].rearrange("p (g c) -> p g c", g=4)[:, :, 0:w], ACT.Copy).then_inc(u_a, 1)
                for n in range(24):
                    t, m, r2 = n // 8, n % 8 // 2, n % 2
                    w = WIDTH[t]
                    if t == 2 and n % 8 == 0:
                        act.wait_ge(y_out[0], 16)
                    act.wait_ge(y_mm, n + 1)
                    out = rows[0:w, t % 2, :, :].rearrange("p s (m q r o) -> p m r q s o", m=4, q=4, r=2)[:, m, r2, :, :, :]
                    act.activation(out, pX[0:w, n % 4, :].rearrange("p (q s o) -> p q s o", q=4, s=Q),
                                   ACT.Gelu_apprx_tanh).then_inc(y_ok, 1)

            @block.vector
            def _(dve):
                c = Steps(dve, ch)
                for n in range(1, 24, 2):
                    t, m = n // 8, n % 8
                    w = WIDTH[t]
                    if m == 1:
                        regroup(dve, t, 1)
                    dve.wait_ge(u_mm, n + 1)
                    dve.tensor_copy(uT[:, 4 * m:4 * m + 4, at[t]:at[t] + w],
                                    pB[:, 1, :].rearrange("p (g c) -> p g c", g=4)[:, :, 0:w]).then_inc(u_d, 1)
                dve.wait_ge(h0_mm, 1)
                for i, h in enumerate((h_re, h_im)):
                    dve.tensor_copy(h[:, :, NCH + 1:CH + 1],
                                    pB[:, 2, i * P:(i + 1) * P].rearrange("p (q a) -> p a q", q=NSEQ)).then_inc(h0_ok, 1)
                dve.wait_ge(h0_ok, 2)

                def col(t, k):
                    return t[:, ds(k, 1)]

                def pair(k, b):
                    R, I = pX[:, 2 * b, :], pX[:, 2 * b + 1, :]
                    C = S.rot_c[:, ds(k, 1), :].rearrange("p o c -> p (o c)")
                    N = S.rot_s[:, ds(k, 1), :].rearrange("p o c -> p (o c)")
                    dve.wait_ge(x_mm, k + 1)
                    dve.wait_ge(scan_ok, 2 * k)
                    c.did(dve.tensor_tensor(rot[:, b, 0, :], R[:, 0:NCH], C, ALU.mult))
                    c.did(dve.tensor_tensor(rot[:, b, 1, :], I[:, 0:NCH], N, ALU.mult))
                    c.did(dve.tensor_tensor(rot[:, b, 2, :], I[:, 0:NCH], C, ALU.mult))
                    c.link(dve.tensor_tensor(rot[:, b, 3, :], R[:, 0:NCH], N, ALU.mult))
                    h0r = h_re[:, ds(k, 1), NCH + 1:CH + 1].rearrange("p o c -> p (o c)")
                    h0i = h_im[:, ds(k, 1), NCH + 1:CH + 1].rearrange("p o c -> p (o c)")
                    c.did(dve.scalar_tensor_tensor(out=f1[:, 0, :], in0=h0r, scalar=col(S.a8_re, k), in1=R[:, NCH:CH],
                                                   op0=ALU.mult, op1=ALU.add))
                    c.link(dve.scalar_tensor_tensor(out=f1[:, 1, :], in0=h0r, scalar=col(S.a8_im, k), in1=I[:, NCH:CH],
                                                    op0=ALU.mult, op1=ALU.add))
                    dve.scalar_tensor_tensor(out=fin[:, 0, :, ds(k, 1)].rearrange("p q o -> p (q o)"), in0=h0i,
                                             scalar=col(S.na8_im, k), in1=f1[:, 0, :], op0=ALU.mult, op1=ALU.add).then_inc(fin_ok, 1)
                    dve.scalar_tensor_tensor(out=fin[:, 1, :, ds(k, 1)].rearrange("p q o -> p (q o)"), in0=h0i,
                                             scalar=col(S.a8_re, k), in1=f1[:, 1, :], op0=ALU.mult, op1=ALU.add).then_inc(fin_ok, 1)
                    dve.wait_ge(fin_ok, 2 * k + 2)
                    c.did(dve.tensor_tensor(rot[:, b, 0, :], rot[:, b, 0, :], rot[:, b, 1, :], ALU.add))
                    c.link(dve.tensor_tensor(rot[:, b, 2, :], rot[:, b, 2, :], rot[:, b, 3, :], ALU.subtract))
                    dve.sem_inc(x_free, 1)
                    dve.wait_ge(h_free, k + 1)
                    for i in range(2):
                        dve.tensor_tensor_scan(scan[:, b, i, :], col(S.decay, k).to_broadcast([P, NCH]),
                                               rot[:, b, 2 * i, :], 0.0, ALU.mult, ALU.add).then_inc(scan_ok, 1)

                with dve.Fori(0, PAIRS // 2) as j:
                    c.done = 16 * j
                    pair(2 * j, 0)
                    pair(2 * j + 1, 1)
                assert c.count == 16
                dve.wait_ge(f_mm, 1)
                for i in range(2):
                    dve.tensor_copy(po[:, i, :], pB[0:PAIRS, 3, i * P:(i + 1) * P]).then_inc(f_ok, 1)
                    dve.tensor_copy(fo[:, i, :], pB[:, 2, i * P:(i + 1) * P]).then_inc(f_ok, 1)

            @block.gpsimd
            def _(pool):
                p = Steps(pool, ph)
                pool.wait_ge(u_mm, 24)
                p.did(pool.memset(h_re[:, :, 0:1], 0.0))
                p.link(pool.memset(h_im[:, :, 0:1], 0.0))
                pool.sem_inc(h_free, 2)

                def pair(k, b):
                    C = S.rot_c[:, ds(k, 1), :].rearrange("p o c -> p (o c)")
                    N = S.rot_s[:, ds(k, 1), :].rearrange("p o c -> p (o c)")
                    re = h_re[:, ds(k, 1), 1:NCH + 1].rearrange("p o c -> p (o c)")
                    im = h_im[:, ds(k, 1), 1:NCH + 1].rearrange("p o c -> p (o c)")
                    pool.wait_ge(scan_ok, 2 * k + 2)
                    p.did(pool.tensor_tensor(re, scan[:, b, 0, :], C, ALU.mult))
                    p.did(pool.tensor_tensor(im, scan[:, b, 0, :], N, ALU.mult))
                    p.did(pool.tensor_tensor(back[:, 0, :], scan[:, b, 1, :], N, ALU.mult))
                    p.link(pool.tensor_tensor(back[:, 1, :], scan[:, b, 1, :], C, ALU.mult))
                    pool.sem_inc(h_free, 1)
                    pool.tensor_tensor(re, re, back[:, 0, :], ALU.subtract).then_inc(h_ok, 1)
                    pool.tensor_tensor(im, im, back[:, 1, :], ALU.add).then_inc(h_ok, 1)
                    pool.wait_ge(h_ok, 2 * k + 2)

                with pool.Fori(0, PAIRS // 2) as j:
                    p.done = 2 + 8 * j
                    pair(2 * j, 0)
                    pair(2 * j + 1, 1)
                assert p.count == 10


def mixout(nc, S, a):
    with ExitStack() as st:
        sb, sem = S.sb, S.sem
        wout = sb(st, "wout", [P, KD, D])
        wglu = sb(st, "wglu", [P, 4, DA])
        wr = sb(st, "wr", [P, KD, NR])
        bglu = sb(st, "bglu", [P, DA])
        br = sb(st, "br", [P, NR])
        gate = sb(st, "gate1", [P, D])
        gain = sb(st, "gain2", [P, D])
        shift = sb(st, "shift2", [P, D])
        cat = sb(st, "cat", [P, 2, D])
        y = sb(st, "y", [P, 2, DA])
        yT = sb(st, "yT", [P, 2, 4, P])
        catT = sb(st, "catT", [P, 2, KD, P])
        z = sb(st, "z", [P, DA])
        mixed = sb(st, "mixed", [P, 2, DA])
        h2 = sb(st, "h2", [P, D])
        h2T = sb(st, "h2T", [P, KD, P])
        junk = sb(st, "junk3", [P, D])
        ssq = sb(st, "ssq2", [P, 1])
        rstd = sb(st, "rstd2", [P, 1])
        newton = sb(st, "newton2", [P, 2])
        pY = S.psum(st, "ps_yT", [P, 512])
        pZ = S.psum(st, "ps_z", [P, 512])
        pC = S.psum(st, "ps_catT", [P, 2, 512])
        pM = S.psum(st, "ps_out", [P, 2, 512])
        pH = S.psum(st, "ps_h2T", [P, 2, 512])
        ident, x2, lg = S.ident, S.x2, S.logits

        mod_in, mod_s, w_in, a_in = sem("mod2_loaded"), sem("mod2_sample_loaded"), sem("wout_loaded"), [sem("cat_loaded0"), sem("cat_loaded1")]
        wg_in, yT_mm, yT_ok, z_mm, z_ok, sg_ok, b_ok = sem("wglu_loaded"), sem("yT_mm"), sem("yT_ok"), sem("z_mm"), sem("z_ok"), sem("sigmoid_ok"), sem("b_ready")
        c_mm, c_a, c_d, o_mm, mul_ok, x2_ok = sem("catT_mm"), sem("catT_act"), sem("catT_dve"), sem("out_mm"), sem("gated"), sem("x2_ready")
        sq_ok, xs_ok, h2_ok, h_mm, h_a, h_d, l_mm, l_ok, h2_out, ch = (sem("ssq2_ready"), sem("x2_scaled"), sem("h2_ready"), sem("h2T_mm"), sem("h2T_act"), sem("h2T_dve"), sem("logit_mm"), sem("logits_ready"), sem("h2_stored"), sem("dve_chain3"))

        def rows_of(i):
            return NS if isinstance(i, int) and i == TP else P

        def dr(t, i):
            return t[TP * P:TOK, :] if isinstance(i, int) and i == TP else t[ds(i * P, P), :]

        def x2_of(i, cols=slice(0, D)):
            return x2[0:rows_of(i), ds(i, 1), cols].rearrange("p o n -> p (o n)")

        def tiles(eng, step):
            step(0, 0, 0)
            prompt_loop(eng, 1, step)
            step(15, 7, 1)
            step(16, 8, 0)

        with nc.Block() as block:
            @block.sync
            def _(sp):
                def load(i, n, b):
                    r = rows_of(i)
                    x = a.x_sample.rearrange("b t d -> (b t) d") if r == NS else a.x_prompt[0, ds(i * P, P), :]
                    sp.dma_start(y[0:r, b, :], dr(S.y_d, i)).then_inc(a_in[b], 16)
                    sp.dma_start(cat[0:r, b, 0:DA], dr(S.a_d, i)).then_inc(a_in[b], 16)
                    sp.dma_start(x2_of(i), x).then_inc(a_in[b], 16)

                load(0, 0, 0)
                sp.dma_start(wglu[:, :, :], a.w_glu[0].rearrange("(k p) n -> p k n", p=P)).then_inc(wg_in, 16)
                sp.dma_start(bglu[:, :], a.b_glu.to_broadcast([P, DA])).then_inc(wg_in, 16)
                sp.dma_start(wout[:, :, :], a.w_out[0].rearrange("(k p) n -> p k n", p=P)).then_inc(w_in, 16)
                for t, c in ((gate, 2), (gain, 4), (shift, 3)):
                    sp.dma_start(t[:, :], S.ada_d[0:1, c * D:(c + 1) * D].to_broadcast([P, D])).then_inc(mod_in, 16)
                load(1, 0, 1)
                sp.dma_start(wr[:, :, 0:EG], a.w_group[0].rearrange("(k p) n -> p k n", p=P)).then_inc(mod_in, 16)
                sp.dma_start(wr[:, :, EG:NR], a.w_expert[0].rearrange("(k p) n -> p k n", p=P)).then_inc(mod_in, 16)
                sp.dma_start(br[:, 0:EG], a.b_group.to_broadcast([P, EG])).then_inc(mod_in, 16)
                sp.dma_start(br[:, EG:NR], a.b_expert.to_broadcast([P, NE])).then_inc(mod_in, 16)

                def step(i, n, b):
                    static = isinstance(i, int)
                    if not (static and i + 2 > TP):
                        sp.wait_ge(c_mm, i + 1)
                        load(i + 2, n + 1, b)
                    if static and i == TP:
                        for q in range(NSEQ):
                            sp.dma_start(gate[q * DSEQ:(q + 1) * DSEQ, :],
                                         S.ada_d[1 + q:2 + q, 2 * D:3 * D].to_broadcast([DSEQ, D])).then_inc(mod_s, 16)
                        for t, c in ((gain, 4), (shift, 3)):
                            for q in range(NSEQ):
                                sp.dma_start(t[q * DSEQ:(q + 1) * DSEQ, :],
                                             S.ada_d[1 + q:2 + q, c * D:(c + 1) * D].to_broadcast([DSEQ, D])).then_inc(mod_s, 16)
                    sp.wait_ge(h2_ok, i + 1)
                    sp.dma_start(dr(S.h2_d, i), h2[0:rows_of(i), :]).then_inc(h2_out, 16)

                prompt_loop(sp, 0, step)
                for i in (14, 15, 16):
                    step(i, i // 2, i % 2)
                sp.wait_ge(h2_out, 16 * NT)

            @block.tensor
            def _(pe):
                def turn_y(i, n, b):
                    r = rows_of(i)
                    pe.wait_ge(a_in[b], 48 * n + 48)
                    pe.wait_ge(yT_ok, i)
                    for k in range(4):
                        last = pe.transpose(pY[:, k * P:k * P + r], y[0:r, b, k * P:(k + 1) * P], ident[0:r, 0:r])
                    last.then_inc(yT_mm, 1)

                def glu(i, n, b, logits_out):
                    r = rows_of(i)
                    pe.wait_ge(yT_ok, i + 1)
                    pe.wait_ge(l_ok, logits_out)
                    for k in range(4):
                        last = pe.matmul(pZ[0:r, :], yT[:, b, k, 0:r], wglu[:, k, :], start=k == 0, stop=k == 3)
                    last.then_inc(z_mm, 1)

                def turn_cat(i, n, b):
                    r = rows_of(i)
                    pe.wait_ge(b_ok, i + 1)
                    pe.wait_ge(c_a, i)
                    pe.wait_ge(c_d, i)
                    for k in range(KD):
                        last = pe.transpose(pC[:, k // 4, k % 4 * P:k % 4 * P + r], cat[0:r, b, k * P:(k + 1) * P],
                                            ident[0:r, 0:r])
                    last.then_inc(c_mm, 1)

                def project(i, b, c):
                    r = rows_of(i)
                    pe.wait_ge(c_a, i + 1)
                    pe.wait_ge(c_d, i + 1)
                    pe.wait_ge(mul_ok, 2 * i + c - (1 if isinstance(i, int) and i == 0 and c else 0))
                    for k in range(KD):
                        last = pe.matmul(pM[0:r, c, :], catT[:, b, k, 0:r], wout[:, k, c * DA:(c + 1) * DA],
                                         start=k == 0, stop=k == KD - 1)
                    last.then_inc(o_mm, 1)

                def logits(i, z_done):
                    r = rows_of(i)
                    pe.wait_ge(h2_ok, i + 1)
                    pe.wait_ge(h_a, i)
                    pe.wait_ge(h_d, i)
                    for k in range(KD):
                        last = pe.transpose(pH[:, k // 4, k % 4 * P:k % 4 * P + r], h2[0:r, k * P:(k + 1) * P],
                                            ident[0:r, 0:r])
                    last.then_inc(h_mm, 1)
                    pe.wait_ge(h_a, i + 1)
                    pe.wait_ge(h_d, i + 1)
                    pe.wait_ge(z_ok, z_done)
                    for k in range(KD):
                        last = pe.matmul(pZ[0:r, 0:NR], h2T[:, k, 0:r], wr[:, k, :], start=k == 0, stop=k == KD - 1)
                    last.then_inc(l_mm, 1)

                def step(i, n, b):
                    first, last = isinstance(i, int) and i == 0, isinstance(i, int) and i == TP
                    if not last:
                        turn_y(i + 1, n + b, 1 - b)
                    project(i, b, 0)
                    if not last:
                        glu(i + 1, n + b, 1 - b, 0 if first else i - 1)
                    project(i, b, 1)
                    if not last:
                        turn_cat(i + 1, n + b, 1 - b)
                    if not first:
                        logits(i - 1, NT if last else i + 2)

                turn_y(0, 0, 0)
                pe.wait_ge(wg_in, 32)
                glu(0, 0, 0, 0)
                turn_cat(0, 0, 0)
                pe.wait_ge(w_in, 16)
                pe.wait_ge(mod_in, 16 * 7)
                tiles(pe, step)
                logits(TP, NT)

            @block.scalar
            def _(act):
                def evac_y(i, b):
                    r = rows_of(i)
                    act.wait_ge(yT_mm, i + 1)
                    act.activation(yT[:, b, :, 0:r], pY[:, :].rearrange("p (k t) -> p k t", k=4)[:, :, 0:r], ACT.Copy).then_inc(yT_ok, 1)

                def sigmoid(i, b):
                    r = rows_of(i)
                    act.wait_ge(z_ok, i + 1)
                    act.activation(z[0:r, :], z[0:r, :], ACT.Sigmoid).then_inc(sg_ok, 1)

                def evac(i, b):
                    r = rows_of(i)
                    act.wait_ge(c_mm, i + 1)
                    act.activation(catT[:, b, 0:4, 0:r], pC[:, 0, :].rearrange("p (k t) -> p k t", k=4)[:, :, 0:r],
                                   ACT.Copy).then_inc(c_a, 1)

                def evac_h(i):
                    r = rows_of(i)
                    act.wait_ge(h_mm, i + 1)
                    act.wait_ge(l_mm, i)
                    act.activation(h2T[:, 0:4, 0:r], pH[:, 0, :].rearrange("p (k t) -> p k t", k=4)[:, :, 0:r],
                                   ACT.Copy).then_inc(h_a, 1)

                def step(i, n, b):
                    first, last = isinstance(i, int) and i == 0, isinstance(i, int) and i == TP
                    if not last:
                        evac_y(i + 1, 1 - b)
                        sigmoid(i + 1, 1 - b)
                        evac(i + 1, 1 - b)
                    if not first:
                        evac_h(i - 1)
                    act.wait_ge(x2_ok, 2 * i + 2)
                    act.wait_ge(xs_ok, i)
                    act.activation(junk[0:rows_of(i), :], x2_of(i), ACT.Square,
                                   accum_out=ssq[0:rows_of(i), :]).then_inc(sq_ok, 1)

                evac_y(0, 0)
                sigmoid(0, 0)
                evac(0, 0)
                tiles(act, step)
                evac_h(TP)

            @block.gpsimd
            def _(pool):
                def gate_y(i, n, b):
                    r = rows_of(i)
                    pool.wait_ge(sg_ok, i + 1)
                    pool.tensor_tensor(cat[0:r, b, DA:D], y[0:r, b, :], z[0:r, :], ALU.mult).then_inc(b_ok, 1)

                def residual(i, c):
                    r = rows_of(i)
                    pool.wait_ge(mul_ok, 2 * i + c + 1)
                    half = x2_of(i, slice(c * DA, (c + 1) * DA))
                    pool.tensor_tensor(half, half, mixed[0:r, c, :], ALU.add).then_inc(x2_ok, 1)

                def step(i, n, b):
                    r = rows_of(i)
                    last = isinstance(i, int) and i == TP
                    residual(i, 0)
                    if not last:
                        gate_y(i + 1, n + b, 1 - b)
                    residual(i, 1)
                    pool.wait_ge(xs_ok, i + 1)
                    pool.tensor_tensor(h2[0:r, :], h2[0:r, :], shift[0:r, :], ALU.add).then_inc(h2_ok, 1)

                pool.wait_ge(a_in[0], 48)
                gate_y(0, 0, 0)
                pool.wait_ge(mod_in, 16 * 7)
                tiles(pool, step)

            @block.vector
            def _(dve):
                c = Steps(dve, ch)

                def gated(i, h):
                    r = rows_of(i)
                    dve.wait_ge(o_mm, 2 * i + h + 1)
                    dve.wait_ge(x2_ok, 2 * i)
                    dve.tensor_tensor(mixed[0:r, h, :], pM[0:r, h, :], gate[0:r, h * DA:(h + 1) * DA], ALU.mult).then_inc(mul_ok, 1)

                def bias_z(i):
                    r = rows_of(i)
                    dve.wait_ge(z_mm, i + 1)
                    dve.wait_ge(b_ok, i)
                    dve.tensor_tensor(z[0:r, :], pZ[0:r, :], bglu[0:r, :], ALU.add).then_inc(z_ok, 1)

                def evac(i, b):
                    r = rows_of(i)
                    dve.wait_ge(c_mm, i + 1)
                    dve.tensor_copy(catT[:, b, 4:8, 0:r],
                                    pC[:, 1, :].rearrange("p (k t) -> p k t", k=4)[:, :, 0:r]).then_inc(c_d, 1)

                def logits(i):
                    r = rows_of(i)
                    dve.wait_ge(h_mm, i + 1)
                    dve.wait_ge(l_mm, i)
                    dve.tensor_copy(h2T[:, 4:8, 0:r],
                                    pH[:, 1, :].rearrange("p (k t) -> p k t", k=4)[:, :, 0:r]).then_inc(h_d, 1)
                    dve.wait_ge(l_mm, i + 1)
                    dve.tensor_tensor(lg[0:r, ds(i, 1), :].rearrange("p o n -> p (o n)"), pZ[0:r, 0:NR], br[0:r, :],
                                      ALU.add).then_inc(l_ok, 1)

                def step(i, n, b):
                    r = rows_of(i)
                    first, last = isinstance(i, int) and i == 0, isinstance(i, int) and i == TP
                    if last:
                        dve.wait_ge(mod_s, 16 * 3 * NSEQ)
                    gated(i, 0)
                    if not last:
                        bias_z(i + 1)
                    gated(i, 1)
                    if not last:
                        evac(i + 1, 1 - b)
                    if not first:
                        logits(i - 1)
                    dve.wait_ge(sq_ok, i + 1)
                    inv_sqrt(dve, c, rstd[0:r, :], ssq[0:r, :], 1.0 / D, newton[0:r, 0:1], newton[0:r, 1:2])
                    dve.wait_ge(h_mm, i)
                    dve.wait_ge(h2_out, 16 * i)
                    dve.scalar_tensor_tensor(out=h2[0:r, :], in0=x2_of(i), scalar=rstd[0:r, :], in1=gain[0:r, :],
                                             op0=ALU.mult, op1=ALU.mult).then_inc(xs_ok, 1)

                dve.wait_ge(wg_in, 32)
                bias_z(0)
                evac(0, 0)
                dve.wait_ge(mod_in, 16 * 7)
                step(0, 0, 0)
                with dve.Fori(0, 7) as j:
                    c.done = INV + 2 * INV * j
                    step(2 * j + 1, j, 1)
                    step(2 * j + 2, j + 1, 0)
                c.done = 15 * INV
                step(15, 7, 1)
                step(16, 8, 0)
                logits(TP)


COLS = NBLK + 3


def route(nc, S):
    with ExitStack() as st:
        sb, sem = S.sb, S.sem
        N2 = 2 * NT
        iota = sb(st, "iota", [P, P])
        tok = sb(st, "tok", [P, N2])
        w4 = sb(st, "w4", [P, EG])
        w32 = sb(st, "w32", [P, NE])
        e32 = sb(st, "e32", [P, NE])
        k128 = sb(st, "k128", [P, NT])
        upper = sb(st, "upper", [P, P])
        ones = sb(st, "ones", [P, P])
        zeros = sb(st, "zeros", [P, 2 * COLS])
        s1 = [sb(st, f"r_one{i}", [P, NT]) for i in range(8)]
        g4 = [sb(st, f"r_four{i}", [P, NT, EG]) for i in range(3)]
        em = sb(st, "r_em", [P, NT, NE])
        oh = [sb(st, f"r_oh{i}", [P, NT, NE]) for i in range(2)]
        picked = sb(st, "r_picked", [P, NT, NE])
        cum = sb(st, "r_cum", [P, NT, NE])
        tot = sb(st, "r_tot", [P, NT, NE])
        cnt, nb, pend, pst, act, rix, t32 = (sb(st, f"r_{n}", [P, NE]) for n in ("cnt", "nb", "pend", "pst", "act", "rix", "t32"))
        cmp17 = sb(st, "r_cmp", [P, NE, NT])
        dest = sb(st, "r_dest", [P, N2])
        bi = sb(st, "r_bi", [P, N2], I32)
        ji = sb(st, "r_ji", [P, N2], I32)
        bf = sb(st, "r_bf", [P, N2])
        jf = sb(st, "r_jf", [P, N2])
        gates = sb(st, "r_gates", [P, N2])
        ohj = sb(st, "r_ohj", [P, 2, P])
        ohb = sb(st, "r_ohb", [P, 2, 2, COLS])
        big = sb(st, "r_big", [1, COLS, NE])
        row = sb(st, "r_row", [1, COLS])
        pre = S.psum(st, "ps_pre", [P, 2, 512])
        pt = S.psum(st, "ps_tot", [P, 2, 512])
        acc = S.psum(st, "ps_slots", [P, 512])
        const_ok, ch, diff_ok, exp_ok = sem("const_ready"), sem("dve_chain4"), sem("diff_ready"), sem("exp_ready")
        one_ok, pre_mm, ohs_ok, acc_mm = sem("onehot_ready"), sem("counts_mm"), sem("slot_onehots"), sem("slots_mm")
        CUT = (0, 9, NT)
        lg = S.logits
        s4, s32 = [P, NT, EG], [P, NT, NE]

        with nc.Block() as block:
            @block.gpsimd
            def _(pool):
                c = Steps(pool, const_ok)

                def iota_f(t, pattern, base, mult):
                    c.did(pool.iota(t, pattern, base=base, channel_multiplier=mult, allow_small_or_imprecise_dtypes=True))

                iota_f(iota[:, :], [[1, P]], 0, 0)
                iota_f(tok[:, :].rearrange("p (k i) -> p k i", k=2), [[0, 2], [P, NT]], 0, 1)
                iota_f(w4[:, :], [[-1, EG]], EG, 0)
                iota_f(w32[:, :], [[-1, NE]], NE, 0)
                iota_f(e32[:, :], [[1, NE]], 0, 0)
                iota_f(k128[:, :], [[P, NT]], 0, 0)
                c.did(pool.memset(ones[:, :], 1.0))
                c.did(pool.memset(zeros[:, :], 0.0))
                c.link(pool.memset(upper[:, :], 1.0))
                c.did(pool.affine_select(out=upper[:, :], in_=upper[:, :], compare_op=ALU.is_gt, fill=0.0, base=0,
                                         pattern=[[1, P]], channel_multiplier=-1))

            @block.scalar
            def _(act_):
                act_.wait_ge(diff_ok, 1)
                act_.activation(g4[1][:, :, :], g4[0][:, :, :], ACT.Exp).then_inc(exp_ok, 1)
                act_.wait_ge(diff_ok, 2)
                act_.activation(s1[5][:, :], s1[4][:, :], ACT.Exp).then_inc(exp_ok, 1)

            @block.tensor
            def _(pe):
                pe.wait_ge(const_ok, 10)
                pe.wait_ge(one_ok, 1)
                for i in range(2):
                    w = (CUT[i + 1] - CUT[i]) * NE
                    rhs = picked[:, CUT[i]:CUT[i + 1], :].rearrange("p i e -> p (i e)")
                    pe.matmul(pre[:, i, 0:w], upper[:, :], rhs, start=True, stop=True).then_inc(pre_mm, 1)
                    pe.matmul(pt[:, i, 0:w], ones[:, :], rhs, start=True, stop=True).then_inc(pre_mm, 1)
                out = acc[:, 0:2 * COLS]
                pe.matmul(out, ones[:, :], zeros[:, :], start=True, stop=False)
                pe.sem_inc(acc_mm, 2)
                with pe.Fori(0, NT) as j:
                    for b in range(2):
                        pe.wait_ge(ohs_ok, 2 * j + b + 1)
                        pe.matmul(out, ohj[:, b, :], ohb[:, b, :, :].rearrange("p t c -> p (t c)"),
                                  start=False, stop=False).then_inc(acc_mm, 1)
                pe.matmul(out, ones[:, :], zeros[:, :], start=False, stop=True).then_inc(acc_mm, 1)

            @block.vector
            def _(dve):
                c = Steps(dve, ch)

                def tt(out, x, y, op):
                    c.link(dve.tensor_tensor(out, x, y, op))

                def ts(out, x, v1, v2, op1, op2=ALU.bypass):
                    c.link(dve.tensor_scalar(out, x, v1, v2, op1, op2) if v2 is not None
                           else dve.tensor_scalar(out, x, v1, None, op1))

                def red(out, x, op):
                    c.link(dve.tensor_reduce(out, x, AX.X, op))

                def first_max(hot, x, weights, best, shape):
                    red(best, x, ALU.max)
                    tt(hot, x, fan(best, shape), ALU.is_equal)
                    tt(hot, hot, weights.unsqueeze(1).to_broadcast(shape), ALU.mult)
                    red(s1[7][:, :], hot, ALU.max)
                    tt(hot, hot, fan(s1[7][:, :], shape), ALU.is_equal)

                gmax, gsum, gw, m1, diff, ex, m2 = (t[:, :] for t in s1[:7])
                dve.wait_ge(const_ok, 10)
                c.link(dve.memset(lg[NS:P, TP, :], 0.0))
                gl, el = lg[:, :, 0:EG], lg[:, :, EG:NR]
                ohg = g4[2][:, :, :]
                first_max(ohg, gl, w4[:, :], gmax, s4)
                dve.tensor_tensor(g4[0][:, :, :], gl, fan(gmax, s4), ALU.subtract).then_inc(diff_ok, 1)
                ts(ohg, ohg, BIG, BIG, ALU.mult, ALU.subtract)
                e4 = em[:, :, :].rearrange("p i (g e) -> p i g e", g=EG)
                tt(e4, el.rearrange("p i (g e) -> p i g e", g=EG),
                   ohg.unsqueeze(3).to_broadcast([P, NT, EG, EPG]), ALU.add)
                hot = [t[:, :, :] for t in oh]
                first_max(hot[0], em[:, :, :], w32[:, :], m1, s32)
                c.link(dve.scalar_tensor_tensor(out=em[:, :, :], in0=hot[0], scalar=-BIG, in1=em[:, :, :], op0=ALU.mult, op1=ALU.add))
                first_max(hot[1], em[:, :, :], w32[:, :], m2, s32)
                dve.tensor_tensor(diff, m2, m1, ALU.subtract).then_inc(diff_ok, 1)
                for t in oh:
                    c.link(dve.memset(t[NS:P, TP, :], 0.0))
                dve.tensor_tensor(picked[:, :, :], hot[0], hot[1], ALU.add).then_inc(one_ok, 1)
                dve.wait_ge(exp_ok, 2)
                red(gsum, g4[1][:, :, :], ALU.add)
                c.link(dve.reciprocal(gw, gsum))
                ts(m1, ex, 1.0, None, ALU.add)
                c.link(dve.reciprocal(m1, m1))
                tt(gates[:, 0:NT], gw, m1, ALU.mult)
                tt(gates[:, NT:N2], gates[:, 0:NT], ex, ALU.mult)
                for k in range(2):
                    at = k * NT + TP
                    c.did(dve.memset(gates[NS:P, at:at + 1], 0.0))
                    c.link(dve.memset(tok[NS:P, at:at + 1], 0.0))
                dve.wait_ge(pre_mm, 4)
                for i in range(2):
                    w = (CUT[i + 1] - CUT[i]) * NE
                    c.link(dve.tensor_copy(tot[:, CUT[i]:CUT[i + 1], :].rearrange("p i e -> p (i e)"), pt[:, i, 0:w]))
                c.link(dve.memset(cum[:, 0, :], 0.0))
                for i in range(1, NT):
                    tt(cum[:, i, :], cum[:, i - 1, :], tot[:, i - 1, :], ALU.add)
                tt(cnt[:, :], cum[:, TP, :], tot[:, TP, :], ALU.add)
                tt(cmp17[:, :, :], fan(cnt[:, :], [P, NE, NT]), k128[:, :].unsqueeze(1).to_broadcast([P, NE, NT]), ALU.is_gt)
                red(nb[:, :], cmp17[:, :, :], ALU.add)
                c.link(dve.tensor_tensor_scan(pend[:, :], ones[:, 0:NE], nb[:, :], 0.0, ALU.mult, ALU.add))
                tt(pst[:, :], pend[:, :], nb[:, :], ALU.subtract)
                ts(t32[:, :], pst[:, :], float(P), None, ALU.mult)
                tt(cum[:, :, :], cum[:, :, :], t32[:, :].unsqueeze(1).to_broadcast(s32), ALU.add)
                for i in range(2):
                    w = (CUT[i + 1] - CUT[i]) * NE
                    part = cum[:, CUT[i]:CUT[i + 1], :].rearrange("p i e -> p (i e)")
                    tt(part, part, pre[:, i, 0:w], ALU.add)
                for k in range(2):
                    tt(picked[:, :, :], hot[k], cum[:, :, :], ALU.mult)
                    red(dest[:, k * NT:(k + 1) * NT], picked[:, :, :], ALU.add)
                c.link(dve.tensor_copy(S.dest[:, :], dest[:, :]))
                ts(bi[:, :], S.dest[:, :], 7, None, ALU.arith_shift_right)
                ts(ji[:, :], S.dest[:, :], P - 1, None, ALU.bitwise_and)
                c.link(dve.tensor_copy(bf[:, :], bi[:, :]))
                c.link(dve.tensor_copy(jf[:, :], ji[:, :]))
                with dve.Fori(0, NT) as j:
                    for b in range(2):
                        n = 2 * j + b
                        dve.wait_ge(acc_mm, n + 1)
                        dve.tensor_scalar(ohj[:, b, :], iota[:, :], jf[:, ds(n, 1)], None, ALU.is_equal)
                        dve.tensor_scalar(ohb[:, b, 0, :], iota[:, 0:COLS], bf[:, ds(n, 1)], tok[:, ds(n, 1)],
                                          ALU.is_equal, ALU.mult)
                        dve.tensor_scalar(ohb[:, b, 1, :], iota[:, 0:COLS], bf[:, ds(n, 1)], gates[:, ds(n, 1)],
                                          ALU.is_equal, ALU.mult).then_inc(ohs_ok, 1)
                ts(act[:, :], cnt[:, :], 0.0, None, ALU.is_gt)
                c.link(dve.tensor_tensor_scan(rix[:, :], ones[:, 0:NE], act[:, :], 0.0, ALU.mult, ALU.add))
                c.link(dve.tensor_copy(S.n_blocks[:, 0:1], pend[0:1, NE - 1:NE]))
                c.link(dve.tensor_copy(S.n_blocks[:, 1:2], rix[0:1, NE - 1:NE]))
                shape = [1, COLS, NE]
                b3 = big[:, :, :]
                tt(b3, fan(iota[0:1, 0:COLS], shape), pst[0:1, :].unsqueeze(1).to_broadcast(shape), ALU.is_ge)
                tt(b3, b3, act[0:1, :].unsqueeze(1).to_broadcast(shape), ALU.mult)
                red(row[:, :], b3, ALU.add)
                ts(row[:, :], row[:, :], -1.0, None, ALU.add)
                c.link(dve.tensor_copy(S.block_run[:, :], row[:, :]))
                shape = [1, NE, NE]
                for out, by, back in ((S.run_expert, e32, 0), (S.run_free, pst, RING - 1)):
                    b3 = big[:, 0:NE, :]
                    ts(row[:, 0:NE], e32[0:1, :], float(1 - back), None, ALU.add)
                    tt(b3, fan(row[:, 0:NE], shape), rix[0:1, :].unsqueeze(1).to_broadcast(shape), ALU.is_equal)
                    tt(b3, b3, act[0:1, :].unsqueeze(1).to_broadcast(shape), ALU.mult)
                    tt(b3, b3, by[0:1, :].unsqueeze(1).to_broadcast(shape), ALU.mult)
                    red(row[:, 0:NE], b3, ALU.add)
                    c.link(dve.tensor_copy(out[:, :], row[:, 0:NE]))
                dve.wait_ge(acc_mm, 2 + N2 + 1)
                c.did(dve.tensor_copy(S.slot_tok[:, :], acc[:, 0:COLS]))
                c.link(dve.tensor_copy(S.slot_gate[:, :], acc[:, COLS:2 * COLS]))


def experts(nc, S, a):
    with ExitStack() as st:
        sb, sem = S.sb, S.sem
        UP, DOWN = KD * 2 * DE, 2 * D
        SIZE = UP + DOWN
        w = sb(st, "expert_w", [P, RING * SIZE])
        xg = sb(st, "xg", [P, 2, D])
        xT = sb(st, "xT", [P, 2, KD, P])
        idx = sb(st, "idx", [P, 2], I32)
        gcol = sb(st, "gcol", [P, 2])
        act_v = sb(st, "silu", [P, DE])
        hid = sb(st, "hid", [P, DE])
        hT = sb(st, "hidT", [P, 2, P])
        yo = sb(st, "yo", [P, 2, D])
        pX = S.psum(st, "ps_xT", [P, 2, 512])
        pU = S.psum(st, "ps_up", [P, 512])
        pT = S.psum(st, "ps_hidT", [P, 512])
        pY = S.psum(st, "ps_y", [P, 2, 512])
        ident = S.ident

        w_in = [sem(f"expert_loaded{i}") for i in range(RING)]
        g_in, y_out = [sem("gathered0"), sem("gathered1")], [sem("y_row_stored0"), sem("y_row_stored1")]
        idx_ok, x_mm, x_a, x_d, u_mm, s_ok, h_ok, t_mm, t_ok, y_mm, y_a, y_d, gc_ok = (sem(n) for n in (
            "idx_ready", "x_mm", "x_act", "x_dve", "up_mm", "silu_ok", "hid_ok", "hid_mm", "hidT_ok", "down_mm",
            "y_act", "y_dve", "gate_col"))
        tail = sem("experts_end")
        idx_seen = sem("idx_seen")
        up = a.w1[0].rearrange("e (k p) n -> e p k n", p=P)
        up3 = a.w3[0].rearrange("e (k p) n -> e p k n", p=P)
        down = a.w2[0].rearrange("e (k p) n -> e p k n", p=P)

        def blocks(eng, step):
            n = eng.value_load(S.n_blocks[0:1, 0:1], min_val=1, max_val=NBLK)
            with eng.Fori(0, NBLK // 2) as j:
                for t in (1, 2):
                    with eng.If(2 * j + t <= n):
                        step(2 * j + t, j, t)
            return n

        with nc.Block() as block:
            @block.sync
            def _(sp):
                runs = sp.value_load(S.n_blocks[0:1, 1:2], min_val=1, max_val=NE)
                with sp.Fori(0, NE // RING) as j:
                    for q in range(RING):
                        r = RING * j + q
                        with sp.If(r < runs):
                            e = sp.value_load(S.run_expert[0:1, ds(r, 1)], min_val=0, max_val=NE - 1)
                            free = sp.value_load(S.run_free[0:1, ds(r, 1)], min_val=0, max_val=NBLK)
                            sp.wait_ge(y_mm, free)
                            wb = w[:, q * SIZE:(q + 1) * SIZE]
                            w13 = wb[:, 0:UP].rearrange("p (k t n) -> p k t n", k=KD, t=2)
                            sp.dma_start(w13[:, :, 0, :], up[ds(e, 1), :, :, :].rearrange("o p k n -> p (o k) n")).then_inc(w_in[q], 16)
                            sp.dma_start(w13[:, :, 1, :], up3[ds(e, 1), :, :, :].rearrange("o p k n -> p (o k) n")).then_inc(w_in[q], 16)
                            sp.dma_start(wb[:, UP:SIZE].rearrange("p (k n) -> p k n", k=2),
                                         down[ds(e, 1), :, :, :].rearrange("o p k n -> p (o k) n")).then_inc(w_in[q], 16)

            @block.gpsimd
            def _(pool):
                def gather(b, par):
                    pool.tensor_copy(idx[:, par:par + 1], S.slot_tok[:, ds(b, 1)]).then_inc(idx_ok, 1)
                    pool.wait_ge(idx_ok, b + 1)
                    pool.sem_inc(idx_seen, 1)
                    pool.indirect_dma_start(out=xg[:, par, :], out_offset=None, in_=S.h2_d,
                                            in_offset=bass.IndirectOffsetOnAxis(ap=idx[:, par:par + 1], axis=0)).then_inc(g_in[par], 16)

                def step(b, j, t):
                    pool.wait_ge(x_mm, b + 1)
                    gather(b + 2, t % 2)

                gather(0, 0)
                gather(1, 1)
                pool.wait_ge(x_mm, 1)
                gather(2, 0)
                blocks(pool, step)

            @block.tensor
            def _(pe):
                def turn_x(b, n, par):
                    pe.wait_ge(g_in[par], 16 * n + 16)
                    pe.wait_ge(x_a, b)
                    pe.wait_ge(x_d, b)
                    for k in range(KD):
                        last = pe.transpose(pX[:, k // 4, k % 4 * P:(k % 4 + 1) * P], xg[:, par, k * P:(k + 1) * P], ident[:, :])
                    last.then_inc(x_mm, 1)

                def run_of(b):
                    return pe.value_load(S.block_run[0:1, ds(b, 1)], min_val=0, max_val=NE - 1)

                def at(run):
                    return (run % RING) * SIZE

                def up_mm(b, par, run):
                    for q in range(RING):
                        pe.wait_ge(w_in[q], 48 * ((run + (RING - q)) // RING))
                    pe.wait_ge(x_a, b + 1)
                    pe.wait_ge(x_d, b + 1)
                    pe.wait_ge(h_ok, b)
                    base = pe.snap(at(run))
                    for k in range(KD):
                        last = pe.matmul(pU[:, :], xT[:, par, k, :], w[:, ds(base + k * 2 * DE, 2 * DE)],
                                         start=k == 0, stop=k == KD - 1)
                    last.then_inc(u_mm, 1)

                def down_mm(b, run):
                    pe.wait_ge(t_ok, b + 1)
                    pe.wait_ge(y_a, b)
                    pe.wait_ge(y_d, b)
                    base = pe.snap(at(run))
                    for c in range(2):
                        for k in range(2):
                            last = pe.matmul(pY[:, c, :], hT[:, k, :], w[:, ds(base + (UP + k * D + c * 512), 512)],
                                             start=k == 0, stop=k == 1)
                    last.then_inc(y_mm, 1)

                def turn_hid(b):
                    pe.wait_ge(h_ok, b + 1)
                    pe.wait_ge(t_ok, b)
                    for k in range(2):
                        last = pe.transpose(pT[:, k * P:(k + 1) * P], hid[:, k * P:(k + 1) * P], ident[:, :])
                    last.then_inc(t_mm, 1)

                def step(b, j, t):
                    turn_x(b + 1, j + (t + 1) // 2, (t + 1) % 2)
                    up_mm(b, t % 2, run_of(b))
                    down_mm(b - 1, run_of(b - 1))
                    turn_hid(b)

                turn_x(0, 0, 0)
                turn_x(1, 0, 1)
                up_mm(0, 0, run_of(0))
                turn_hid(0)
                blocks(pe, step)

            @block.scalar
            def _(act):
                def evac_x(b, par):
                    act.wait_ge(x_mm, b + 1)
                    act.activation(xT[:, par, 0:4, :], pX[:, 0, :].rearrange("p (k t) -> p k t", k=4), ACT.Copy).then_inc(x_a, 1)

                def silu(b):
                    act.wait_ge(u_mm, b + 1)
                    act.activation(act_v[:, :], pU[:, 0:DE], ACT.Silu).then_inc(s_ok, 1)

                def out(b, n, par):
                    act.wait_ge(y_mm, b + 1)
                    act.wait_ge(gc_ok, b + 1)
                    act.wait_ge(y_out[par], 16 * n)
                    act.activation(yo[:, par, 0:512], pY[:, 0, :], ACT.Copy, scale=gcol[:, par:par + 1]).then_inc(y_a, 1)
                    act.wait_ge(y_a, b + 1)
                    act.wait_ge(y_d, b + 1)
                    act.dma_start(S.yb_d[ds(b * P, P), :], yo[:, par, :]).then_inc(y_out[par], 16)

                def step(b, j, t):
                    evac_x(b + 1, (t + 1) % 2)
                    silu(b)
                    out(b - 1, j, (t + 1) % 2)

                evac_x(0, 0)
                evac_x(1, 1)
                silu(0)
                n = blocks(act, step)
                act.wait_ge(y_out[0], 16 * ((n + 1) // 2))
                act.sem_inc(tail, 1)
                act.wait_ge(y_out[1], 16 * (n // 2))
                act.sem_inc(tail, 1)

            @block.vector
            def _(dve):
                def evac_x(b, par):
                    dve.wait_ge(x_mm, b + 1)
                    dve.tensor_copy(xT[:, par, 4:8, :], pX[:, 1, :].rearrange("p (k t) -> p k t", k=4)).then_inc(x_d, 1)

                def hidden(b):
                    dve.wait_ge(s_ok, b + 1)
                    dve.tensor_tensor(hid[:, :], act_v[:, :], pU[:, DE:2 * DE], ALU.mult).then_inc(h_ok, 1)

                def evac_hid(b):
                    dve.wait_ge(t_mm, b + 1)
                    dve.tensor_copy(hT[:, :, :], pT[:, 0:2 * P].rearrange("p (k t) -> p k t", k=2)).then_inc(t_ok, 1)

                def out(b, n, par):
                    dve.wait_ge(gc_ok, b + 1)
                    dve.wait_ge(y_mm, b + 1)
                    dve.wait_ge(y_out[par], 16 * n)
                    dve.tensor_scalar(yo[:, par, 512:D], pY[:, 1, :], gcol[:, par:par + 1], None, ALU.mult).then_inc(y_d, 1)

                def step(b, j, t):
                    prev = (t + 1) % 2
                    dve.tensor_copy(gcol[:, prev:prev + 1], S.slot_gate[:, ds(b - 1, 1)]).then_inc(gc_ok, 1)
                    evac_x(b + 1, prev)
                    hidden(b)
                    out(b - 1, j, prev)
                    evac_hid(b)

                evac_x(0, 0)
                evac_x(1, 1)
                hidden(0)
                evac_hid(0)
                blocks(dve, step)


def final(nc, S, a, o):
    with ExitStack() as st:
        sb, sem = S.sb, S.sem
        gate = sb(st, "gate2", [P, D])
        gf = sb(st, "gf", [P, D])
        yg = sb(st, "yg", [P, 2, 2, D])
        idx = sb(st, "idx2", [P, 2, 2], I32)
        junk = sb(st, "junk4", [P, D])
        out = sb(st, "out_rows", [P, 2, D])
        ssq = sb(st, "ssq3", [P, 2])
        rstd = sb(st, "rstd3", [P, 1])
        newton = sb(st, "newton3", [P, 2])
        x2 = S.x2
        mod_in, mod_s, idx_ok, sum_ok, mul_ok, x_ok, sq_ok, o_ok, ch = (sem(n) for n in (
            "mod3_loaded", "mod3_sample_loaded", "idx2_ready", "rows_summed", "rows_gated", "x3_ready", "ssq3_ready",
            "out_ready", "dve_chain5"))
        s1_ok, idx_seen = sem("rows_added"), sem("idx2_seen")
        y_in, o_out = [sem("rows_gathered0"), sem("rows_gathered1")], [sem("out_stored0"), sem("out_stored1")]

        def rows_of(i):
            return NS if isinstance(i, int) and i == TP else P

        def x2_of(i):
            return x2[0:rows_of(i), ds(i, 1), :].rearrange("p o n -> p (o n)")

        with nc.Block() as block:
            @block.sync
            def _(sp):
                sp.dma_start(gate[:, :], S.ada_d[0:1, 5 * D:6 * D].to_broadcast([P, D])).then_inc(mod_in, 16)
                sp.dma_start(gf[:, :], a.g_final.to_broadcast([P, D])).then_inc(mod_in, 16)

                def step(i, n, b):
                    sp.wait_ge(o_ok, i + 1)
                    if rows_of(i) == NS:
                        sp.dma_start(o.y_sample.rearrange("b t d -> (b t) d"), out[0:NS, b, :]).then_inc(o_out[b], 16)
                    else:
                        sp.dma_start(o.y_prompt[0, ds(i * P, P), :], out[:, b, :]).then_inc(o_out[b], 16)

                prompt_loop(sp, 0, step)
                step(14, 7, 0)
                sp.wait_ge(mul_ok, TP)
                for q in range(NSEQ):
                    sp.dma_start(gate[q * DSEQ:(q + 1) * DSEQ, :],
                                 S.ada_d[1 + q:2 + q, 5 * D:6 * D].to_broadcast([DSEQ, D])).then_inc(mod_s, 16)
                step(15, 7, 1)
                step(16, 8, 0)
                sp.wait_ge(o_out[0], 16 * 9)
                sp.wait_ge(o_out[1], 16 * 8)

            @block.gpsimd
            def _(pool):
                def gather(i, n, b):
                    r = rows_of(i)
                    pool.wait_ge(sum_ok, i + 1)
                    for k in range(2):
                        pool.tensor_copy(idx[0:r, b, k:k + 1], S.dest[0:r, ds(i + k * NT, 1)]).then_inc(idx_ok, 1)
                    pool.wait_ge(idx_ok, 2 * i + 2)
                    pool.sem_inc(idx_seen, 1)
                    for k in range(2):
                        pool.indirect_dma_start(out=yg[0:r, b, k, :], out_offset=None, in_=S.yb_d,
                                                in_offset=bass.IndirectOffsetOnAxis(ap=idx[0:r, b, k:k + 1], axis=0)).then_inc(y_in[b], 16)

                def step(i, n, b):
                    if not (isinstance(i, int) and i == TP):
                        gather(i + 1, n + b, 1 - b)
                    pool.wait_ge(mul_ok, i + 1)
                    pool.tensor_tensor(x2_of(i), x2_of(i), yg[0:rows_of(i), b, 0, :], ALU.add).then_inc(x_ok, 1)

                gather(0, 0, 0)
                prompt_loop(pool, 0, step)
                for i in (14, 15, 16):
                    step(i, i // 2, i % 2)

            @block.scalar
            def _(act):
                def step(i, n, b):
                    r = rows_of(i)
                    act.wait_ge(sq_ok, i)
                    act.wait_ge(x_ok, i + 1)
                    act.activation(junk[0:r, :], x2_of(i), ACT.Square, accum_out=ssq[0:r, b:b + 1]).then_inc(sq_ok, 1)

                prompt_loop(act, 0, step)
                for i in (14, 15, 16):
                    step(i, i // 2, i % 2)

            @block.vector
            def _(dve):
                c = Steps(dve, ch)

                def rows_in(i, n, b):
                    r = rows_of(i)
                    if isinstance(i, int) and i == TP:
                        dve.wait_ge(mod_s, 16 * NSEQ)
                    dve.wait_ge(y_in[b], 32 * n + 32)
                    y0, y1 = yg[0:r, b, 0, :], yg[0:r, b, 1, :]
                    dve.tensor_tensor(y1, y0, y1, ALU.add).then_inc(s1_ok, 1)
                    dve.wait_ge(s1_ok, i + 1)
                    dve.tensor_tensor(y0, y1, gate[0:r, :], ALU.mult).then_inc(mul_ok, 1)

                def norm(i, n, b):
                    r = rows_of(i)
                    dve.wait_ge(sq_ok, i + 1)
                    dve.sem_inc(sum_ok, 1)
                    inv_sqrt(dve, c, rstd[0:r, :], ssq[0:r, b:b + 1], 1.0 / D, newton[0:r, 0:1], newton[0:r, 1:2])
                    dve.wait_ge(o_out[b], 16 * n)
                    dve.scalar_tensor_tensor(out=out[0:r, b, :], in0=x2_of(i), scalar=rstd[0:r, :], in1=gf[0:r, :],
                                             op0=ALU.mult, op1=ALU.mult).then_inc(o_ok, 1)

                def step(i, n, b):
                    if not (isinstance(i, int) and i == TP):
                        rows_in(i + 1, n + b, 1 - b)
                    norm(i, n, b)

                dve.sem_inc(sum_ok, 2)
                dve.wait_ge(mod_in, 32)
                rows_in(0, 0, 0)
                with dve.Fori(0, 7) as j:
                    c.done = 2 * INV * j
                    step(2 * j, j, 0)
                    step(2 * j + 1, j, 1)
                c.done = 14 * INV
                for i in (14, 15, 16):
                    step(i, i // 2, i % 2)


_INS = ['x_prompt', 'x_sample', 'state_ssm_re', 'state_ssm_im', 'c_prompt', 'c_sample', 'w_ada', 'b_ada',
        'g_norm1', 'g_norm2', 'w_in', 'ln_g', 'ln_b', 'w_s', 'b_s', 'lam_re', 'lam_im', 'log_dt',
        'ssm_b_re', 'ssm_b_im', 'ssm_c_re', 'ssm_c_im', 'ssm_d', 'w_glu', 'b_glu', 'w_out',
        'w_group', 'b_group', 'w_expert', 'b_expert', 'w1', 'w3', 'w2', 'g_final']
_OUTS = [('y_prompt', (1, SEQ, D)), ('y_sample', (NSEQ, DSEQ, D)),
         ('ssm_re_prompt', (1, 1, G, ST)), ('ssm_im_prompt', (1, 1, G, ST)),
         ('ssm_re_sample', (1, NSEQ, G, ST)), ('ssm_im_sample', (1, NSEQ, G, ST)),
         ('v_sample', (1, NSEQ, DSEQ, DA))]


def kernel(**inputs):
    import concourse.bacc as _bacc
    from concourse.bass_utils import run_bass_kernel_spmd as _run

    nc = _bacc.Bacc("TRN2", target_bir_lowering=False, num_devices=1)
    arrays, ins, outs = {}, {}, {}
    for name in _INS:
        x = np.ascontiguousarray(inputs[name])
        if x.ndim == 1:
            x = x.reshape(1, -1)
        arrays[f"in_{name}"] = x
        ins[name] = nc.dram_tensor(f"in_{name}", x.shape, mybir.dt.from_np(x.dtype), kind="ExternalInput").ap()
    for name, shape in _OUTS:
        outs[name] = nc.dram_tensor(f"out_{name}", shape, F32, kind="ExternalOutput").ap()
    build(nc, Inputs(ins), Outputs(outs))
    r = _run(nc, [arrays], core_ids=[0])
    return tuple(r.results[0][f"out_{name}"] for name, _ in _OUTS)
```

```python
from contextlib import ExitStack

import numpy as np
import concourse.bass as bass
from concourse import mybir

F32 = mybir.dt.float32
F32R = mybir.dt.float32r
I32 = mybir.dt.int32
U32 = mybir.dt.uint32
ACT = mybir.ActivationFunctionType
ALU = mybir.AluOpType
AX = mybir.AxisListType
ds = bass.ds

P = 128
D = 1024
KD = D // P
SEQ = 2048
NSEQ = 8
DSEQ = 8
TP = SEQ // P
NS = NSEQ * DSEQ
NT = TP + 1
TOK = SEQ + NS
DA = 512
HEADS = 4
HD = 128
G = 32
GC = 16
ST = 64
PAIRS = G // 2
Q = 8
NCH = SEQ // Q
CH = NCH + NSEQ
EG = 4
EPG = 8
NE = EG * EPG
DE = 256
NR = EG + NE
NBLK = TOK * 2 // P + NE - 1
FULL = TOK * 2 // P
EPS = 1e-6
BIG = 1e30
RING = 4
TWO_PI = 2 * np.pi
MAGIC = 1.5 * 2 ** 23
PI_HI = float(np.float32(6.28125))
PI_MID = float(np.float32(np.float64(TWO_PI) - 6.28125))
PI_LO = float(TWO_PI - 6.28125 - PI_MID)


class Inputs:

    def __init__(self, t):
        self.x_prompt = t["x_prompt"]
        self.x_sample = t["x_sample"]
        self.state_ssm_re = t["state_ssm_re"]
        self.state_ssm_im = t["state_ssm_im"]
        self.c_prompt = t["c_prompt"]
        self.c_sample = t["c_sample"]
        self.w_ada = t["w_ada"]
        self.b_ada = t["b_ada"]
        self.g_norm1 = t["g_norm1"]
        self.g_norm2 = t["g_norm2"]
        self.w_in = t["w_in"]
        self.ln_g = t["ln_g"]
        self.ln_b = t["ln_b"]
        self.w_s = t["w_s"]
        self.b_s = t["b_s"]
        self.lam_re = t["lam_re"]
        self.lam_im = t["lam_im"]
        self.log_dt = t["log_dt"]
        self.ssm_b_re = t["ssm_b_re"]
        self.ssm_b_im = t["ssm_b_im"]
        self.ssm_c_re = t["ssm_c_re"]
        self.ssm_c_im = t["ssm_c_im"]
        self.ssm_d = t["ssm_d"]
        self.w_glu = t["w_glu"]
        self.b_glu = t["b_glu"]
        self.w_out = t["w_out"]
        self.w_group = t["w_group"]
        self.b_group = t["b_group"]
        self.w_expert = t["w_expert"]
        self.b_expert = t["b_expert"]
        self.w1 = t["w1"]
        self.w3 = t["w3"]
        self.w2 = t["w2"]
        self.g_final = t["g_final"]


class Outputs:

    def __init__(self, t):
        self.y_prompt = t["y_prompt"]
        self.y_sample = t["y_sample"]
        self.ssm_re_prompt = t["ssm_re_prompt"]
        self.ssm_im_prompt = t["ssm_im_prompt"]
        self.ssm_re_sample = t["ssm_re_sample"]
        self.ssm_im_sample = t["ssm_im_sample"]
        self.v_sample = t["v_sample"]


class Shared:

    def __init__(self, sb, psum, sem):
        self.sb, self.psum, self.sem = sb, psum, sem


class Steps:

    def __init__(self, eng, sem, done=0):
        self.eng, self.sem, self.done, self.count = eng, sem, done, 0

    def did(self, ins):
        ins.then_inc(self.sem, 1)
        self.done = self.done + 1
        self.count += 1

    def link(self, ins):
        self.did(ins)
        self.eng.wait_ge(self.sem, self.done)

    def at(self, done):
        self.done = done

    def sync(self):
        self.eng.wait_ge(self.sem, self.done)


def fan(ap, shape):
    return ap.unsqueeze(len(shape) - 1).to_broadcast(shape)


def build(nc, a, o):
    ctx = ExitStack()
    with ctx:
        ctx.enter_context(nc.allow_non_contiguous_dma(reason="small parameter loads"))

        def sb(stack, name, shape, dt=F32):
            return stack.enter_context(nc.sbuf_tensor(name, shape, dt))

        def psum(stack, name, shape):
            return stack.enter_context(nc.psum_tensor(name, shape, F32))

        def sem(name):
            t = names.enter_context(nc.semaphore(name))
            used.append(t)
            return t

        def dram(name, shape):
            return nc.dram_tensor(name, shape, F32, kind="Internal").ap()

        S = Shared(sb, psum, sem)
        S.ada_d = dram("ada_rows", (9, 6 * D))
        S.kpad_d = dram("toeplitz_rows", (GC, G, 2 * P))
        S.a_d = dram("gmlp_rows", (TOK, DA))
        S.s_d = dram("s5_in_rows", (TOK, DA))
        S.y_d = dram("s5_out_rows", (TOK, DA))
        S.h2_d = dram("moe_in_rows", (TOK, D))
        S.x2_d = dram("x2_rows", (TOK, D))
        S.rot_d = dram("rotations", (P, PAIRS, 2, NCH))
        S.yb_d = dram("expert_rows", (NBLK * P, D))
        S.ident = sb(ctx, "ident", [P, P])
        names, used = ExitStack(), []
        with ExitStack() as early:
            tables(S, early)
            setup(nc, S, a)
            mixin(nc, S, a, o)
            s5(nc, S, a, o)
        with nc.Block() as block:
            @block.gpsimd
            def _(pool):
                for t in used:
                    pool.sem_clear(t)
        names.close()
        S.logits = sb(ctx, "logits", [P, NT, NR])
        mixout(nc, S, a)
        S.dest = sb(ctx, "dest", [P, NT * 2], I32)
        S.slot_tok = sb(ctx, "slot_tok", [P, NBLK + 3], I32)
        S.slot_gate = sb(ctx, "slot_gate", [P, NBLK + 3])
        S.n_blocks = sb(ctx, "n_blocks", [1, 2], I32)
        S.block_run = sb(ctx, "block_run", [1, NBLK + 3], I32)
        S.run_expert = sb(ctx, "run_expert", [1, NE], I32)
        S.run_free = sb(ctx, "run_free", [1, NE], I32)
        route(nc, S)
        experts(nc, S, a)
        final(nc, S, a, o)
        names.close()


def tables(S, stack):
    sb = S.sb
    S.m_re = sb(stack, "m_re", [P, PAIRS, 9, GC])
    S.m_im = sb(stack, "m_im", [P, PAIRS, 9, GC])
    S.wx = sb(stack, "wx", [P, PAIRS, 2, P])
    S.decay = sb(stack, "decay", [P, PAIRS])
    S.a8_re = sb(stack, "a8_re", [P, PAIRS])
    S.a8_im = sb(stack, "a8_im", [P, PAIRS])
    S.na8_im = sb(stack, "na8_im", [P, PAIRS])
    S.ws = sb(stack, "ws", [P, HEADS, P])
    S.ws_samp = sb(stack, "ws_samp", [NS, HEADS, NS])
    S.bs = sb(stack, "bs", [P, HEADS])
    S.bs_samp = sb(stack, "bs_samp", [NS, HEADS])


def setup(nc, S, a):
    with ExitStack() as st:
        sb, sem = S.sb, S.sem
        NW = 12
        WB = 2
        c9 = sb(st, "c9", [9, D])
        sc9 = c9
        rows = sb(st, "rows", [9, 6 * D])
        cT = sb(st, "cT", [P, KD, 9])
        wada = sb(st, "wada", [P, WB, KD, 512])
        bada = sb(st, "bada", [9, 6 * D])
        g12 = sb(st, "g12", [9, 2, D])
        lam = sb(st, "lam", [PAIRS, 2, P])
        lr = sb(st, "lr", [P, PAIRS])
        li = sb(st, "li", [P, PAIRS])
        dt = sb(st, "dt", [P, PAIRS])
        tmp = [sb(st, f"tmp{i}", [P, PAIRS]) for i in range(8)]
        pw_re = sb(st, "pw_re", [P, PAIRS, 9])
        pw_im = sb(st, "pw_im", [P, PAIRS, 9])
        pr_re = sb(st, "pr_re", [P, PAIRS, Q])
        pr_im = sb(st, "pr_im", [P, PAIRS, Q])
        b_in = sb(st, "b_in", [P, 2, PAIRS, GC])
        bb = sb(st, "bb", [P, 2, PAIRS, GC])
        c_in = sb(st, "c_in", [P, 2, 2, P])
        cc = sb(st, "cc", [P, 2, PAIRS, GC])
        big1 = sb(st, "big1", [P, PAIRS, 9, GC])
        zero = sb(st, "zero", [GC, P])
        dd = sb(st, "dd", [GC, G])
        dtmp = sb(st, "dtmp", [GC, G, GC])
        rot_ok, rot_out = sem("rot_ready"), sem("rot_stored")
        ws_in = sb(st, "ws_in", [P, HEADS, P])
        vk = sb(st, "vk", [P, G, P])
        v = [vk[:, 0:PAIRS, :].rearrange("p a (s h) -> p a s h", s=Q),
             vk[:, PAIRS:G, :].rearrange("p a (s h) -> p a s h", s=Q)]
        rot = sb(st, "rot_all", [P, PAIRS, 2, NCH])
        k0 = vk[0:GC, :, :]
        pm = S.psum(st, "ps_misc", [P, 4, 512])
        pa = S.psum(st, "ps_ada", [P, WB, 512])
        ident = S.ident

        id_steps, z_k0, z_ws = sem("id_steps"), sem("z_k0"), sem("z_ws")
        c_in_s, small, w_s, bada_s = sem("c_loaded"), sem("small_loaded"), [sem(f"wada_loaded{i}") for i in range(WB)], sem("bada_loaded")
        ws_cp, ws_mask, ws_blk = sem("ws_copied"), sem("ws_masked"), sem("ws_blocks")
        ada_free = sem("ada_bank_free")
        act_s, pe_s, dve_s, ada_mm, ada_ev, rows_ok, rows_out = (sem("setup_act"), sem("setup_pe"), sem("setup_dve"), sem("ada_mm"), sem("ada_evac"), sem("ada_rows_ready"), sem("ada_rows_stored"))
        k_ok, k_out, chan = sem("k0_ready"), sem("k0_stored"), sem("dve_chain")
        w_view = a.w_ada[0].rearrange("(k p) n -> p k n", p=P)

        with nc.Block() as block:
            @block.sync
            def _(sp):
                sp.dma_start(c9[0:1, :], a.c_prompt).then_inc(c_in_s, 16)
                sp.dma_start(c9[1:9, :], a.c_sample).then_inc(c_in_s, 16)
                sp.dma_start(lam[:, 0, :], a.lam_re[0].rearrange("(a g) p -> a (g p)", g=2)).then_inc(small, 16)
                sp.dma_start(lam[:, 1, :], a.lam_im[0].rearrange("(a g) p -> a (g p)", g=2)).then_inc(small, 16)
                ldt = a.log_dt[0:1, :].rearrange("o (a g) -> o g a", g=2)
                for g in range(2):
                    sp.dma_start(dt[g * ST:(g + 1) * ST, :], ldt[:, g, :].to_broadcast([ST, PAIRS])).then_inc(small, 16)
                for i, t in enumerate((a.ssm_b_re, a.ssm_b_im)):
                    sp.dma_start(b_in[:, i, :, :], t[0].rearrange("(a g) p h -> (g p) a h", g=2)).then_inc(small, 16)
                for i, t in enumerate((a.ssm_c_re, a.ssm_c_im)):
                    cv = t[0].rearrange("(b a g) o p -> b a o g p", b=2, g=2)
                    for h in range(2):
                        for q in range(8):
                            sp.dma_start(c_in[q * GC:(q + 1) * GC, i, h, :].rearrange("o (g p) -> o g p", g=2),
                                         cv[h, q, :, :, :]).then_inc(small, 16)
                sp.dma_start(dd[:, :], a.ssm_d[0].rearrange("g h -> h g")).then_inc(small, 16)
                sp.dma_start(ws_in[:, :, :], a.w_s[0].rearrange("h t s -> t h s")).then_inc(small, 16)
                sp.dma_start(S.bs[:, :], a.b_s[0].rearrange("h t -> t h")).then_inc(small, 16)
                for q in range(NSEQ):
                    sp.dma_start(S.bs_samp[q * DSEQ:(q + 1) * DSEQ, :],
                                 a.b_s[0].rearrange("h t -> t h")[0:DSEQ, :]).then_inc(small, 16)
                sp.dma_start(bada[:, :], a.b_ada.to_broadcast([9, 6 * D])).then_inc(bada_s, 16)
                sp.dma_start(g12[:, 0, :], a.g_norm1.to_broadcast([9, D])).then_inc(bada_s, 16)
                sp.dma_start(g12[:, 1, :], a.g_norm2.to_broadcast([9, D])).then_inc(bada_s, 16)
                for n in range(NW):
                    if n >= WB:
                        sp.wait_ge(ada_mm, n - WB + 1)
                    sp.dma_start(wada[:, n % WB, :, :], w_view[:, :, n * 512:(n + 1) * 512]).then_inc(w_s[n % WB], 16)
                sp.wait_ge(ws_mask, 1)
                sp.wait_ge(z_ws, 1)
                for q in range(NSEQ):
                    r = slice(q * DSEQ, (q + 1) * DSEQ)
                    sp.dma_start(S.ws_samp[r, :, r], S.ws[0:DSEQ, :, 0:DSEQ]).then_inc(ws_blk, 16)
                sp.wait_ge(rot_ok, 1)
                sp.dma_start(S.rot_d, rot[:, :, :, :]).then_inc(rot_out, 16)
                sp.wait_ge(k_ok, 1)
                sp.wait_ge(z_k0, 1)
                sp.dma_start(S.kpad_d[:, :, 0:P], zero[:, :].unsqueeze(1).to_broadcast([GC, G, P])).then_inc(k_out, 16)
                sp.dma_start(S.kpad_d[:, :, P:2 * P], k0).then_inc(k_out, 16)
                sp.wait_ge(rows_ok, 5)
                sp.dma_start(S.ada_d, rows[:, :]).then_inc(rows_out, 16)
                sp.wait_ge(ws_blk, 16 * NSEQ)
                sp.wait_ge(k_out, 32)
                sp.wait_ge(rot_out, 16)
                sp.wait_ge(rows_out, 16)

            @block.gpsimd
            def _(pool):
                ids = Steps(pool, id_steps)
                ids.link(pool.memset(ident[:, :], 0.0))
                ids.did(pool.affine_select(out=ident[:, :], in_=ident[:, :], compare_op=ALU.not_equal, fill=1.0,
                                           base=0, pattern=[[-1, P]], channel_multiplier=1))
                pool.memset(zero[:, :], 0.0).then_inc(z_k0, 1)
                pool.memset(S.ws_samp[:, :, :], 0.0).then_inc(z_ws, 1)
                pool.wait_ge(ws_cp, 1)
                pool.affine_select(out=S.ws[:, :, :], in_=S.ws[:, :, :], compare_op=ALU.is_ge, fill=0.0, base=0,
                                   pattern=[[0, HEADS], [1, P]], channel_multiplier=-1).then_inc(ws_mask, 1)
                pool.wait_ge(bada_s, 48)
                pool.wait_ge(ada_ev, NW)
                rk = Steps(pool, rows_ok)
                rk.link(pool.tensor_tensor(rows[:, :], rows[:, :], bada[:, :], ALU.add))
                for at in (1, 4):
                    rk.did(pool.tensor_scalar(rows[:, at * D:(at + 1) * D], rows[:, at * D:(at + 1) * D], 1.0, None, ALU.add))
                rk.sync()
                for i, at in enumerate((1, 4)):
                    rk.did(pool.tensor_tensor(rows[:, at * D:(at + 1) * D], rows[:, at * D:(at + 1) * D], g12[:, i, :], ALU.mult))

            @block.scalar
            def _(act):
                act.wait_ge(c_in_s, 32)
                st_ = Steps(act, act_s)
                st_.did(act.activation(sc9[:, :], c9[:, :], ACT.Silu))
                act.wait_ge(small, 16 * N_SMALL)
                st_.link(act.activation(tmp[7][:, :], dt[:, :], ACT.Exp))
                act.wait_ge(dve_s, 2)
                st_.did(act.activation(tmp[2][:, :], tmp[0][:, :], ACT.Exp))
                st_.did(act.activation(S.decay[:, :], tmp[0][:, :], ACT.Exp, scale=float(Q)))
                st_.did(act.activation(tmp[3][:, :], tmp[1][:, :], ACT.Sin))
                st_.did(act.activation(tmp[4][:, :], tmp[1][:, :], ACT.Sin, scale=0.5))
                for i in range(2):
                    act.wait_ge(pe_s, 3 + i)
                    st_.did(act.activation(cc[:, i, :, :].rearrange("p a o -> p (a o)"), pm[:, i, 256:512], ACT.Copy))
                act.wait_ge(pe_s, 5)
                act.activation(S.ws[:, :, :].rearrange("p h t -> p (h t)"), pm[:, 2, :], ACT.Copy).then_inc(ws_cp, 1)
                act.sem_inc(ada_free, WB)
                with act.Fori(0, NW // WB) as j:
                    for b in range(WB):
                        act.wait_ge(ada_mm, WB * j + b + 1)
                        act.activation(rows[:, ds((WB * j + b) * 512, 512)], pa[0:9, b, :], ACT.Copy).then_inc(ada_free, 1)
                act.wait_ge(ada_free, WB + NW)
                act.sem_inc(ada_ev, NW)
                for n in range(8):
                    act.wait_ge(pe_s, 6 + n)
                    st_.did(act.activation(
                        S.wx[:, 2 * n:2 * n + 2, :, :].rearrange("p a r s -> p (a r s)"), pm[:, n % 2, :], ACT.Copy))

            @block.tensor
            def _(pe):
                ps = Steps(pe, pe_s)
                pe.wait_ge(id_steps, 2)
                pe.wait_ge(act_s, 1)
                for k in range(KD):
                    last = pe.transpose(pm[:, 0, k * 9:(k + 1) * 9], sc9[:, k * P:(k + 1) * P], ident[0:9, 0:9])
                ps.did(last)
                pe.wait_ge(small, 16 * N_SMALL)
                pe.transpose(pm[:, 1, 0:PAIRS], lam[:, 0, :], ident[0:PAIRS, 0:PAIRS])
                ps.did(pe.transpose(pm[:, 1, PAIRS:2 * PAIRS], lam[:, 1, :], ident[0:PAIRS, 0:PAIRS]))
                pe.wait_ge(chan, 3)
                for i in range(2):
                    for h in range(2):
                        last = pe.transpose(pm[:, i, 256 + h * P:256 + (h + 1) * P], c_in[:, i, h, :], ident[:, :])
                    ps.did(last)
                for h in range(HEADS):
                    last = pe.transpose(pm[:, 2, h * P:(h + 1) * P], ws_in[:, h, :], ident[:, :])
                ps.did(last)
                with pe.Fori(0, NW // WB) as j:
                    for b in range(WB):
                        pe.wait_ge(w_s[b], 16 * j + 16)
                        pe.wait_ge(ada_free, WB * j + b + 1)
                        for k in range(KD):
                            last = pe.matmul(pa[0:9, b, :], cT[:, k, :], wada[:, b, k, :], start=k == 0, stop=k == KD - 1)
                        last.then_inc(ada_mm, 1)
                for n in range(8):
                    if n == 0:
                        pe.wait_ge(dve_s, 4)
                        pe.wait_ge(act_s, 8)
                    if n >= 2:
                        pe.wait_ge(act_s, 9 + n - 2)
                    for q in range(4):
                        last = pe.transpose(pm[:, n % 2, q * P:(q + 1) * P],
                                            v[q % 2][:, 2 * n + q // 2, :, :].rearrange("p s h -> p (s h)"), ident[:, :])
                    ps.did(last)
                pe.wait_ge(dve_s, 5)
                for n in range(8):
                    if n >= 2:
                        pe.wait_ge(dve_s, 5 + n - 1)
                    for q in range(4):
                        g = 8 * (n // 2) + 2 * q + n % 2
                        r = slice((g % 2) * ST, (g % 2) * ST + ST)
                        for i, m in enumerate((S.m_re, S.m_im)):
                            last = pe.matmul(pm[0:GC, 2 + n % 2, q * P:(q + 1) * P], bb[r, i, g // 2, :],
                                             m[r, g // 2, 0:Q, :].rearrange("p k o -> p (k o)"),
                                             start=i == 0, stop=i == 1)
                    ps.did(last)

            @block.vector
            def _(dve):
                ch = Steps(dve, chan)
                dv = Steps(dve, dve_s)

                def tt(out, x, y, op):
                    ch.link(dve.tensor_tensor(out, x, y, op))

                def cmul(o_re, o_im, x_re, x_im, y_re, y_im, t, shape=None):
                    ch.did(dve.tensor_tensor(o_re, x_re, y_re, ALU.mult))
                    ch.did(dve.tensor_tensor(o_im, x_re, y_im, ALU.mult))
                    tt(t, x_im, y_im, ALU.mult)
                    tt(o_re, o_re, t, ALU.subtract)
                    tt(t, x_im, y_re, ALU.mult)
                    tt(o_im, o_im, t, ALU.add)

                dve.wait_ge(pe_s, 1)
                ch.link(dve.tensor_copy(cT[:, :, :].rearrange("p k n -> p (k n)"), pm[:, 0, 0:9 * KD]))
                dve.wait_ge(pe_s, 2)
                ch.did(dve.tensor_copy(lr[:, :], pm[:, 1, 0:PAIRS]))
                ch.link(dve.tensor_copy(li[:, :], pm[:, 1, PAIRS:2 * PAIRS]))
                dve.wait_ge(act_s, 2)
                T = [t[:, :] for t in tmp]
                dv.did(dve.tensor_tensor(T[0], lr[:, :], T[7], ALU.mult))
                tt(T[1], li[:, :], T[7], ALU.mult)
                ch.link(dve.tensor_scalar(T[5], T[1], 1.0 / TWO_PI, MAGIC, ALU.mult, ALU.add))
                ch.link(dve.tensor_scalar(T[5], T[5], MAGIC, None, ALU.subtract))
                for part in (PI_HI, PI_MID):
                    ch.link(dve.scalar_tensor_tensor(out=T[1], in0=T[5], scalar=-part, in1=T[1], op0=ALU.mult, op1=ALU.add))
                dv.did(dve.scalar_tensor_tensor(out=T[1], in0=T[5], scalar=-PI_LO, in1=T[1], op0=ALU.mult, op1=ALU.add))
                dve.wait_ge(act_s, 6)
                tt(T[5], T[4], T[4], ALU.mult)
                ch.link(dve.tensor_scalar(T[5], T[5], -2.0, 1.0, ALU.mult, ALU.add))
                ch.did(dve.memset(pw_re[:, :, 0], 1.0))
                ch.did(dve.memset(pw_im[:, :, 0], 0.0))
                tt(pw_re[:, :, 1], T[2], T[5], ALU.mult)
                tt(pw_im[:, :, 1], T[2], T[3], ALU.mult)
                for k in range(2, 9):
                    cmul(pw_re[:, :, k], pw_im[:, :, k], pw_re[:, :, k - 1], pw_im[:, :, k - 1],
                         pw_re[:, :, 1], pw_im[:, :, 1], T[6])
                for s in range(Q):
                    ch.did(dve.tensor_copy(pr_re[:, :, s], pw_re[:, :, Q - 1 - s]))
                    ch.did(dve.tensor_copy(pr_im[:, :, s], pw_im[:, :, Q - 1 - s]))
                ch.did(dve.tensor_copy(S.a8_re[:, :], pw_re[:, :, 8]))
                ch.did(dve.tensor_copy(S.a8_im[:, :], pw_im[:, :, 8]))
                ch.link(dve.tensor_scalar(S.na8_im[:, :], pw_im[:, :, 8], -1.0, None, ALU.mult))
                ch.link(dve.tensor_scalar(T[0], pw_re[:, :, 1], -1.0, None, ALU.add))
                ch.did(dve.tensor_tensor(T[1], lr[:, :], lr[:, :], ALU.mult))
                tt(T[2], li[:, :], li[:, :], ALU.mult)
                tt(T[1], T[1], T[2], ALU.add)
                ch.link(dve.reciprocal(T[1], T[1]))
                ch.did(dve.tensor_tensor(T[2], T[0], lr[:, :], ALU.mult))
                tt(T[4], pw_im[:, :, 1], li[:, :], ALU.mult)
                tt(T[2], T[2], T[4], ALU.add)
                tt(T[2], T[2], T[1], ALU.mult)
                ch.did(dve.tensor_tensor(T[6], pw_im[:, :, 1], lr[:, :], ALU.mult))
                tt(T[4], T[0], li[:, :], ALU.mult)
                tt(T[6], T[6], T[4], ALU.subtract)
                tt(T[6], T[6], T[1], ALU.mult)
                s3 = [P, PAIRS, GC]
                t256 = big1[:, :, 0, :]
                cmul(bb[:, 0, :, :], bb[:, 1, :, :], fan(T[2], s3), fan(T[6], s3), b_in[:, 0, :, :], b_in[:, 1, :, :], t256)
                s4 = [P, PAIRS, Q, GC]
                pr, pi = fan(pr_re[:, :, :], s4), fan(pr_im[:, :, :], s4)
                b_re = bb[:, 0, :, :].unsqueeze(2).to_broadcast(s4)
                b_im = bb[:, 1, :, :].unsqueeze(2).to_broadcast(s4)
                t4 = big1[:, :, 0:Q, :]
                ch.did(dve.tensor_tensor(v[0], pr, b_re, ALU.mult))
                ch.did(dve.tensor_tensor(v[1], pr, b_im, ALU.mult))
                tt(t4, pi, b_im, ALU.mult)
                dv.did(dve.tensor_tensor(v[0], v[0], t4, ALU.subtract))
                dv.sync()
                tt(t4, pi, b_re, ALU.mult)
                dv.did(dve.tensor_tensor(v[1], v[1], t4, ALU.add))
                dv.sync()
                dve.wait_ge(act_s, 8)
                s9 = [P, PAIRS, 9, GC]
                q_re, q_im = fan(pw_re[:, :, :], s9), fan(pw_im[:, :, :], s9)
                c_re = cc[:, 0, :, :].unsqueeze(2).to_broadcast(s9)
                c_im = cc[:, 1, :, :].unsqueeze(2).to_broadcast(s9)
                m_re, m_im, t9 = S.m_re[:, :, :, :], S.m_im[:, :, :, :], big1[:, :, :, :]
                ch.did(dve.tensor_tensor(m_re, q_re, c_re, ALU.mult))
                ch.did(dve.tensor_tensor(m_im, q_im, c_re, ALU.mult))
                tt(t9, q_im, c_im, ALU.mult)
                tt(m_re, m_re, t9, ALU.subtract)
                tt(t9, q_re, c_im, ALU.mult)
                tt(m_im, m_im, t9, ALU.add)
                dv.did(dve.tensor_scalar(m_im, m_im, -1.0, None, ALU.mult))
                ch.link(dve.tensor_tensor(dtmp[:, :, :], ident[0:GC, 0:GC].unsqueeze(1).to_broadcast([GC, G, GC]),
                                          fan(dd[:, :], [GC, G, GC]), ALU.mult))
                rc, rs = rot[:, :, 0, :], rot[:, :, 1, :]
                sq = [(T[5], T[3]), (T[0], T[1])]
                for i in range(3):
                    (x, y), (u, w) = sq[i % 2], sq[(i + 1) % 2]
                    cmul(u, w, x, y, x, y, T[2])
                ch.did(dve.memset(rc[:, :, 0:1], 1.0))
                ch.link(dve.memset(rs[:, :, 0:1], 0.0))
                n, i = 1, 1
                while n < NCH:
                    (x, y), (u, w) = sq[i % 2], sq[(i + 1) % 2]
                    sh = [P, PAIRS, n]
                    half = big1[:, :, :, :].rearrange("p a k o -> p a (k o)")[:, :, 0:n]
                    cmul(rc[:, :, n:2 * n], rs[:, :, n:2 * n], rc[:, :, 0:n], rs[:, :, 0:n], fan(x, sh), fan(y, sh), half)
                    cmul(u, w, x, y, x, y, T[2])
                    n, i = 2 * n, i + 1
                dve.sem_inc(rot_ok, 1)
                for n in range(8):
                    dve.wait_ge(pe_s, 14 + n)
                    dv.did(dve.tensor_copy(k0[:, 8 * (n // 2) + n % 2:8 * (n // 2) + 8:2, :],
                                           pm[0:GC, 2 + n % 2, :].rearrange("h (g k) -> h g k", g=4)))
                dv.sync()
                dve.tensor_tensor(k0[:, :, 0:GC], k0[:, :, 0:GC], dtmp[:, :, :], ALU.add).then_inc(k_ok, 1)



N_SMALL = 2 + 2 + 2 + 32 + 1 + 1 + 1 + NSEQ


def split_matmul(pe, out, left, right, n):
    for k in range(n):
        pe.matmul(out, left(0, k), right(0, k), start=k == 0, stop=False)
        pe.matmul(out, left(0, k), right(1, k), start=False, stop=False)
        last = pe.matmul(out, left(1, k), right(0, k), start=False, stop=k == n - 1)
    return last


def prompt_loop(eng, first, body, after=None):
    for b in range(2):
        body(first + b, (first + b) // 2, (first + b) % 2)
    with eng.Fori(1, 7) as j:
        if after is not None:
            after(j)
        for b in range(2):
            t = first + b
            body(2 * j + t, j + t // 2, t % 2)


def inv_sqrt(eng, c, y, total, share, x, t):
    c.link(eng.tensor_scalar(x, total, share, EPS, ALU.mult, ALU.add))
    c.link(eng.tensor_scalar(y.bitcast(I32), x.bitcast(I32), -0.5, float(0x5F3759DF), ALU.mult, ALU.add))
    for _ in range(3):
        c.link(eng.tensor_tensor(t, y, y, ALU.mult))
        c.link(eng.tensor_tensor(t, t, x, ALU.mult))
        c.link(eng.tensor_scalar(t, t, -0.5, 1.5, ALU.mult, ALU.add))
        c.link(eng.tensor_tensor(y, y, t, ALU.mult))


INV = 2 + 3 * 4


def mixin(nc, S, a, o):
    with ExitStack() as st:
        sb, sem = S.sb, S.sem
        win_hi = sb(st, "win_hi", [P, KD, 3 * DA], F32R)
        win_lo = sb(st, "win_lo", [P, KD, 3 * DA], F32R)
        raw = sb(st, "win_raw", [P, 2, KD // 2, DA])
        x = sb(st, "x", [P, 2, D])
        hT_hi = sb(st, "hT_hi", [P, 2, KD, P], F32R)
        hT_lo = sb(st, "hT_lo", [P, 2, KD, P], F32R)
        gain = sb(st, "gain1", [P, D])
        shift = sb(st, "shift1", [P, D])
        lng = sb(st, "lng", [P, DA])
        lnb = sb(st, "lnb", [P, DA])
        junk2 = sb(st, "junk2", [P, DA])
        ssq = sb(st, "ssq1", [P, 2])
        rstd = sb(st, "rstd1", [P, 2])
        v = sb(st, "v", [P, DA])
        u = sb(st, "u", [P, DA])
        a_row = sb(st, "a_row", [P, DA])
        s_row = sb(st, "s_row", [P, DA])
        mean = sb(st, "mean", [P, HEADS])
        var = sb(st, "var", [P, HEADS])
        newton = sb(st, "newton1", [P, 2, HEADS])
        pT = S.psum(st, "ps_hT", [P, 2, 512])
        pV = S.psum(st, "ps_v", [P, 512])
        pU = S.psum(st, "ps_u", [P, 512])
        pS = S.psum(st, "ps_s", [P, 512])
        pM = S.psum(st, "ps_mix", [P, 512])
        junk = S.psum(st, "ps_squares", [P, 2 * 512])
        ident = S.ident

        mod_in, mod_samp, win_in = sem("mod1_loaded"), sem("mod1_sample_loaded"), [sem(f"win_loaded{i}") for i in range(2)]
        win_h, win_l = sem("win_hi_ready"), sem("win_lo_ready")
        x_in = [sem("x_loaded0"), sem("x_loaded1")]
        ssq_ok, ch, h_ok, hT_mm, hT_a, hT_d = sem("ssq1_ready"), sem("dve_chain1"), sem("h_ready"), sem("hT_transposed"), sem("hT_evac_act"), sem("hT_evac_dve")
        v_mm, v_ok, cen_ok, var_ok, vhat_ok, vn_ok = sem("v_mm"), sem("v_gelu"), sem("v_centred"), sem("v_var"), sem("v_scaled"), sem("v_normed")
        u_mm, u_ok, s_mm, s_ok, m_mm, a_ok = sem("u_mm"), sem("u_gelu"), sem("s_mm"), sem("s_copied"), sem("mix_mm"), sem("a_ready")
        xn_ok, s_out, a_out, v_out = sem("x_scaled"), sem("s_stored"), sem("a_stored"), sem("v_stored")
        w_view = a.w_in[0].rearrange("(k p) n -> p k n", p=P)
        x_rows = a.x_prompt[0]
        samp_rows = a.x_sample.rearrange("b t d -> (b t) d")

        def half_k(n):
            return slice(n % 2 * KD // 2, (n % 2 + 1) * KD // 2)

        def cols(n):
            c = (1, 0, 2)[n // 2]
            return slice(c * DA, (c + 1) * DA)

        def rows_of(i):
            return NS if isinstance(i, int) and i == TP else P

        def dr(t, i):
            return t[TP * P:TOK, :] if isinstance(i, int) and i == TP else t[ds(i * P, P), :]

        with nc.Block() as block:
            @block.sync
            def _(sp):
                sp.dma_start(x[:, 0, :], x_rows[0:P, :]).then_inc(x_in[0], 16)
                sp.dma_start(gain[:, :], S.ada_d[0:1, D:2 * D].to_broadcast([P, D])).then_inc(mod_in, 16)
                sp.dma_start(shift[:, :], S.ada_d[0:1, 0:D].to_broadcast([P, D])).then_inc(mod_in, 16)
                sp.dma_start(lng[:, :], a.ln_g.rearrange("o h d -> o (h d)").to_broadcast([P, DA])).then_inc(mod_in, 16)
                sp.dma_start(lnb[:, :], a.ln_b.rearrange("o h d -> o (h d)").to_broadcast([P, DA])).then_inc(mod_in, 16)
                sp.dma_start(x[:, 1, :], x_rows[P:2 * P, :]).then_inc(x_in[1], 16)
                for n in range(6):
                    if n >= 2:
                        sp.wait_ge(win_l, n - 1)
                    sp.dma_start(raw[:, n % 2, :, :], w_view[:, half_k(n), cols(n)]).then_inc(win_in[n % 2], 16)

                def stores(i, n, b):
                    r = rows_of(i)
                    sp.wait_ge(s_ok, i + 1)
                    sp.dma_start(dr(S.s_d, i), s_row[0:r, :]).then_inc(s_out, 16)
                    sp.wait_ge(a_ok, i + 1)
                    sp.dma_start(dr(S.a_d, i), a_row[0:r, :]).then_inc(a_out, 16)

                def step(i, n, b):
                    sp.wait_ge(hT_mm, i + 1)
                    sp.dma_start(x[:, b, :], x_rows[ds((i + 2) * P, P), :]).then_inc(x_in[b], 16)
                    stores(i, n, b)

                prompt_loop(sp, 0, step)
                sp.wait_ge(hT_mm, 15)
                sp.dma_start(x[0:NS, 0, :], samp_rows).then_inc(x_in[0], 16)
                stores(14, 7, 0)
                sp.wait_ge(h_ok, TP)
                for k, t in enumerate((gain, shift)):
                    for q in range(NSEQ):
                        sp.dma_start(t[q * DSEQ:(q + 1) * DSEQ, :],
                                     S.ada_d[1 + q:2 + q, (1 - k) * D:(2 - k) * D].to_broadcast([DSEQ, D])).then_inc(mod_samp, 16)
                stores(15, 7, 1)
                stores(16, 8, 0)
                sp.wait_ge(vn_ok, 2 * NT)
                sp.dma_start(o.v_sample[0].rearrange("b t d -> (b t) d"), v[0:NS, :]).then_inc(v_out, 16)
                sp.wait_ge(v_out, 16)
                sp.wait_ge(s_out, 16 * NT)
                sp.wait_ge(a_out, 16 * NT)

            @block.gpsimd
            def _(pool):

                def shift_h(i, n, b):
                    r = rows_of(i)
                    pool.wait_ge(xn_ok, i + 1)
                    pool.tensor_tensor(x[0:r, b, :], x[0:r, b, :], shift[0:r, :], ALU.add).then_inc(h_ok, 1)

                def affine_v(i):
                    r = rows_of(i)
                    pool.wait_ge(vhat_ok, i + 1)
                    pool.tensor_tensor(v[0:r, :], v[0:r, :], lng[0:r, :], ALU.mult).then_inc(vn_ok, 1)
                    pool.wait_ge(vn_ok, 2 * i + 1)
                    pool.tensor_tensor(v[0:r, :], v[0:r, :], lnb[0:r, :], ALU.add).then_inc(vn_ok, 1)

                pool.wait_ge(mod_in, 64)
                shift_h(0, 0, 0)

                def step(i, n, b):
                    if not (isinstance(i, int) and i == TP):
                        shift_h(i + 1, n + b, 1 - b)
                    affine_v(i)

                prompt_loop(pool, 0, step)
                for i in (14, 15, 16):
                    step(i, i // 2, i % 2)

            @block.scalar
            def _(act):
                def square(i, n, b):
                    r = rows_of(i)
                    act.wait_ge(x_in[b], 16 * n + 16)
                    act.wait_ge(xn_ok, i)
                    act.activation(junk[0:r, :], x[0:r, b, :], ACT.Square, accum_out=ssq[0:r, b:b + 1]).then_inc(ssq_ok, 1)

                def evac(i, n, b):
                    r = rows_of(i)
                    act.wait_ge(hT_mm, i + 1)
                    for h in range(2):
                        act.activation(hT_hi[:, b, 4 * h:4 * h + 4, 0:r],
                                       pT[:, h, :].rearrange("p (k t) -> p k t", k=4)[:, :, 0:r], ACT.Copy).then_inc(hT_a, 1)

                def step(i, n, b):
                    r = rows_of(i)
                    last = isinstance(i, int) and i == TP
                    if not last:
                        square(i + 1, n + b, 1 - b)
                    act.wait_ge(v_mm, i + 1)
                    act.activation(v[0:r, :], pV[0:r, :], ACT.Gelu_apprx_tanh).then_inc(v_ok, 1)
                    if not last:
                        evac(i + 1, n + b, 1 - b)
                    act.wait_ge(cen_ok, i + 1)
                    for h in range(HEADS):
                        s = act.activation(junk2[0:r, h * HD:(h + 1) * HD], v[0:r, h * HD:(h + 1) * HD], ACT.Square,
                                           accum_out=var[0:r, h:h + 1])
                    s.then_inc(var_ok, 1)
                    act.wait_ge(u_mm, i + 1)
                    act.wait_ge(a_ok, i)
                    act.activation(u[0:r, :], pU[0:r, :], ACT.Gelu_apprx_tanh).then_inc(u_ok, 1)
                    act.wait_ge(s_mm, i + 1)
                    act.wait_ge(s_out, 16 * i)
                    act.activation(s_row[0:r, :], pS[0:r, :], ACT.Copy).then_inc(s_ok, 1)

                square(0, 0, 0)
                for n in range(6):
                    act.wait_ge(win_in[n % 2], 16 * (n // 2 + 1))
                    act.activation(win_hi[:, half_k(n), cols(n)], raw[:, n % 2, :, :], ACT.Copy).then_inc(win_h, 1)
                    if n == 1:
                        evac(0, 0, 0)
                prompt_loop(act, 0, step)
                for i in (14, 15, 16):
                    step(i, i // 2, i % 2)

            @block.tensor
            def _(pe):
                def transposes(i, n, b):
                    r = rows_of(i)
                    pe.wait_ge(h_ok, i + 1)
                    pe.wait_ge(hT_d, 2 * i)
                    for k in range(KD):
                        last = pe.transpose(pT[:, k // 4, k % 4 * P:k % 4 * P + r], x[0:r, b, k * P:(k + 1) * P],
                                            ident[0:r, 0:r])
                    last.then_inc(hT_mm, 1)

                def project(out, i, b, c, free, done):
                    r = rows_of(i)
                    pe.wait_ge(free, i)
                    last = split_matmul(pe, out[0:r, :], lambda t, k: (hT_hi, hT_lo)[t][:, b, k, 0:r],
                                        lambda t, k: (win_hi, win_lo)[t][:, k, c * DA:(c + 1) * DA], KD)
                    last.then_inc(done, 1)

                def step(i, n, b):
                    r = rows_of(i)
                    samp = isinstance(i, int) and i == TP
                    pe.wait_ge(hT_d, 2 * i + 2)
                    if isinstance(i, int) and i == 0:
                        pe.wait_ge(win_l, 2)
                    project(pV, i, b, 1, v_ok, v_mm)
                    if not samp:
                        transposes(i + 1, n + b, 1 - b)
                    if isinstance(i, int) and i == 0:
                        pe.wait_ge(win_l, 4)
                    project(pU, i, b, 0, u_ok, u_mm)
                    if isinstance(i, int) and i == 0:
                        pe.wait_ge(win_l, 6)
                    project(pS, i, b, 2, s_ok, s_mm)
                    pe.wait_ge(vn_ok, 2 * i + 2)
                    pe.wait_ge(a_ok, i)
                    w = S.ws_samp if samp else S.ws
                    for h in range(HEADS):
                        last = pe.matmul(pM[0:r, h * HD:(h + 1) * HD], w[:, h, :], v[0:r, h * HD:(h + 1) * HD],
                                         start=True, stop=True)
                    last.then_inc(m_mm, 1)

                transposes(0, 0, 0)
                prompt_loop(pe, 0, step)
                for i in (14, 15, 16):
                    step(i, i // 2, i % 2)

            @block.vector
            def _(dve):
                c = Steps(dve, ch)

                def scale_x(i, n, b):
                    r = rows_of(i)
                    dve.wait_ge(ssq_ok, i + 1)
                    inv_sqrt(dve, c, rstd[0:r, 0:1], ssq[0:r, b:b + 1], 1.0 / D, newton[0:r, 0, 0:1], newton[0:r, 1, 0:1])
                    dve.scalar_tensor_tensor(out=x[0:r, b, :], in0=x[0:r, b, :], scalar=rstd[0:r, 0:1],
                                             in1=gain[0:r, :], op0=ALU.mult, op1=ALU.mult).then_inc(xn_ok, 1)

                def low_part(i, b):
                    r = rows_of(i)
                    for h in range(2):
                        dve.wait_ge(hT_a, 2 * i + h + 1)
                        ks = slice(4 * h, 4 * h + 4)
                        dve.tensor_tensor(hT_lo[:, b, ks, 0:r], pT[:, h, :].rearrange("p (k t) -> p k t", k=4)[:, :, 0:r],
                                          hT_hi[:, b, ks, 0:r].bitcast(F32), ALU.subtract).then_inc(hT_d, 1)

                def step(i, n, b):
                    r = rows_of(i)
                    samp = isinstance(i, int) and i == TP
                    if not samp:
                        if isinstance(i, int) and i == TP - 1:
                            dve.wait_ge(mod_samp, 16 * 2 * NSEQ)
                        scale_x(i + 1, n + b, 1 - b)
                    v3 = v[0:r, :].rearrange("p (h d) -> p h d", h=HEADS)
                    s3 = [r, HEADS, HD]
                    dve.wait_ge(v_ok, i + 1)
                    c.link(dve.tensor_reduce(mean[0:r, :], v3, AX.X, ALU.add))
                    c.link(dve.tensor_scalar(mean[0:r, :], mean[0:r, :], 1.0 / HD, None, ALU.mult))
                    dve.tensor_tensor(v3, v3, fan(mean[0:r, :], s3), ALU.subtract).then_inc(cen_ok, 1)
                    if not samp:
                        low_part(i + 1, 1 - b)
                    dve.wait_ge(var_ok, i + 1)
                    inv_sqrt(dve, c, mean[0:r, :], var[0:r, :], 1.0 / HD, newton[0:r, 0, :], newton[0:r, 1, :])
                    dve.tensor_tensor(v3, v3, fan(mean[0:r, :], s3), ALU.mult).then_inc(vhat_ok, 1)
                    dve.wait_ge(m_mm, i + 1)
                    dve.wait_ge(u_ok, i + 1)
                    dve.wait_ge(a_out, 16 * i)
                    bs = S.bs_samp if samp else S.bs
                    for h in range(HEADS):
                        hs = slice(h * HD, (h + 1) * HD)
                        last = dve.scalar_tensor_tensor(out=a_row[0:r, hs], in0=pM[0:r, hs], scalar=bs[0:r, h:h + 1],
                                                        in1=u[0:r, hs], op0=ALU.add, op1=ALU.mult)
                    last.then_inc(a_ok, 1)

                dve.wait_ge(mod_in, 64)
                scale_x(0, 0, 0)
                for n in range(6):
                    dve.wait_ge(win_h, n + 1)
                    dve.tensor_tensor(win_lo[:, half_k(n), cols(n)], raw[:, n % 2, :, :],
                                      win_hi[:, half_k(n), cols(n)].bitcast(F32), ALU.subtract).then_inc(win_l, 1)
                    if n == 1:
                        low_part(0, 0)
                prompt_loop(dve, 0, step, lambda j: c.at(INV + CH1 * j))
                c.at(INV + CH1 * 7)
                for i in (14, 15, 16):
                    step(i, i // 2, i % 2)


CH1 = 2 * (2 * INV + 2)


def s5(nc, S, a, o):
    with ExitStack() as st:
        sb, sem = S.sb, S.sem
        rows = sb(st, "chunk_rows", [P, 2, Q, DA])
        uT = sb(st, "uT", [P, G, CH])
        h_re = sb(st, "h_re", [P, PAIRS, CH + 1])
        h_im = sb(st, "h_im", [P, PAIRS, CH + 1])
        h0_in = sb(st, "h0_in", [P, 2, P])
        fin = sb(st, "fin", [P, 2, NSEQ, PAIRS])
        f1 = sb(st, "f1", [P, 2, NSEQ])
        rows_samp = sb(st, "samp_rows", [NSEQ, Q, DA])
        toep = sb(st, "toep", [P, G, P])
        turn = sb(st, "turn", [P, 4, 2, NCH])
        rot = sb(st, "rot", [P, 2, 4, NCH])
        scan = sb(st, "scan", [P, 2, 2, NCH])
        back = sb(st, "back", [P, 2, NCH])
        fo = sb(st, "fo", [P, 2, P])
        po = sb(st, "po", [PAIRS, 2, P])
        pX = S.psum(st, "ps_x", [P, 4, 512])
        pB = S.psum(st, "ps_b", [P, 4, 512])
        ident = S.ident

        rows_in, u_mm, u_a, u_d, h0_l, h0_mm, h0_ok = [sem(f"chunks_loaded{i}") for i in range(3)], sem("uT_mm"), sem("uT_evac_act"), sem("uT_evac_dve"), sem("h0_loaded"), sem("h0_mm"), sem("h0_ready")
        x_mm, x_free, scan_ok, h_ok, ch, ph = sem("state_mm"), sem("state_free"), sem("scan_ready"), sem("state_ready"), sem("dve_chain2"), sem("pool_chain2")
        y_mm, y_ok, y_out, f_mm, f_ok, f_out, fin_ok = sem("y_mm"), sem("y_gelu"), [sem("y_stored")], sem("final_mm"), sem("final_copied"), sem("final_stored"), sem("sample_state")
        h_free = sem("scan_free")
        WIDTH = (P, P, NSEQ)
        at = (0, P, NCH)
        s_rows = S.s_d.rearrange("(c s) n -> c s n", s=Q)
        y_rows = S.y_d.rearrange("(c s) n -> c s n", s=Q)

        by_group = [h[:, :, :].rearrange("p a c -> p (a c)")[:, 0:Q * DA] for h in (h_re, h_im, h_re)]
        toep_in, turn_in = sem("toep_loaded"), [sem(f"turn_loaded{i}") for i in range(4)]

        def row_tile(t):
            return rows_samp[:, :, :] if t == 2 else rows[:, t, :, :]

        perm_a, perm_d = sem("regrouped_act"), sem("regrouped_dve")

        def regroup(eng, t, half):
            w = WIDTH[t]
            gs = slice(half * G // 2, (half + 1) * G // 2)
            eng.wait_ge(rows_in[t], 16)
            if t == 2:
                eng.wait_ge(u_mm, 8)
            dst = by_group[t][0:w, :].rearrange("p (g s h) -> p g s h", g=G, s=Q)[:, gs, :, :]
            src = row_tile(t).rearrange("p s (g h) -> p g s h", g=G)[:, gs, :, :]
            if half == 0:
                eng.activation(dst, src, ACT.Copy).then_inc(perm_a, 1)
            else:
                eng.tensor_copy(dst, src).then_inc(perm_d, 1)

        with nc.Block() as block:
            @block.sync
            def _(sp):
                for t in range(2):
                    sp.dma_start(rows[:, t, :, :], s_rows[at[t]:at[t] + P, :, :]).then_inc(rows_in[t], 16)
                for i, x in enumerate((a.state_ssm_re, a.state_ssm_im)):
                    sp.dma_start(h0_in[:, i, :], x[0].rearrange("q (a g) p -> (q a) (g p)", g=2)).then_inc(h0_l, 16)
                sp.dma_start(rows_samp[:, :, :], s_rows[NCH:CH, :, :]).then_inc(rows_in[2], 16)
                for k in range(4):
                    sp.dma_start(turn[:, k, :, :], S.rot_d[:, k, :, :]).then_inc(turn_in[k], 16)
                for s in range(Q):
                    sp.dma_start(toep[s * GC:(s + 1) * GC, :, :], S.kpad_d[:, :, P - s * GC:2 * P - s * GC]).then_inc(toep_in, 16)
                for k in range(4, PAIRS):
                    sp.wait_ge(h_ok, 2 * (k - 3))
                    sp.dma_start(turn[:, k % 4, :, :], S.rot_d[:, k, :, :]).then_inc(turn_in[k % 4], 16)
                for t in range(3):
                    sp.wait_ge(y_ok, 20 + 2 * t)
                    sp.dma_start(y_rows[at[t]:at[t] + WIDTH[t], :, :], row_tile(t)).then_inc(y_out[0], 16)
                sp.wait_ge(f_ok, 4)
                for i, (x, y) in enumerate(((o.ssm_re_prompt, o.ssm_re_sample), (o.ssm_im_prompt, o.ssm_im_sample))):
                    sp.dma_start(x[0, 0].rearrange("(a g) p -> a (g p)", g=2), po[:, i, :]).then_inc(f_out, 16)
                    sp.dma_start(y[0].rearrange("q (a g) p -> (q a) (g p)", g=2), fo[:, i, :]).then_inc(f_out, 16)
                sp.wait_ge(f_out, 64)
                sp.wait_ge(y_out[0], 48)

            @block.tensor
            def _(pe):
                for n in range(24):
                    t, m = n // 8, n % 8
                    w = WIDTH[t]
                    if m % 4 == 0:
                        pe.wait_ge((perm_a, perm_d)[m // 4], t + 1)
                    if n >= 2:
                        pe.wait_ge((u_a, u_d)[n % 2], n // 2)
                    for q in range(4):
                        g = 4 * m + q
                        last = pe.transpose(pB[:, n % 2, q * P:q * P + w], by_group[t][0:w, g * P:(g + 1) * P],
                                            ident[0:w, 0:w])
                    last.then_inc(u_mm, 1)
                pe.wait_ge(h0_l, 32)
                for i in range(2):
                    last = pe.transpose(pB[:, 2, i * P:(i + 1) * P], h0_in[:, i, :], ident[:, :])
                last.then_inc(h0_mm, 1)
                pe.wait_ge(u_a, 12)
                pe.wait_ge(u_d, 12)
                def additions(k):
                    if k >= 2:
                        pe.wait_ge(x_free, k - 1)
                    for i in range(2):
                        for g in range(2):
                            r = slice(g * ST, (g + 1) * ST)
                            last = pe.matmul(pX[r, 2 * (k % 2) + i, 0:CH], S.wx[:, k, i, r], uT[:, 2 * k + g, :],
                                             start=True, stop=True)
                    last.then_inc(x_mm, 1)
                def outputs(n):
                    m, t, r2 = n // 6, n % 6 // 2, n % 2
                    w = WIDTH[t]
                    r = slice(r2 * ST, (r2 + 1) * ST)
                    if n == 0:
                        pe.wait_ge(toep_in, 16 * Q)
                    if n >= 4:
                        pe.wait_ge(y_ok, n - 3)
                    for q in range(4):
                        k = 4 * m + q
                        g = 2 * k + r2
                        if t == 0 and r2 == 0:
                            pe.wait_ge(h_ok, 2 * (k + 1))
                        c0 = at[t] + (1 if t == 2 else 0)
                        out = pB[0:w, n % 4, q * P:(q + 1) * P]
                        pe.matmul(out, uT[:, g, at[t]:at[t] + w], toep[:, g, :], start=True, stop=False)
                        pe.matmul(out, h_re[r, k, c0:c0 + w], S.m_re[r, k, 1:9, :].rearrange("p k o -> p (k o)"),
                                  start=False, stop=False)
                        last = pe.matmul(out, h_im[r, k, c0:c0 + w], S.m_im[r, k, 1:9, :].rearrange("p k o -> p (k o)"),
                                         start=False, stop=True)
                    last.then_inc(y_mm, 1)

                for k in range(4):
                    additions(k)
                pe.wait_ge(h0_ok, 2)
                for m in range(4):
                    for n in range(6 * m, 6 * m + 6):
                        if m < 3 and n % 6 < 4:
                            additions(4 * m + 4 + n % 6)
                        outputs(n)
                pe.wait_ge(y_ok, 24)
                pe.wait_ge(fin_ok, 2 * PAIRS)
                for i, h in enumerate((h_re, h_im)):
                    pe.transpose(pB[0:PAIRS, 3, i * P:(i + 1) * P], h[:, :, NCH], ident[:, :])
                for i in range(2):
                    last = pe.transpose(pB[:, 2, i * P:(i + 1) * P], fin[:, i, :, :].rearrange("p q a -> p (q a)"), ident[:, :])
                last.then_inc(f_mm, 1)

            @block.scalar
            def _(act):
                for n in range(0, 24, 2):
                    t, m = n // 8, n % 8
                    w = WIDTH[t]
                    if m == 0:
                        regroup(act, t, 0)
                    act.wait_ge(u_mm, n + 1)
                    act.activation(uT[:, 4 * m:4 * m + 4, at[t]:at[t] + w],
                                   pB[:, 0, :].rearrange("p (g c) -> p g c", g=4)[:, :, 0:w], ACT.Copy).then_inc(u_a, 1)
                for n in range(24):
                    m, t, r2 = n // 6, n % 6 // 2, n % 2
                    w = WIDTH[t]
                    act.wait_ge(y_mm, n + 1)
                    out = row_tile(t).rearrange("p s (m q r o) -> p m r q s o", m=4, q=4, r=2)[:, m, r2, :, :, :]
                    act.activation(out, pB[0:w, n % 4, :].rearrange("p (q s o) -> p q s o", q=4, s=Q),
                                   ACT.Gelu_apprx_tanh).then_inc(y_ok, 1)

            @block.vector
            def _(dve):
                c = Steps(dve, ch)
                for n in range(1, 24, 2):
                    t, m = n // 8, n % 8
                    w = WIDTH[t]
                    if m == 1:
                        regroup(dve, t, 1)
                    dve.wait_ge(u_mm, n + 1)
                    dve.tensor_copy(uT[:, 4 * m:4 * m + 4, at[t]:at[t] + w],
                                    pB[:, 1, :].rearrange("p (g c) -> p g c", g=4)[:, :, 0:w]).then_inc(u_d, 1)
                dve.wait_ge(h0_mm, 1)
                for i, h in enumerate((h_re, h_im)):
                    dve.tensor_copy(h[:, :, NCH + 1:CH + 1],
                                    pB[:, 2, i * P:(i + 1) * P].rearrange("p (q a) -> p a q", q=NSEQ)).then_inc(h0_ok, 1)
                dve.wait_ge(h0_ok, 2)

                def col(t, k):
                    return t[:, ds(k, 1)]

                def pair(k, b, q, j):
                    dve.wait_ge(turn_in[q], 16 * j + 16)
                    R, I = pX[:, 2 * b, :], pX[:, 2 * b + 1, :]
                    C, N = turn[:, q, 0, :], turn[:, q, 1, :]
                    dve.wait_ge(x_mm, k + 1)
                    dve.wait_ge(scan_ok, 2 * k + 2)
                    c.did(dve.tensor_tensor(rot[:, b, 0, :], R[:, 0:NCH], C, ALU.mult))
                    c.did(dve.tensor_tensor(rot[:, b, 1, :], I[:, 0:NCH], N, ALU.mult))
                    c.did(dve.tensor_tensor(rot[:, b, 2, :], I[:, 0:NCH], C, ALU.mult))
                    c.link(dve.tensor_tensor(rot[:, b, 3, :], R[:, 0:NCH], N, ALU.mult))
                    h0r = h_re[:, ds(k, 1), NCH + 1:CH + 1].rearrange("p o c -> p (o c)")
                    h0i = h_im[:, ds(k, 1), NCH + 1:CH + 1].rearrange("p o c -> p (o c)")
                    c.did(dve.scalar_tensor_tensor(out=f1[:, 0, :], in0=h0r, scalar=col(S.a8_re, k), in1=R[:, NCH:CH],
                                                   op0=ALU.mult, op1=ALU.add))
                    c.link(dve.scalar_tensor_tensor(out=f1[:, 1, :], in0=h0r, scalar=col(S.a8_im, k), in1=I[:, NCH:CH],
                                                    op0=ALU.mult, op1=ALU.add))
                    dve.scalar_tensor_tensor(out=fin[:, 0, :, ds(k, 1)].rearrange("p q o -> p (q o)"), in0=h0i,
                                             scalar=col(S.na8_im, k), in1=f1[:, 0, :], op0=ALU.mult, op1=ALU.add).then_inc(fin_ok, 1)
                    dve.scalar_tensor_tensor(out=fin[:, 1, :, ds(k, 1)].rearrange("p q o -> p (q o)"), in0=h0i,
                                             scalar=col(S.a8_re, k), in1=f1[:, 1, :], op0=ALU.mult, op1=ALU.add).then_inc(fin_ok, 1)
                    dve.wait_ge(fin_ok, 2 * k + 2)
                    c.did(dve.tensor_tensor(rot[:, b, 0, :], rot[:, b, 0, :], rot[:, b, 1, :], ALU.add))
                    c.link(dve.tensor_tensor(rot[:, b, 2, :], rot[:, b, 2, :], rot[:, b, 3, :], ALU.subtract))
                    dve.sem_inc(x_free, 1)
                    dve.wait_ge(h_free, k + 1)
                    for i in range(2):
                        dve.tensor_tensor_scan(scan[:, b, i, :], col(S.decay, k).to_broadcast([P, NCH]),
                                               rot[:, b, 2 * i, :], 0.0, ALU.mult, ALU.add).then_inc(scan_ok, 1)

                dve.sem_inc(scan_ok, 2)
                with dve.Fori(0, PAIRS // 4) as j:
                    c.at(8 * 4 * j)
                    for q in range(4):
                        pair(4 * j + q, q % 2, q, j)
                assert c.count == 8 * 4
                dve.wait_ge(f_mm, 1)
                for i in range(2):
                    dve.tensor_copy(po[:, i, :], pB[0:PAIRS, 3, i * P:(i + 1) * P]).then_inc(f_ok, 1)
                    dve.tensor_copy(fo[:, i, :], pB[:, 2, i * P:(i + 1) * P]).then_inc(f_ok, 1)

            @block.gpsimd
            def _(pool):
                p = Steps(pool, ph)
                pool.wait_ge(u_mm, 24)
                p.did(pool.memset(h_re[:, :, 0:1], 0.0))
                p.link(pool.memset(h_im[:, :, 0:1], 0.0))
                pool.sem_inc(h_free, 2)

                def pair(k, b, q):
                    C, N = turn[:, q, 0, :], turn[:, q, 1, :]
                    re = h_re[:, ds(k, 1), 1:NCH + 1].rearrange("p o c -> p (o c)")
                    im = h_im[:, ds(k, 1), 1:NCH + 1].rearrange("p o c -> p (o c)")
                    pool.wait_ge(scan_ok, 2 * k + 4)
                    p.did(pool.tensor_tensor(re, scan[:, b, 0, :], C, ALU.mult))
                    p.did(pool.tensor_tensor(im, scan[:, b, 0, :], N, ALU.mult))
                    p.did(pool.tensor_tensor(back[:, 0, :], scan[:, b, 1, :], N, ALU.mult))
                    p.link(pool.tensor_tensor(back[:, 1, :], scan[:, b, 1, :], C, ALU.mult))
                    pool.sem_inc(h_free, 1)
                    pool.tensor_tensor(re, re, back[:, 0, :], ALU.subtract).then_inc(h_ok, 1)
                    pool.tensor_tensor(im, im, back[:, 1, :], ALU.add).then_inc(h_ok, 1)
                    pool.wait_ge(h_ok, 2 * k + 2)

                with pool.Fori(0, PAIRS // 4) as j:
                    p.at(2 + 4 * 4 * j)
                    for q in range(4):
                        pair(4 * j + q, q % 2, q)
                assert p.count == 2 + 4 * 4


def mixout(nc, S, a):
    with ExitStack() as st:
        sb, sem = S.sb, S.sem
        raw = sb(st, "weights_raw", [P, 2, 2 * D])
        wout_hi = sb(st, "wout_hi", [P, KD, D], F32R)
        wout_lo = sb(st, "wout_lo", [P, KD, D], F32R)
        wglu_hi = sb(st, "wglu_hi", [P, 4, DA], F32R)
        wglu_lo = sb(st, "wglu_lo", [P, 4, DA], F32R)
        wr = sb(st, "wr", [P, KD, NR])
        bglu = sb(st, "bglu", [P, DA])
        br = sb(st, "br", [P, NR])
        gate = sb(st, "gate1", [P, D])
        gain = sb(st, "gain2", [P, D])
        shift = sb(st, "shift2", [P, D])
        blank = sb(st, "blank", [P, D])
        cat = sb(st, "cat", [P, 2, D])
        x2 = sb(st, "x2", [P, 2, D])
        yT_hi = sb(st, "yT_hi", [P, 4, P], F32R)
        yT_lo = sb(st, "yT_lo", [P, 4, P], F32R)
        catT_hi = sb(st, "catT_hi", [P, KD, P], F32R)
        catT_lo = sb(st, "catT_lo", [P, KD, P], F32R)
        z = sb(st, "z", [P, DA])
        mixed = sb(st, "mixed", [P, 2, DA])
        h2 = sb(st, "h2", [P, D])
        h2T = sb(st, "h2T", [P, KD, P])
        junk = sb(st, "junk3", [P, D])
        ssq = sb(st, "ssq2", [P, 1])
        rstd = sb(st, "rstd2", [P, 1])
        newton = sb(st, "newton2", [P, 2])
        pY = S.psum(st, "ps_yT", [P, 512])
        pZ = S.psum(st, "ps_z", [P, 512])
        pC = S.psum(st, "ps_catT", [P, 2, 512])
        pM = S.psum(st, "ps_out", [P, 2, 512])
        pH = S.psum(st, "ps_h2T", [P, 2, 512])
        ident, lg = S.ident, S.logits

        mod_in, mod_s, w_in, w_h, w_l = sem("mod2_loaded"), sem("mod2_sample_loaded"), [sem(f"weights_loaded{i}") for i in range(2)], sem("weights_hi"), sem("weights_lo")
        a_in, x_in = [sem("cat_loaded0"), sem("cat_loaded1")], [sem("x2_in0"), sem("x2_in1")]
        yT_mm, yT_a, yT_d, z_mm, z_ok, sg_ok, b_ok = sem("yT_mm"), sem("yT_hi_ready"), sem("yT_lo_ready"), sem("z_mm"), sem("z_ok"), sem("sigmoid_ok"), sem("y_gated")
        c_mm, c_a, c_d, o_mm, mul_ok, x2_ok = sem("catT_mm"), sem("catT_hi_ready"), sem("catT_lo_ready"), sem("out_mm"), sem("gated"), sem("x2_ready")
        sq_ok, xs_ok, h2_ok, h_mm, h_a, h_d, l_mm, l_ok, h2_out, ch = (sem("ssq2_ready"), sem("x2_scaled"), sem("h2_ready"), sem("h2T_mm"), sem("h2T_act"), sem("h2T_dve"), sem("logit_mm"), sem("logits_ready"), sem("h2_stored"), sem("dve_chain3"))
        x2_out, blank_ok, blank_out = sem("x2_stored"), sem("blank_ready"), sem("blank_stored")
        w_glu, w_out = a.w_glu[0].rearrange("(k p) n -> p k n", p=P), a.w_out[0].rearrange("(k p) n -> p k n", p=P)
        NPART = 5

        def part(t_glu, t_out, n):
            return t_glu[:, :, :] if n == 0 else t_out[:, 2 * n - 2:2 * n, :]

        def raw_part(n):
            return raw[:, n % 2, :].rearrange("p (k n) -> p k n", k=4 if n == 0 else 2)

        def rows_of(i):
            return NS if isinstance(i, int) and i == TP else P

        def dr(t, i):
            return t[TP * P:TOK, :] if isinstance(i, int) and i == TP else t[ds(i * P, P), :]

        def tiles(eng, step):
            step(0, 0, 0)
            prompt_loop(eng, 1, step)
            step(15, 7, 1)
            step(16, 8, 0)

        with nc.Block() as block:
            @block.sync
            def _(sp):
                def load_cat(i, b):
                    r = rows_of(i)
                    sp.dma_start(cat[0:r, b, DA:D], dr(S.y_d, i)).then_inc(a_in[b], 16)
                    sp.dma_start(cat[0:r, b, 0:DA], dr(S.a_d, i)).then_inc(a_in[b], 16)

                def load_x(i, b):
                    x = a.x_sample.rearrange("b t d -> (b t) d") if rows_of(i) == NS else a.x_prompt[0, ds(i * P, P), :]
                    sp.dma_start(x2[0:rows_of(i), b, :], x).then_inc(x_in[b], 16)

                load_cat(0, 0)
                for n in range(NPART):
                    if n >= 2:
                        sp.wait_ge(w_l, n - 1)
                    sp.dma_start(raw_part(n), part(w_glu, w_out, n)).then_inc(w_in[n % 2], 16)
                    if n == 1:
                        sp.dma_start(bglu[:, :], a.b_glu.to_broadcast([P, DA])).then_inc(mod_in, 16)
                        for t, c in ((gate, 2), (gain, 4), (shift, 3)):
                            sp.dma_start(t[:, :], S.ada_d[0:1, c * D:(c + 1) * D].to_broadcast([P, D])).then_inc(mod_in, 16)
                        load_x(0, 0)
                        load_cat(1, 1)
                        sp.dma_start(wr[:, :, 0:EG], a.w_group[0].rearrange("(k p) n -> p k n", p=P)).then_inc(mod_in, 16)
                        sp.dma_start(wr[:, :, EG:NR], a.w_expert[0].rearrange("(k p) n -> p k n", p=P)).then_inc(mod_in, 16)
                        sp.dma_start(br[:, 0:EG], a.b_group.to_broadcast([P, EG])).then_inc(mod_in, 16)
                        sp.dma_start(br[:, EG:NR], a.b_expert.to_broadcast([P, NE])).then_inc(mod_in, 16)
                load_x(1, 1)
                sp.wait_ge(blank_ok, 1)

                def step(i, n, b):
                    static = isinstance(i, int)
                    if not (static and i + 2 > TP):
                        sp.wait_ge(c_mm, i + 1)
                        load_cat(i + 2, b)
                    if static and i == TP:
                        for q in range(NSEQ):
                            sp.dma_start(gate[q * DSEQ:(q + 1) * DSEQ, :],
                                         S.ada_d[1 + q:2 + q, 2 * D:3 * D].to_broadcast([DSEQ, D])).then_inc(mod_s, 16)
                        for t, c in ((gain, 4), (shift, 3)):
                            for q in range(NSEQ):
                                sp.dma_start(t[q * DSEQ:(q + 1) * DSEQ, :],
                                             S.ada_d[1 + q:2 + q, c * D:(c + 1) * D].to_broadcast([DSEQ, D])).then_inc(mod_s, 16)
                    sp.wait_ge(x2_ok, 2 * i + 2)
                    sp.dma_start(dr(S.x2_d, i), x2[0:rows_of(i), b, :]).then_inc(x2_out, 16)
                    for k in range(2):
                        if not (static and 2 * i + k >= NBLK - FULL):
                            sp.dma_start(S.yb_d[ds((FULL + k + 2 * i) * P, P), :], blank[:, :]).then_inc(blank_out, 16)
                    sp.wait_ge(h2_ok, i + 1)
                    sp.dma_start(dr(S.h2_d, i), h2[0:rows_of(i), :]).then_inc(h2_out, 16)
                    if not (static and i + 2 > TP):
                        sp.wait_ge(x2_out, 16 * i + 16)
                        load_x(i + 2, b)

                prompt_loop(sp, 0, step)
                for i in (14, 15, 16):
                    step(i, i // 2, i % 2)
                sp.wait_ge(h2_out, 16 * NT)
                sp.wait_ge(x2_out, 16 * NT)
                sp.wait_ge(blank_out, 16 * (NBLK - FULL))

            @block.tensor
            def _(pe):
                def turn_y(i, n, b):
                    r = rows_of(i)
                    pe.wait_ge(a_in[b], 32 * n + 32)
                    pe.wait_ge(yT_d, i)
                    for k in range(4):
                        last = pe.transpose(pY[:, k * P:k * P + r], cat[0:r, b, DA + k * P:DA + (k + 1) * P], ident[0:r, 0:r])
                    last.then_inc(yT_mm, 1)

                def glu(i, n, b, logits_out):
                    r = rows_of(i)
                    pe.wait_ge(yT_d, i + 1)
                    pe.wait_ge(l_ok, logits_out)
                    split_matmul(pe, pZ[0:r, :], lambda t, k: (yT_hi, yT_lo)[t][:, k, 0:r],
                                 lambda t, k: (wglu_hi, wglu_lo)[t][:, k, :], 4).then_inc(z_mm, 1)

                def turn_cat(i, n, b):
                    r = rows_of(i)
                    pe.wait_ge(b_ok, i + 1)
                    pe.wait_ge(c_d, 2 * i)
                    for k in range(KD):
                        last = pe.transpose(pC[:, k // 4, k % 4 * P:k % 4 * P + r], cat[0:r, b, k * P:(k + 1) * P],
                                            ident[0:r, 0:r])
                    last.then_inc(c_mm, 1)

                def project(i, b, c):
                    r = rows_of(i)
                    pe.wait_ge(c_d, 2 * i + 2)
                    if not (isinstance(i, int) and i == 0):
                        pe.wait_ge(mul_ok, 2 * i - 1 + c)
                    cols = slice(c * DA, (c + 1) * DA)
                    split_matmul(pe, pM[0:r, c, :], lambda t, k: (catT_hi, catT_lo)[t][:, k, 0:r],
                                 lambda t, k: (wout_hi, wout_lo)[t][:, k, cols], KD).then_inc(o_mm, 1)

                def logits(i, z_done):
                    r = rows_of(i)
                    pe.wait_ge(h2_ok, i + 1)
                    pe.wait_ge(h_a, i)
                    pe.wait_ge(h_d, i)
                    for k in range(KD):
                        last = pe.transpose(pH[:, k // 4, k % 4 * P:k % 4 * P + r], h2[0:r, k * P:(k + 1) * P],
                                            ident[0:r, 0:r])
                    last.then_inc(h_mm, 1)
                    pe.wait_ge(h_a, i + 1)
                    pe.wait_ge(h_d, i + 1)
                    pe.wait_ge(z_ok, z_done)
                    for k in range(KD):
                        last = pe.matmul(pZ[0:r, 0:NR], h2T[:, k, 0:r], wr[:, k, :], start=k == 0, stop=k == KD - 1)
                    last.then_inc(l_mm, 1)

                def step(i, n, b):
                    first, last = isinstance(i, int) and i == 0, isinstance(i, int) and i == TP
                    if not last:
                        turn_y(i + 1, n + b, 1 - b)
                    project(i, b, 0)
                    if not last:
                        glu(i + 1, n + b, 1 - b, 0 if first else i - 1)
                    project(i, b, 1)
                    if not last:
                        turn_cat(i + 1, n + b, 1 - b)
                    if not first:
                        logits(i - 1, NT if last else i + 2)

                turn_y(0, 0, 0)
                pe.wait_ge(w_l, 1)
                glu(0, 0, 0, 0)
                turn_cat(0, 0, 0)
                pe.wait_ge(w_l, NPART)
                pe.wait_ge(mod_in, 16 * 8)
                tiles(pe, step)
                logits(TP, NT)

            @block.scalar
            def _(act):
                def evac_y(i, b):
                    r = rows_of(i)
                    act.wait_ge(yT_mm, i + 1)
                    act.activation(yT_hi[:, :, 0:r], pY[:, :].rearrange("p (k t) -> p k t", k=4)[:, :, 0:r], ACT.Copy).then_inc(yT_a, 1)

                def sigmoid(i, b):
                    r = rows_of(i)
                    act.wait_ge(z_ok, i + 1)
                    act.activation(z[0:r, :], z[0:r, :], ACT.Sigmoid).then_inc(sg_ok, 1)

                def evac(i, b):
                    r = rows_of(i)
                    act.wait_ge(c_mm, i + 1)
                    for h in range(2):
                        act.activation(catT_hi[:, 4 * h:4 * h + 4, 0:r],
                                       pC[:, h, :].rearrange("p (k t) -> p k t", k=4)[:, :, 0:r], ACT.Copy).then_inc(c_a, 1)

                def evac_h(i):
                    r = rows_of(i)
                    act.wait_ge(h_mm, i + 1)
                    act.wait_ge(l_mm, i)
                    act.activation(h2T[:, 0:4, 0:r], pH[:, 0, :].rearrange("p (k t) -> p k t", k=4)[:, :, 0:r],
                                   ACT.Copy).then_inc(h_a, 1)

                def step(i, n, b):
                    first, last = isinstance(i, int) and i == 0, isinstance(i, int) and i == TP
                    if not last:
                        evac_y(i + 1, 1 - b)
                        sigmoid(i + 1, 1 - b)
                        evac(i + 1, 1 - b)
                    if not first:
                        evac_h(i - 1)
                    act.wait_ge(x2_ok, 2 * i + 2)
                    act.wait_ge(xs_ok, i)
                    act.activation(junk[0:rows_of(i), :], x2[0:rows_of(i), b, :], ACT.Square,
                                   accum_out=ssq[0:rows_of(i), :]).then_inc(sq_ok, 1)

                evac_y(0, 0)
                for n in range(NPART):
                    act.wait_ge(w_in[n % 2], 16 * (n // 2 + 1))
                    act.activation(part(wglu_hi, wout_hi, n), raw_part(n), ACT.Copy).then_inc(w_h, 1)
                    if n == 1:
                        sigmoid(0, 0)
                evac(0, 0)
                tiles(act, step)
                evac_h(TP)

            @block.gpsimd
            def _(pool):
                def gate_y(i, n, b):
                    r = rows_of(i)
                    pool.wait_ge(sg_ok, i + 1)
                    pool.tensor_tensor(cat[0:r, b, DA:D], cat[0:r, b, DA:D], z[0:r, :], ALU.mult).then_inc(b_ok, 1)

                def residual(i, n, b, c):
                    r = rows_of(i)
                    if c == 0:
                        pool.wait_ge(x_in[b], 16 * n + 16)
                    pool.wait_ge(mul_ok, 2 * i + c + 1)
                    half = x2[0:r, b, c * DA:(c + 1) * DA]
                    pool.tensor_tensor(half, half, mixed[0:r, c, :], ALU.add).then_inc(x2_ok, 1)

                def step(i, n, b):
                    r = rows_of(i)
                    last = isinstance(i, int) and i == TP
                    residual(i, n, b, 0)
                    if not last:
                        gate_y(i + 1, n + b, 1 - b)
                    residual(i, n, b, 1)
                    pool.wait_ge(xs_ok, i + 1)
                    pool.tensor_tensor(h2[0:r, :], h2[0:r, :], shift[0:r, :], ALU.add).then_inc(h2_ok, 1)

                pool.memset(blank[:, :], 0.0).then_inc(blank_ok, 1)
                gate_y(0, 0, 0)
                tiles(pool, step)

            @block.vector
            def _(dve):
                c = Steps(dve, ch)

                def gated(i, h):
                    r = rows_of(i)
                    dve.wait_ge(o_mm, 2 * i + h + 1)
                    dve.wait_ge(x2_ok, 2 * i)
                    dve.tensor_tensor(mixed[0:r, h, :], pM[0:r, h, :], gate[0:r, h * DA:(h + 1) * DA], ALU.mult).then_inc(mul_ok, 1)

                def bias_z(i):
                    r = rows_of(i)
                    dve.wait_ge(z_mm, i + 1)
                    dve.wait_ge(b_ok, i)
                    dve.tensor_tensor(z[0:r, :], pZ[0:r, :], bglu[0:r, :], ALU.add).then_inc(z_ok, 1)

                def rest(lo, hi, ps, r):
                    return dve.tensor_tensor(lo, ps.rearrange("p (k t) -> p k t", k=4)[:, :, 0:r], hi.bitcast(F32), ALU.subtract)

                def low_y(i):
                    r = rows_of(i)
                    dve.wait_ge(yT_a, i + 1)
                    rest(yT_lo[:, :, 0:r], yT_hi[:, :, 0:r], pY[:, :], r).then_inc(yT_d, 1)

                def low_cat(i):
                    r = rows_of(i)
                    for h in range(2):
                        ks = slice(4 * h, 4 * h + 4)
                        dve.wait_ge(c_a, 2 * i + h + 1)
                        rest(catT_lo[:, ks, 0:r], catT_hi[:, ks, 0:r], pC[:, h, :], r).then_inc(c_d, 1)

                def logits(i):
                    r = rows_of(i)
                    dve.wait_ge(h_mm, i + 1)
                    dve.wait_ge(l_mm, i)
                    dve.tensor_copy(h2T[:, 4:8, 0:r],
                                    pH[:, 1, :].rearrange("p (k t) -> p k t", k=4)[:, :, 0:r]).then_inc(h_d, 1)
                    dve.wait_ge(l_mm, i + 1)
                    dve.tensor_tensor(lg[0:r, ds(i, 1), :].rearrange("p o n -> p (o n)"), pZ[0:r, 0:NR], br[0:r, :],
                                      ALU.add).then_inc(l_ok, 1)

                def step(i, n, b):
                    r = rows_of(i)
                    first, last = isinstance(i, int) and i == 0, isinstance(i, int) and i == TP
                    if last:
                        dve.wait_ge(mod_s, 16 * 3 * NSEQ)
                    if not last:
                        low_y(i + 1)
                    gated(i, 0)
                    if not last:
                        bias_z(i + 1)
                    gated(i, 1)
                    if not last:
                        low_cat(i + 1)
                    if not first:
                        logits(i - 1)
                    dve.wait_ge(sq_ok, i + 1)
                    inv_sqrt(dve, c, rstd[0:r, :], ssq[0:r, :], 1.0 / D, newton[0:r, 0:1], newton[0:r, 1:2])
                    dve.wait_ge(h_mm, i)
                    dve.wait_ge(h2_out, 16 * i)
                    dve.scalar_tensor_tensor(out=h2[0:r, :], in0=x2[0:r, b, :], scalar=rstd[0:r, :], in1=gain[0:r, :],
                                             op0=ALU.mult, op1=ALU.mult).then_inc(xs_ok, 1)

                low_y(0)
                for n in range(NPART):
                    dve.wait_ge(w_h, n + 1)
                    dve.tensor_tensor(part(wglu_lo, wout_lo, n), raw_part(n), part(wglu_hi, wout_hi, n).bitcast(F32),
                                      ALU.subtract).then_inc(w_l, 1)
                    if n == 0:
                        dve.wait_ge(mod_in, 16 * 8)
                        bias_z(0)
                low_cat(0)
                step(0, 0, 0)
                prompt_loop(dve, 1, step, lambda j: c.at(INV + 2 * INV * j))
                c.at(15 * INV)
                step(15, 7, 1)
                step(16, 8, 0)
                logits(TP)


COLS = NBLK + 3


def route(nc, S):
    with ExitStack() as st:
        sb, sem = S.sb, S.sem
        N2 = 2 * NT
        iota = sb(st, "iota", [P, P])
        tok = sb(st, "tok", [P, N2])
        w4 = sb(st, "w4", [P, EG])
        w32 = sb(st, "w32", [P, NE])
        e32 = sb(st, "e32", [P, NE])
        k128 = sb(st, "k128", [P, NT])
        upper = sb(st, "upper", [P, P])
        ones = sb(st, "ones", [P, P])
        zeros = sb(st, "zeros", [P, 2 * COLS])
        s1 = [sb(st, f"r_one{i}", [P, NT]) for i in range(8)]
        g4 = [sb(st, f"r_four{i}", [P, NT, EG]) for i in range(3)]
        em = sb(st, "r_em", [P, NT, NE])
        oh = [sb(st, f"r_oh{i}", [P, NT, NE]) for i in range(2)]
        picked = sb(st, "r_picked", [P, NT, NE])
        cum = sb(st, "r_cum", [P, NT, NE])
        tot = sb(st, "r_tot", [P, NT, NE])
        cnt, nb, pend, pst, act, rix, t32 = (sb(st, f"r_{n}", [P, NE]) for n in ("cnt", "nb", "pend", "pst", "act", "rix", "t32"))
        cmp17 = sb(st, "r_cmp", [P, NE, NT])
        dest = sb(st, "r_dest", [P, N2])
        bi = sb(st, "r_bi", [P, N2], I32)
        ji = sb(st, "r_ji", [P, N2], I32)
        bf = sb(st, "r_bf", [P, N2])
        jf = sb(st, "r_jf", [P, N2])
        gates = sb(st, "r_gates", [P, N2])
        ohj = sb(st, "r_ohj", [P, 2, P])
        ohb = sb(st, "r_ohb", [P, 2, 2, COLS])
        big = sb(st, "r_big", [1, COLS, NE])
        row = sb(st, "r_row", [1, COLS])
        pre = S.psum(st, "ps_pre", [P, 2, 512])
        pt = S.psum(st, "ps_tot", [P, 2, 512])
        acc = S.psum(st, "ps_slots", [P, 512])
        const_ok, ch, diff_ok, exp_ok = sem("const_ready"), sem("dve_chain4"), sem("diff_ready"), sem("exp_ready")
        one_ok, pre_mm, ohs_ok, acc_mm = sem("onehot_ready"), sem("counts_mm"), sem("slot_onehots"), sem("slots_mm")
        CUT = (0, 9, NT)
        lg = S.logits
        s4, s32 = [P, NT, EG], [P, NT, NE]

        with nc.Block() as block:
            @block.gpsimd
            def _(pool):
                c = Steps(pool, const_ok)

                def iota_f(t, pattern, base, mult):
                    c.did(pool.iota(t, pattern, base=base, channel_multiplier=mult, allow_small_or_imprecise_dtypes=True))

                iota_f(iota[:, :], [[1, P]], 0, 0)
                iota_f(tok[:, :].rearrange("p (k i) -> p k i", k=2), [[0, 2], [P, NT]], 0, 1)
                iota_f(w4[:, :], [[-1, EG]], EG, 0)
                iota_f(w32[:, :], [[-1, NE]], NE, 0)
                iota_f(e32[:, :], [[1, NE]], 0, 0)
                iota_f(k128[:, :], [[P, NT]], 0, 0)
                c.did(pool.memset(ones[:, :], 1.0))
                c.did(pool.memset(zeros[:, :], 0.0))
                c.link(pool.memset(upper[:, :], 1.0))
                c.did(pool.affine_select(out=upper[:, :], in_=upper[:, :], compare_op=ALU.is_gt, fill=0.0, base=0,
                                         pattern=[[1, P]], channel_multiplier=-1))

            @block.scalar
            def _(act_):
                act_.wait_ge(diff_ok, 1)
                act_.activation(g4[1][:, :, :], g4[0][:, :, :], ACT.Exp).then_inc(exp_ok, 1)
                act_.wait_ge(diff_ok, 2)
                act_.activation(s1[5][:, :], s1[4][:, :], ACT.Exp).then_inc(exp_ok, 1)

            @block.tensor
            def _(pe):
                pe.wait_ge(const_ok, 10)
                pe.wait_ge(one_ok, 1)
                for i in range(2):
                    w = (CUT[i + 1] - CUT[i]) * NE
                    rhs = picked[:, CUT[i]:CUT[i + 1], :].rearrange("p i e -> p (i e)")
                    pe.matmul(pre[:, i, 0:w], upper[:, :], rhs, start=True, stop=True).then_inc(pre_mm, 1)
                    pe.matmul(pt[:, i, 0:w], ones[:, :], rhs, start=True, stop=True).then_inc(pre_mm, 1)
                out = acc[:, 0:2 * COLS]
                pe.matmul(out, ones[:, :], zeros[:, :], start=True, stop=False)
                pe.sem_inc(acc_mm, 2)
                with pe.Fori(0, NT) as j:
                    for b in range(2):
                        pe.wait_ge(ohs_ok, 2 * j + b + 1)
                        pe.matmul(out, ohj[:, b, :], ohb[:, b, :, :].rearrange("p t c -> p (t c)"),
                                  start=False, stop=False).then_inc(acc_mm, 1)
                pe.matmul(out, ones[:, :], zeros[:, :], start=False, stop=True).then_inc(acc_mm, 1)

            @block.vector
            def _(dve):
                c = Steps(dve, ch)

                def tt(out, x, y, op):
                    c.link(dve.tensor_tensor(out, x, y, op))

                def ts(out, x, v1, v2, op1, op2=ALU.bypass):
                    c.link(dve.tensor_scalar(out, x, v1, v2, op1, op2) if v2 is not None
                           else dve.tensor_scalar(out, x, v1, None, op1))

                def red(out, x, op):
                    c.link(dve.tensor_reduce(out, x, AX.X, op))

                def first_max(hot, x, weights, best, shape):
                    red(best, x, ALU.max)
                    tt(hot, x, fan(best, shape), ALU.is_equal)
                    tt(hot, hot, weights.unsqueeze(1).to_broadcast(shape), ALU.mult)
                    red(s1[7][:, :], hot, ALU.max)
                    tt(hot, hot, fan(s1[7][:, :], shape), ALU.is_equal)

                gmax, gsum, gw, m1, diff, ex, m2 = (t[:, :] for t in s1[:7])
                dve.wait_ge(const_ok, 10)
                c.link(dve.memset(lg[NS:P, TP, :], 0.0))
                gl, el = lg[:, :, 0:EG], lg[:, :, EG:NR]
                ohg = g4[2][:, :, :]
                first_max(ohg, gl, w4[:, :], gmax, s4)
                dve.tensor_tensor(g4[0][:, :, :], gl, fan(gmax, s4), ALU.subtract).then_inc(diff_ok, 1)
                ts(ohg, ohg, BIG, BIG, ALU.mult, ALU.subtract)
                e4 = em[:, :, :].rearrange("p i (g e) -> p i g e", g=EG)
                tt(e4, el.rearrange("p i (g e) -> p i g e", g=EG),
                   ohg.unsqueeze(3).to_broadcast([P, NT, EG, EPG]), ALU.add)
                hot = [t[:, :, :] for t in oh]
                first_max(hot[0], em[:, :, :], w32[:, :], m1, s32)
                c.link(dve.scalar_tensor_tensor(out=em[:, :, :], in0=hot[0], scalar=-BIG, in1=em[:, :, :], op0=ALU.mult, op1=ALU.add))
                first_max(hot[1], em[:, :, :], w32[:, :], m2, s32)
                dve.tensor_tensor(diff, m2, m1, ALU.subtract).then_inc(diff_ok, 1)
                for t in oh:
                    c.link(dve.memset(t[NS:P, TP, :], 0.0))
                dve.tensor_tensor(picked[:, :, :], hot[0], hot[1], ALU.add).then_inc(one_ok, 1)
                dve.wait_ge(exp_ok, 2)
                red(gsum, g4[1][:, :, :], ALU.add)
                c.link(dve.reciprocal(gw, gsum))
                ts(m1, ex, 1.0, None, ALU.add)
                c.link(dve.reciprocal(m1, m1))
                tt(gates[:, 0:NT], gw, m1, ALU.mult)
                tt(gates[:, NT:N2], gates[:, 0:NT], ex, ALU.mult)
                for k in range(2):
                    at = k * NT + TP
                    c.did(dve.memset(gates[NS:P, at:at + 1], 0.0))
                    c.link(dve.memset(tok[NS:P, at:at + 1], 0.0))
                dve.wait_ge(pre_mm, 4)
                for i in range(2):
                    w = (CUT[i + 1] - CUT[i]) * NE
                    c.link(dve.tensor_copy(tot[:, CUT[i]:CUT[i + 1], :].rearrange("p i e -> p (i e)"), pt[:, i, 0:w]))
                c.link(dve.memset(cum[:, 0, :], 0.0))
                for i in range(1, NT):
                    tt(cum[:, i, :], cum[:, i - 1, :], tot[:, i - 1, :], ALU.add)
                tt(cnt[:, :], cum[:, TP, :], tot[:, TP, :], ALU.add)
                tt(cmp17[:, :, :], fan(cnt[:, :], [P, NE, NT]), k128[:, :].unsqueeze(1).to_broadcast([P, NE, NT]), ALU.is_gt)
                red(nb[:, :], cmp17[:, :, :], ALU.add)
                c.link(dve.tensor_tensor_scan(pend[:, :], ones[:, 0:NE], nb[:, :], 0.0, ALU.mult, ALU.add))
                tt(pst[:, :], pend[:, :], nb[:, :], ALU.subtract)
                ts(t32[:, :], pst[:, :], float(P), None, ALU.mult)
                tt(cum[:, :, :], cum[:, :, :], t32[:, :].unsqueeze(1).to_broadcast(s32), ALU.add)
                for i in range(2):
                    w = (CUT[i + 1] - CUT[i]) * NE
                    part = cum[:, CUT[i]:CUT[i + 1], :].rearrange("p i e -> p (i e)")
                    tt(part, part, pre[:, i, 0:w], ALU.add)
                for k in range(2):
                    tt(picked[:, :, :], hot[k], cum[:, :, :], ALU.mult)
                    red(dest[:, k * NT:(k + 1) * NT], picked[:, :, :], ALU.add)
                c.link(dve.tensor_copy(S.dest[:, :], dest[:, :]))
                ts(bi[:, :], S.dest[:, :], 7, None, ALU.arith_shift_right)
                ts(ji[:, :], S.dest[:, :], P - 1, None, ALU.bitwise_and)
                c.link(dve.tensor_copy(bf[:, :], bi[:, :]))
                c.link(dve.tensor_copy(jf[:, :], ji[:, :]))
                with dve.Fori(0, NT) as j:
                    for b in range(2):
                        n = 2 * j + b
                        dve.wait_ge(acc_mm, n + 1)
                        dve.tensor_scalar(ohj[:, b, :], iota[:, :], jf[:, ds(n, 1)], None, ALU.is_equal)
                        dve.tensor_scalar(ohb[:, b, 0, :], iota[:, 0:COLS], bf[:, ds(n, 1)], tok[:, ds(n, 1)],
                                          ALU.is_equal, ALU.mult)
                        dve.tensor_scalar(ohb[:, b, 1, :], iota[:, 0:COLS], bf[:, ds(n, 1)], gates[:, ds(n, 1)],
                                          ALU.is_equal, ALU.mult).then_inc(ohs_ok, 1)
                ts(act[:, :], cnt[:, :], 0.0, None, ALU.is_gt)
                c.link(dve.tensor_tensor_scan(rix[:, :], ones[:, 0:NE], act[:, :], 0.0, ALU.mult, ALU.add))
                c.link(dve.tensor_copy(S.n_blocks[:, 0:1], pend[0:1, NE - 1:NE]))
                c.link(dve.tensor_copy(S.n_blocks[:, 1:2], rix[0:1, NE - 1:NE]))
                shape = [1, COLS, NE]
                b3 = big[:, :, :]
                tt(b3, fan(iota[0:1, 0:COLS], shape), pst[0:1, :].unsqueeze(1).to_broadcast(shape), ALU.is_ge)
                tt(b3, b3, act[0:1, :].unsqueeze(1).to_broadcast(shape), ALU.mult)
                red(row[:, :], b3, ALU.add)
                ts(row[:, :], row[:, :], -1.0, None, ALU.add)
                c.link(dve.tensor_copy(S.block_run[:, :], row[:, :]))
                shape = [1, NE, NE]
                for out, by, back in ((S.run_expert, e32, 0), (S.run_free, pst, RING - 1)):
                    b3 = big[:, 0:NE, :]
                    ts(row[:, 0:NE], e32[0:1, :], float(1 - back), None, ALU.add)
                    tt(b3, fan(row[:, 0:NE], shape), rix[0:1, :].unsqueeze(1).to_broadcast(shape), ALU.is_equal)
                    tt(b3, b3, act[0:1, :].unsqueeze(1).to_broadcast(shape), ALU.mult)
                    tt(b3, b3, by[0:1, :].unsqueeze(1).to_broadcast(shape), ALU.mult)
                    red(row[:, 0:NE], b3, ALU.add)
                    c.link(dve.tensor_copy(out[:, :], row[:, 0:NE]))
                dve.wait_ge(acc_mm, 2 + N2 + 1)
                c.did(dve.tensor_copy(S.slot_tok[:, :], acc[:, 0:COLS]))
                c.link(dve.tensor_copy(S.slot_gate[:, :], acc[:, COLS:2 * COLS]))


def experts(nc, S, a):
    with ExitStack() as st:
        sb, sem = S.sb, S.sem
        UP, DOWN = KD * 2 * DE, 2 * D
        SIZE = UP + DOWN
        w = sb(st, "expert_w", [P, RING * SIZE])
        xg = sb(st, "xg", [P, 2, D])
        xT = sb(st, "xT", [P, 2, KD, P])
        idx = sb(st, "idx", [P, 2], I32)
        gcol = sb(st, "gcol", [P, 2])
        act_v = sb(st, "silu", [P, DE])
        hid = sb(st, "hid", [P, DE])
        hT = sb(st, "hidT", [P, 2, P])
        yo = sb(st, "yo", [P, 2, D])
        pX = S.psum(st, "ps_xT", [P, 2, 512])
        pU = S.psum(st, "ps_up", [P, 512])
        pT = S.psum(st, "ps_hidT", [P, 512])
        pY = S.psum(st, "ps_y", [P, 2, 512])
        ident = S.ident

        w_in = [sem(f"expert_loaded{i}") for i in range(RING)]
        g_in, y_out = [sem("gathered0"), sem("gathered1")], [sem("y_row_stored0"), sem("y_row_stored1")]
        idx_ok, x_mm, x_a, x_d, u_mm, s_ok, h_ok, t_mm, t_ok, y_mm, y_a, y_d, gc_ok = (sem(n) for n in (
            "idx_ready", "x_mm", "x_act", "x_dve", "up_mm", "silu_ok", "hid_ok", "hid_mm", "hidT_ok", "down_mm",
            "y_act", "y_dve", "gate_col"))
        tail = sem("experts_end")
        idx_seen = sem("idx_seen")
        up = a.w1[0].rearrange("e (k p) n -> e p k n", p=P)
        up3 = a.w3[0].rearrange("e (k p) n -> e p k n", p=P)
        down = a.w2[0].rearrange("e (k p) n -> e p k n", p=P)

        def blocks(eng, step):
            n = eng.value_load(S.n_blocks[0:1, 0:1], min_val=1, max_val=NBLK)
            with eng.Fori(0, NBLK // 2) as j:
                for t in (1, 2):
                    with eng.If(2 * j + t <= n):
                        step(2 * j + t, j, t)
            return n

        with nc.Block() as block:
            @block.sync
            def _(sp):
                runs = sp.value_load(S.n_blocks[0:1, 1:2], min_val=1, max_val=NE)
                with sp.Fori(0, NE // RING) as j:
                    for q in range(RING):
                        r = RING * j + q
                        with sp.If(r < runs):
                            e = sp.value_load(S.run_expert[0:1, ds(r, 1)], min_val=0, max_val=NE - 1)
                            free = sp.value_load(S.run_free[0:1, ds(r, 1)], min_val=0, max_val=NBLK)
                            sp.wait_ge(y_mm, free)
                            wb = w[:, q * SIZE:(q + 1) * SIZE]
                            w13 = wb[:, 0:UP].rearrange("p (k t n) -> p k t n", k=KD, t=2)
                            sp.dma_start(w13[:, :, 0, :], up[ds(e, 1), :, :, :].rearrange("o p k n -> p (o k) n")).then_inc(w_in[q], 16)
                            sp.dma_start(w13[:, :, 1, :], up3[ds(e, 1), :, :, :].rearrange("o p k n -> p (o k) n")).then_inc(w_in[q], 16)
                            sp.dma_start(wb[:, UP:SIZE].rearrange("p (k n) -> p k n", k=2),
                                         down[ds(e, 1), :, :, :].rearrange("o p k n -> p (o k) n")).then_inc(w_in[q], 16)

            @block.gpsimd
            def _(pool):
                def gather(b, par):
                    pool.tensor_copy(idx[:, par:par + 1], S.slot_tok[:, ds(b, 1)]).then_inc(idx_ok, 1)
                    pool.wait_ge(idx_ok, b + 1)
                    pool.sem_inc(idx_seen, 1)
                    pool.indirect_dma_start(out=xg[:, par, :], out_offset=None, in_=S.h2_d,
                                            in_offset=bass.IndirectOffsetOnAxis(ap=idx[:, par:par + 1], axis=0)).then_inc(g_in[par], 16)

                def step(b, j, t):
                    pool.wait_ge(x_mm, b + 1)
                    gather(b + 2, t % 2)

                gather(0, 0)
                gather(1, 1)
                pool.wait_ge(x_mm, 1)
                gather(2, 0)
                blocks(pool, step)

            @block.tensor
            def _(pe):
                def turn_x(b, n, par):
                    pe.wait_ge(g_in[par], 16 * n + 16)
                    pe.wait_ge(x_a, b)
                    pe.wait_ge(x_d, b)
                    for k in range(KD):
                        last = pe.transpose(pX[:, k // 4, k % 4 * P:(k % 4 + 1) * P], xg[:, par, k * P:(k + 1) * P], ident[:, :])
                    last.then_inc(x_mm, 1)

                def run_of(b):
                    return pe.value_load(S.block_run[0:1, ds(b, 1)], min_val=0, max_val=NE - 1)

                def at(run):
                    return (run % RING) * SIZE

                def up_mm(b, par, run):
                    for q in range(RING):
                        pe.wait_ge(w_in[q], 48 * ((run + (RING - q)) // RING))
                    pe.wait_ge(x_a, b + 1)
                    pe.wait_ge(x_d, b + 1)
                    pe.wait_ge(h_ok, b)
                    base = pe.snap(at(run))
                    for k in range(KD):
                        last = pe.matmul(pU[:, :], xT[:, par, k, :], w[:, ds(base + k * 2 * DE, 2 * DE)],
                                         start=k == 0, stop=k == KD - 1)
                    last.then_inc(u_mm, 1)

                def down_mm(b, run):
                    pe.wait_ge(t_ok, b + 1)
                    pe.wait_ge(y_a, b)
                    pe.wait_ge(y_d, b)
                    base = pe.snap(at(run))
                    for c in range(2):
                        for k in range(2):
                            last = pe.matmul(pY[:, c, :], hT[:, k, :], w[:, ds(base + (UP + k * D + c * 512), 512)],
                                             start=k == 0, stop=k == 1)
                    last.then_inc(y_mm, 1)

                def turn_hid(b):
                    pe.wait_ge(h_ok, b + 1)
                    pe.wait_ge(t_ok, b)
                    for k in range(2):
                        last = pe.transpose(pT[:, k * P:(k + 1) * P], hid[:, k * P:(k + 1) * P], ident[:, :])
                    last.then_inc(t_mm, 1)

                def step(b, j, t):
                    turn_x(b + 1, j + (t + 1) // 2, (t + 1) % 2)
                    up_mm(b, t % 2, run_of(b))
                    down_mm(b - 1, run_of(b - 1))
                    turn_hid(b)

                turn_x(0, 0, 0)
                turn_x(1, 0, 1)
                up_mm(0, 0, run_of(0))
                turn_hid(0)
                blocks(pe, step)

            @block.scalar
            def _(act):
                def evac_x(b, par):
                    act.wait_ge(x_mm, b + 1)
                    act.activation(xT[:, par, 0:4, :], pX[:, 0, :].rearrange("p (k t) -> p k t", k=4), ACT.Copy).then_inc(x_a, 1)

                def silu(b):
                    act.wait_ge(u_mm, b + 1)
                    act.activation(act_v[:, :], pU[:, 0:DE], ACT.Silu).then_inc(s_ok, 1)

                def out(b, n, par):
                    act.wait_ge(y_mm, b + 1)
                    act.wait_ge(gc_ok, b + 1)
                    act.wait_ge(y_out[par], 16 * n)
                    act.activation(yo[:, par, 0:512], pY[:, 0, :], ACT.Copy, scale=gcol[:, par:par + 1]).then_inc(y_a, 1)
                    act.wait_ge(y_a, b + 1)
                    act.wait_ge(y_d, b + 1)
                    act.dma_start(S.yb_d[ds(b * P, P), :], yo[:, par, :]).then_inc(y_out[par], 16)

                def step(b, j, t):
                    evac_x(b + 1, (t + 1) % 2)
                    silu(b)
                    out(b - 1, j, (t + 1) % 2)

                evac_x(0, 0)
                evac_x(1, 1)
                silu(0)
                n = blocks(act, step)
                act.wait_ge(y_out[0], 16 * ((n + 1) // 2))
                act.sem_inc(tail, 1)
                act.wait_ge(y_out[1], 16 * (n // 2))
                act.sem_inc(tail, 1)

            @block.vector
            def _(dve):
                def evac_x(b, par):
                    dve.wait_ge(x_mm, b + 1)
                    dve.tensor_copy(xT[:, par, 4:8, :], pX[:, 1, :].rearrange("p (k t) -> p k t", k=4)).then_inc(x_d, 1)

                def hidden(b):
                    dve.wait_ge(s_ok, b + 1)
                    dve.tensor_tensor(hid[:, :], act_v[:, :], pU[:, DE:2 * DE], ALU.mult).then_inc(h_ok, 1)

                def evac_hid(b):
                    dve.wait_ge(t_mm, b + 1)
                    dve.tensor_copy(hT[:, :, :], pT[:, 0:2 * P].rearrange("p (k t) -> p k t", k=2)).then_inc(t_ok, 1)

                def out(b, n, par):
                    dve.wait_ge(gc_ok, b + 1)
                    dve.wait_ge(y_mm, b + 1)
                    dve.wait_ge(y_out[par], 16 * n)
                    dve.tensor_scalar(yo[:, par, 512:D], pY[:, 1, :], gcol[:, par:par + 1], None, ALU.mult).then_inc(y_d, 1)

                def step(b, j, t):
                    prev = (t + 1) % 2
                    dve.tensor_copy(gcol[:, prev:prev + 1], S.slot_gate[:, ds(b - 1, 1)]).then_inc(gc_ok, 1)
                    evac_x(b + 1, prev)
                    hidden(b)
                    out(b - 1, j, prev)
                    evac_hid(b)

                evac_x(0, 0)
                evac_x(1, 1)
                hidden(0)
                evac_hid(0)
                blocks(dve, step)


def final(nc, S, a, o):
    with ExitStack() as st:
        sb, sem = S.sb, S.sem
        NB = 4
        gate = sb(st, "gate2", [P, D])
        gf = sb(st, "gf", [P, D])
        yg = sb(st, "yg", [P, NB, 2, D])
        idx = sb(st, "idx2", [P, NB, 2], I32)
        x3 = sb(st, "x3", [P, NB, D])
        junk = sb(st, "junk4", [P, D])
        out = sb(st, "out_rows", [P, NB, D])
        ssq = sb(st, "ssq3", [P, NB])
        rstd = sb(st, "rstd3", [P, 1])
        newton = sb(st, "newton3", [P, 2])
        mod_in, mod_s, idx_ok, mul_ok, x_ok, sq_ok, o_ok, ch = (sem(n) for n in (
            "mod3_loaded", "mod3_sample_loaded", "idx2_ready", "rows_gated", "x3_ready", "ssq3_ready",
            "out_ready", "dve_chain5"))
        s1_ok, idx_seen = sem("rows_added"), sem("idx2_seen")
        x_in, y_in, o_out = ([sem(f"{n}{i}") for i in range(NB)] for n in ("x2_loaded", "rows_gathered", "out_stored"))

        def rows_of(i):
            return NS if isinstance(i, int) and i == TP else P

        def tiles(eng, step, at=None):
            for i in range(NB):
                step(i, 0, i)
            with eng.Fori(1, TP // NB - 1) as j:
                if at is not None:
                    at(NB * j)
                for b in range(NB):
                    step(NB * j + b, j, b)
            if at is not None:
                at(TP - NB)
            for i in range(TP - NB, NT):
                step(i, i // NB, i % NB)

        with nc.Block() as block:
            @block.sync
            def _(sp):
                def load(i, b):
                    rows = S.x2_d[TP * P:TOK, :] if rows_of(i) == NS else S.x2_d[ds(i * P, P), :]
                    sp.dma_start(x3[0:rows_of(i), b, :], rows).then_inc(x_in[b], 16)

                load(0, 0)
                sp.dma_start(gate[:, :], S.ada_d[0:1, 5 * D:6 * D].to_broadcast([P, D])).then_inc(mod_in, 16)
                sp.dma_start(gf[:, :], a.g_final.to_broadcast([P, D])).then_inc(mod_in, 16)
                for i in range(1, NB):
                    load(i, i)

                def step(i, n, b):
                    if isinstance(i, int) and i == TP - 1:
                        sp.wait_ge(mul_ok, TP)
                        for q in range(NSEQ):
                            sp.dma_start(gate[q * DSEQ:(q + 1) * DSEQ, :],
                                         S.ada_d[1 + q:2 + q, 5 * D:6 * D].to_broadcast([DSEQ, D])).then_inc(mod_s, 16)
                    sp.wait_ge(o_ok, i + 1)
                    if rows_of(i) == NS:
                        sp.dma_start(o.y_sample.rearrange("b t d -> (b t) d"), out[0:NS, b, :]).then_inc(o_out[b], 16)
                    else:
                        sp.dma_start(o.y_prompt[0, ds(i * P, P), :], out[:, b, :]).then_inc(o_out[b], 16)
                    if not isinstance(i, int) or i + NB < NT:
                        load(i + NB, b)

                tiles(sp, step)
                for b in range(NB):
                    sp.wait_ge(o_out[b], 16 * ((NT - 1 - b) // NB + 1))

            @block.gpsimd
            def _(pool):
                def gather(i, b):
                    r = rows_of(i)
                    for k in range(2):
                        pool.tensor_copy(idx[0:r, b, k:k + 1], S.dest[0:r, ds(i + k * NT, 1)]).then_inc(idx_ok, 1)
                    pool.wait_ge(idx_ok, 2 * i + 2)
                    pool.sem_inc(idx_seen, 1)
                    for k in range(2):
                        pool.indirect_dma_start(out=yg[0:r, b, k, :], out_offset=None, in_=S.yb_d,
                                                in_offset=bass.IndirectOffsetOnAxis(ap=idx[0:r, b, k:k + 1], axis=0)).then_inc(y_in[b], 16)

                def step(i, n, b):
                    r = rows_of(i)
                    if not isinstance(i, int) or i + NB - 1 < NT:
                        if not (isinstance(i, int) and i == 0):
                            pool.wait_ge(x_ok, i)
                        gather(i + NB - 1, (b + NB - 1) % NB)
                    pool.wait_ge(mul_ok, i + 1)
                    pool.wait_ge(x_in[b], 16 * n + 16)
                    pool.tensor_tensor(x3[0:r, b, :], x3[0:r, b, :], yg[0:r, b, 0, :], ALU.add).then_inc(x_ok, 1)

                for i in range(NB - 1):
                    gather(i, i)
                tiles(pool, step)

            @block.scalar
            def _(act):
                def step(i, n, b):
                    r = rows_of(i)
                    act.wait_ge(sq_ok, i)
                    act.wait_ge(x_ok, i + 1)
                    act.activation(junk[0:r, :], x3[0:r, b, :], ACT.Square, accum_out=ssq[0:r, b:b + 1]).then_inc(sq_ok, 1)

                tiles(act, step)

            @block.vector
            def _(dve):
                c = Steps(dve, ch)

                def rows_in(i, n, b):
                    r = rows_of(i)
                    if isinstance(i, int) and i == TP:
                        dve.wait_ge(mod_s, 16 * NSEQ)
                    dve.wait_ge(y_in[b], 32 * n + 32)
                    y0, y1 = yg[0:r, b, 0, :], yg[0:r, b, 1, :]
                    dve.tensor_tensor(y1, y0, y1, ALU.add).then_inc(s1_ok, 1)
                    dve.wait_ge(s1_ok, i + 1)
                    dve.tensor_tensor(y0, y1, gate[0:r, :], ALU.mult).then_inc(mul_ok, 1)

                def norm(i, n, b):
                    r = rows_of(i)
                    dve.wait_ge(sq_ok, i + 1)
                    inv_sqrt(dve, c, rstd[0:r, :], ssq[0:r, b:b + 1], 1.0 / D, newton[0:r, 0:1], newton[0:r, 1:2])
                    if not (isinstance(n, int) and n == 0):
                        dve.wait_ge(o_out[b], 16 * n)
                    dve.scalar_tensor_tensor(out=out[0:r, b, :], in0=x3[0:r, b, :], scalar=rstd[0:r, :], in1=gf[0:r, :],
                                             op0=ALU.mult, op1=ALU.mult).then_inc(o_ok, 1)

                def step(i, n, b):
                    if not (isinstance(i, int) and i == TP):
                        rows_in(i + 1, n + (b + 1) // NB, (b + 1) % NB)
                    norm(i, n, b)

                dve.wait_ge(mod_in, 32)
                rows_in(0, 0, 0)
                tiles(dve, step, lambda i: c.at(INV * i))


_INS = ['x_prompt', 'x_sample', 'state_ssm_re', 'state_ssm_im', 'c_prompt', 'c_sample', 'w_ada', 'b_ada',
        'g_norm1', 'g_norm2', 'w_in', 'ln_g', 'ln_b', 'w_s', 'b_s', 'lam_re', 'lam_im', 'log_dt',
        'ssm_b_re', 'ssm_b_im', 'ssm_c_re', 'ssm_c_im', 'ssm_d', 'w_glu', 'b_glu', 'w_out',
        'w_group', 'b_group', 'w_expert', 'b_expert', 'w1', 'w3', 'w2', 'g_final']
_OUTS = [('y_prompt', (1, SEQ, D)), ('y_sample', (NSEQ, DSEQ, D)),
         ('ssm_re_prompt', (1, 1, G, ST)), ('ssm_im_prompt', (1, 1, G, ST)),
         ('ssm_re_sample', (1, NSEQ, G, ST)), ('ssm_im_sample', (1, NSEQ, G, ST)),
         ('v_sample', (1, NSEQ, DSEQ, DA))]


def kernel(**inputs):
    import concourse.bacc as _bacc
    from concourse.bass_utils import run_bass_kernel_spmd as _run

    nc = _bacc.Bacc("TRN2", target_bir_lowering=False, num_devices=1)
    arrays, ins, outs = {}, {}, {}
    for name in _INS:
        x = np.ascontiguousarray(inputs[name])
        if x.ndim == 1:
            x = x.reshape(1, -1)
        arrays[f"in_{name}"] = x
        ins[name] = nc.dram_tensor(f"in_{name}", x.shape, mybir.dt.from_np(x.dtype), kind="ExternalInput").ap()
    for name, shape in _OUTS:
        outs[name] = nc.dram_tensor(f"out_{name}", shape, F32, kind="ExternalOutput").ap()
    build(nc, Inputs(ins), Outputs(outs))
    r = _run(nc, [arrays], core_ids=[0])
    return tuple(r.results[0][f"out_{name}"] for name, _ in _OUTS)
```

```python
from contextlib import ExitStack

import numpy as np
import concourse.bass as bass
from concourse import mybir

F32 = mybir.dt.float32
F32R = mybir.dt.float32r
I32 = mybir.dt.int32
U32 = mybir.dt.uint32
ACT = mybir.ActivationFunctionType
ALU = mybir.AluOpType
AX = mybir.AxisListType
ds = bass.ds

P = 128
D = 1024
KD = D // P
SEQ = 2048
NSEQ = 8
DSEQ = 8
TP = SEQ // P
NS = NSEQ * DSEQ
NT = TP + 1
TOK = SEQ + NS
DA = 512
HEADS = 4
HD = 128
G = 32
GC = 16
ST = 64
PAIRS = G // 2
Q = 8
NCH = SEQ // Q
CH = NCH + NSEQ
EG = 4
EPG = 8
NE = EG * EPG
DE = 256
NR = EG + NE
NBLK = TOK * 2 // P + NE - 1
FULL = TOK * 2 // P
EPS = 1e-6
BIG = 1e30
TWO_PI = 2 * np.pi
MAGIC = 1.5 * 2 ** 23
PI_HI = float(np.float32(6.28125))
PI_MID = float(np.float32(np.float64(TWO_PI) - 6.28125))
PI_LO = float(TWO_PI - 6.28125 - PI_MID)


class Inputs:

    def __init__(self, t):
        self.x_prompt = t["x_prompt"]
        self.x_sample = t["x_sample"]
        self.state_ssm_re = t["state_ssm_re"]
        self.state_ssm_im = t["state_ssm_im"]
        self.c_prompt = t["c_prompt"]
        self.c_sample = t["c_sample"]
        self.w_ada = t["w_ada"]
        self.b_ada = t["b_ada"]
        self.g_norm1 = t["g_norm1"]
        self.g_norm2 = t["g_norm2"]
        self.w_in = t["w_in"]
        self.ln_g = t["ln_g"]
        self.ln_b = t["ln_b"]
        self.w_s = t["w_s"]
        self.b_s = t["b_s"]
        self.lam_re = t["lam_re"]
        self.lam_im = t["lam_im"]
        self.log_dt = t["log_dt"]
        self.ssm_b_re = t["ssm_b_re"]
        self.ssm_b_im = t["ssm_b_im"]
        self.ssm_c_re = t["ssm_c_re"]
        self.ssm_c_im = t["ssm_c_im"]
        self.ssm_d = t["ssm_d"]
        self.w_glu = t["w_glu"]
        self.b_glu = t["b_glu"]
        self.w_out = t["w_out"]
        self.w_group = t["w_group"]
        self.b_group = t["b_group"]
        self.w_expert = t["w_expert"]
        self.b_expert = t["b_expert"]
        self.w1 = t["w1"]
        self.w3 = t["w3"]
        self.w2 = t["w2"]
        self.g_final = t["g_final"]


class Outputs:

    def __init__(self, t):
        self.y_prompt = t["y_prompt"]
        self.y_sample = t["y_sample"]
        self.ssm_re_prompt = t["ssm_re_prompt"]
        self.ssm_im_prompt = t["ssm_im_prompt"]
        self.ssm_re_sample = t["ssm_re_sample"]
        self.ssm_im_sample = t["ssm_im_sample"]
        self.v_sample = t["v_sample"]


class Shared:

    def __init__(self, sb, psum, sem):
        self.sb, self.psum, self.sem = sb, psum, sem


class Steps:

    def __init__(self, eng, sem, done=0):
        self.eng, self.sem, self.done, self.count = eng, sem, done, 0

    def did(self, ins):
        ins.then_inc(self.sem, 1)
        self.done = self.done + 1
        self.count += 1

    def link(self, ins):
        self.did(ins)
        self.eng.wait_ge(self.sem, self.done)

    def at(self, done):
        self.done = done

    def sync(self):
        self.eng.wait_ge(self.sem, self.done)


def fan(ap, shape):
    return ap.unsqueeze(len(shape) - 1).to_broadcast(shape)


def build(nc, a, o):
    ctx = ExitStack()
    with ctx:
        ctx.enter_context(nc.allow_non_contiguous_dma(reason="small parameter loads"))

        def sb(stack, name, shape, dt=F32):
            return stack.enter_context(nc.sbuf_tensor(name, shape, dt))

        def psum(stack, name, shape):
            return stack.enter_context(nc.psum_tensor(name, shape, F32))

        def sem(name):
            t = names.enter_context(nc.semaphore(name))
            used.append(t)
            return t

        def dram(name, shape):
            return nc.dram_tensor(name, shape, F32, kind="Internal").ap()

        S = Shared(sb, psum, sem)
        S.ada_d = dram("ada_rows", (9, 6 * D))
        S.kpad_d = dram("toeplitz_rows", (GC, G, 2 * P))
        S.a_d = dram("gmlp_rows", (TOK, DA))
        S.s_d = dram("s5_in_rows", (TOK, DA))
        S.y_d = dram("s5_out_rows", (TOK, DA))
        S.h2_d = dram("moe_in_rows", (TOK, D))
        S.x2_d = dram("x2_rows", (TOK, D))
        S.rot_d = dram("rotations", (P, PAIRS, 2, NCH))
        S.yb_d = dram("expert_rows", (NBLK * P, D))
        S.ident = sb(ctx, "ident", [P, P])
        names, used = ExitStack(), []
        with ExitStack() as early:
            tables(S, early)
            setup(nc, S, a)
            mixin(nc, S, a, o)
            spent, names = names, ExitStack()
            S.spent = range(used[0].num, used[-1].num + 1)
            assert [t.num for t in used] == list(S.spent)
            s5(nc, S, a, o)
        spent.close()
        S.logits = sb(ctx, "logits", [P, NT, NR])
        mixout(nc, S, a)
        S.dest = sb(ctx, "dest", [P, NT * 2], I32)
        S.slot_tok = sb(ctx, "slot_tok", [P, COLS], I32)
        S.slot_gate = sb(ctx, "slot_gate", [P, COLS])
        S.n_blocks = sb(ctx, "n_blocks", [1, 2], I32)
        S.block_run = sb(ctx, "block_run", [1, COLS], I32)
        S.run_expert = sb(ctx, "run_expert", [1, NE], I32)
        S.block_split = sb(ctx, "block_split", [1, COLS], I32)
        S.block_next = sb(ctx, "block_next", [1, COLS], I32)
        S.raw = sb(ctx, "expert_raw", [P, 2, 3, KD * DE])
        S.w_in = [[sem(f"w{t}_loaded{q}") for q in range(2)] for t in ("1", "3", "2")]
        route(nc, S, a)
        experts(nc, S, a)
        final(nc, S, a, o)
        names.close()


def tables(S, stack):
    sb = S.sb
    S.m_re = sb(stack, "m_re", [P, PAIRS, 9, GC])
    S.m_im = sb(stack, "m_im", [P, PAIRS, 9, GC])
    S.wx = sb(stack, "wx", [P, PAIRS, 2, P])
    S.decay = sb(stack, "decay", [P, PAIRS])
    S.a8_re = sb(stack, "a8_re", [P, PAIRS])
    S.a8_im = sb(stack, "a8_im", [P, PAIRS])
    S.na8_im = sb(stack, "na8_im", [P, PAIRS])
    S.ws = sb(stack, "ws", [P, HEADS, P])
    S.ws_samp = sb(stack, "ws_samp", [NS, HEADS, NS])
    S.bs = sb(stack, "bs", [P, HEADS])
    S.bs_samp = sb(stack, "bs_samp", [NS, HEADS])


def setup(nc, S, a):
    with ExitStack() as st:
        sb, sem = S.sb, S.sem
        NW = 12
        WB = 2
        c9 = sb(st, "c9", [9, D])
        sc9 = c9
        rows = sb(st, "rows", [9, 6 * D])
        cT = sb(st, "cT", [P, KD, 9])
        wada = sb(st, "wada", [P, WB, KD, 512])
        ada = sb(st, "ada_part", [9, WB, 512])
        g12 = sb(st, "g12", [9, 2, D])
        lam = sb(st, "lam", [PAIRS, 2, P])
        lr = sb(st, "lr", [P, PAIRS])
        li = sb(st, "li", [P, PAIRS])
        dt = sb(st, "dt", [P, PAIRS])
        tmp = [sb(st, f"tmp{i}", [P, PAIRS]) for i in range(8)]
        pw_re = sb(st, "pw_re", [P, PAIRS, 9])
        pw_im = sb(st, "pw_im", [P, PAIRS, 9])
        pr_re = sb(st, "pr_re", [P, PAIRS, Q])
        pr_im = sb(st, "pr_im", [P, PAIRS, Q])
        b_in = sb(st, "b_in", [P, 2, PAIRS, GC])
        bb = sb(st, "bb", [P, 2, PAIRS, GC])
        c_in = sb(st, "c_in", [P, 2, 2, P])
        cc = sb(st, "cc", [P, 2, PAIRS, GC])
        big1 = sb(st, "big1", [P, PAIRS, 9, GC])
        big2 = sb(st, "big2", [P, PAIRS, 9, GC])
        zero = sb(st, "zero", [GC, P])
        dd = sb(st, "dd", [GC, G])
        dtmp = sb(st, "dtmp", [GC, G, GC])
        ada_used = sem("ada_part_used")
        powers_ok, pool_m = sem("powers_ready"), sem("pool_m")
        lam_in, ssm_c_in = sem("lam_loaded"), sem("ssm_c_loaded")
        rot_ok, rot_out = sem("rot_ready"), sem("rot_stored")
        ws_in = sb(st, "ws_in", [P, HEADS, P])
        vk = sb(st, "vk", [P, G, P])
        v = [vk[:, 0:PAIRS, :].rearrange("p a (s h) -> p a s h", s=Q),
             vk[:, PAIRS:G, :].rearrange("p a (s h) -> p a s h", s=Q)]
        rot = sb(st, "rot_all", [P, PAIRS, 2, NCH])
        k0 = vk[0:GC, :, :]
        pm = S.psum(st, "ps_misc", [P, 4, 512])
        pa = S.psum(st, "ps_ada", [P, WB, 512])
        ident = S.ident

        id_steps, z_k0, z_ws = sem("id_steps"), sem("z_k0"), sem("z_ws")
        c_in_s, small, w_s, bada_s = sem("c_loaded"), sem("small_loaded"), [sem(f"wada_loaded{i}") for i in range(WB)], sem("bada_loaded")
        ws_cp, ws_mask, ws_blk = sem("ws_copied"), sem("ws_masked"), sem("ws_blocks")
        ada_free = sem("ada_bank_free")
        act_s, pe_s, dve_s, ada_mm, rows_ok, rows_out = (sem("setup_act"), sem("setup_pe"), sem("setup_dve"), sem("ada_mm"), sem("ada_rows_ready"), sem("ada_rows_stored"))
        k_ok, k_out, chan = sem("k0_ready"), sem("k0_stored"), sem("dve_chain")
        w_view = a.w_ada[0].rearrange("(k p) n -> p k n", p=P)

        with nc.Block() as block:
            @block.sync
            def _(sp):
                def load_ada(n):
                    sp.dma_start(wada[:, n % WB, :, :], w_view[:, :, n * 512:(n + 1) * 512]).then_inc(w_s[n % WB], 16)

                sp.dma_start(c9[0:1, :], a.c_prompt).then_inc(c_in_s, 16)
                sp.dma_start(c9[1:9, :], a.c_sample).then_inc(c_in_s, 16)
                sp.dma_start(lam[:, 0, :], a.lam_re[0].rearrange("(a g) p -> a (g p)", g=2)).then_inc(lam_in, 16)
                sp.dma_start(lam[:, 1, :], a.lam_im[0].rearrange("(a g) p -> a (g p)", g=2)).then_inc(lam_in, 16)
                ldt = a.log_dt[0:1, :].rearrange("o (a g) -> o g a", g=2)
                for g in range(2):
                    sp.dma_start(dt[g * ST:(g + 1) * ST, :], ldt[:, g, :].to_broadcast([ST, PAIRS])).then_inc(lam_in, 16)
                for n in range(WB):
                    load_ada(n)
                for i, t in enumerate((a.ssm_b_re, a.ssm_b_im)):
                    sp.dma_start(b_in[:, i, :, :], t[0].rearrange("(a g) p h -> (g p) a h", g=2)).then_inc(small, 16)
                sp.dma_start(dd[:, :], a.ssm_d[0].rearrange("g h -> h g")).then_inc(small, 16)
                sp.dma_start(ws_in[:, :, :], a.w_s[0].rearrange("h t s -> t h s")).then_inc(small, 16)
                sp.dma_start(S.bs[:, :], a.b_s[0].rearrange("h t -> t h")).then_inc(small, 16)
                for q in range(NSEQ):
                    sp.dma_start(S.bs_samp[q * DSEQ:(q + 1) * DSEQ, :],
                                 a.b_s[0].rearrange("h t -> t h")[0:DSEQ, :]).then_inc(small, 16)
                sp.dma_start(rows[:, :], a.b_ada.to_broadcast([9, 6 * D])).then_inc(bada_s, 16)
                sp.dma_start(g12[:, 0, :], a.g_norm1.to_broadcast([9, D])).then_inc(bada_s, 16)
                sp.dma_start(g12[:, 1, :], a.g_norm2.to_broadcast([9, D])).then_inc(bada_s, 16)
                for n in range(WB, NW):
                    sp.wait_ge(ada_mm, n - WB + 1)
                    load_ada(n)
                sp.wait_ge(ws_mask, 1)
                sp.wait_ge(z_ws, 1)
                for q in range(NSEQ):
                    r = slice(q * DSEQ, (q + 1) * DSEQ)
                    sp.dma_start(S.ws_samp[r, :, r], S.ws[0:DSEQ, :, 0:DSEQ]).then_inc(ws_blk, 16)
                sp.wait_ge(rot_ok, 1)
                sp.dma_start(S.rot_d, rot[:, :, :, :]).then_inc(rot_out, 16)
                sp.wait_ge(k_ok, 1)
                sp.wait_ge(z_k0, 1)
                sp.dma_start(S.kpad_d[:, :, 0:P], zero[:, :].unsqueeze(1).to_broadcast([GC, G, P])).then_inc(k_out, 16)
                sp.dma_start(S.kpad_d[:, :, P:2 * P], k0).then_inc(k_out, 16)
                sp.wait_ge(rows_ok, NW + 8)
                sp.dma_start(S.ada_d, rows[:, :]).then_inc(rows_out, 16)
                sp.wait_ge(ws_blk, 16 * NSEQ)
                sp.wait_ge(k_out, 32)
                sp.wait_ge(rot_out, 16)
                sp.wait_ge(rows_out, 16)

            @block.gpsimd
            def _(pool):
                ids = Steps(pool, id_steps)
                ids.link(pool.memset(ident[:, :], 0.0))
                ids.did(pool.affine_select(out=ident[:, :], in_=ident[:, :], compare_op=ALU.not_equal, fill=1.0,
                                           base=0, pattern=[[-1, P]], channel_multiplier=1))
                pool.memset(zero[:, :], 0.0).then_inc(z_k0, 1)
                pool.memset(S.ws_samp[:, :, :], 0.0).then_inc(z_ws, 1)
                pool.wait_ge(ws_cp, 1)
                pool.affine_select(out=S.ws[:, :, :], in_=S.ws[:, :, :], compare_op=ALU.is_ge, fill=0.0, base=0,
                                   pattern=[[0, HEADS], [1, P]], channel_multiplier=-1).then_inc(ws_mask, 1)
                s9 = [P, PAIRS, 9, GC]
                im = Steps(pool, pool_m)
                m_im, t9 = S.m_im[:, :, :, :], big2[:, :, :, :]

                def imag_step(n):
                    if n == 1:
                        pool.wait_ge(powers_ok, 1)
                        pool.wait_ge(act_s, 8)
                        im.did(pool.tensor_tensor(m_im, fan(pw_im[:, :, :], s9), cc[:, 0, :, :].unsqueeze(2).to_broadcast(s9), ALU.mult))
                    if n == 2:
                        im.link(pool.tensor_tensor(t9, fan(pw_re[:, :, :], s9), cc[:, 1, :, :].unsqueeze(2).to_broadcast(s9), ALU.mult))
                    if n == 3:
                        im.link(pool.tensor_tensor(m_im, m_im, t9, ALU.add))
                    if n == 4:
                        im.did(pool.tensor_scalar(m_im, m_im, -1.0, None, ALU.mult))

                pool.wait_ge(bada_s, 48)
                rk = Steps(pool, rows_ok)
                pool.sem_inc(ada_used, WB)
                for n in range(NW):
                    part = rows[:, n * 512:(n + 1) * 512]
                    pool.wait_ge(ada_free, WB + n + 1)
                    rk.link(pool.tensor_tensor(part, part, ada[:, n % WB, :], ALU.add))
                    pool.sem_inc(ada_used, 1)
                    if n // 2 in (1, 4):
                        rk.link(pool.tensor_scalar(part, part, 1.0, None, ALU.add))
                        rk.did(pool.tensor_tensor(part, part, g12[:, n // 6, n % 2 * 512:(n % 2 + 1) * 512], ALU.mult))
                    imag_step(n)

            @block.scalar
            def _(act):
                act.wait_ge(c_in_s, 32)
                st_ = Steps(act, act_s)
                st_.did(act.activation(sc9[:, :], c9[:, :], ACT.Silu))
                act.wait_ge(lam_in, 64)
                st_.link(act.activation(tmp[7][:, :], dt[:, :], ACT.Exp))
                act.wait_ge(dve_s, 2)
                st_.did(act.activation(tmp[2][:, :], tmp[0][:, :], ACT.Exp))
                st_.did(act.activation(S.decay[:, :], tmp[0][:, :], ACT.Exp, scale=float(Q)))
                st_.did(act.activation(tmp[3][:, :], tmp[1][:, :], ACT.Sin))
                st_.did(act.activation(tmp[4][:, :], tmp[1][:, :], ACT.Sin, scale=0.5))
                for i, t in enumerate((a.ssm_c_re, a.ssm_c_im)):
                    cv = t[0].rearrange("(b a g) o p -> b a o g p", b=2, g=2)
                    for h in range(2):
                        for q in range(8):
                            act.dma_start(c_in[q * GC:(q + 1) * GC, i, h, :].rearrange("o (g p) -> o g p", g=2),
                                          cv[h, q, :, :, :]).then_inc(ssm_c_in, 16)
                for i in range(2):
                    act.wait_ge(pe_s, 3 + i)
                    st_.did(act.activation(cc[:, i, :, :].rearrange("p a o -> p (a o)"), pm[:, i, 256:512], ACT.Copy))
                act.wait_ge(pe_s, 5)
                act.activation(S.ws[:, :, :].rearrange("p h t -> p (h t)"), pm[:, 2, :], ACT.Copy).then_inc(ws_cp, 1)
                act.sem_inc(ada_free, WB)

                def evac_ada(j):
                    for b in range(WB):
                        act.wait_ge(ada_mm, WB * j + b + 1)
                        act.wait_ge(ada_used, WB * j + b + 1)
                        act.activation(ada[:, b, :], pa[0:9, b, :], ACT.Copy).then_inc(ada_free, 1)

                with act.Fori(0, 4) as j:
                    evac_ada(j)
                for n in range(8):
                    act.wait_ge(pe_s, 6 + n)
                    st_.did(act.activation(
                        S.wx[:, 2 * n:2 * n + 2, :, :].rearrange("p a r s -> p (a r s)"), pm[:, n % 2, :], ACT.Copy))
                for n in range(8):
                    act.wait_ge(pe_s, 14 + n)
                    st_.did(act.activation(k0[:, 8 * (n // 2) + n % 2:8 * (n // 2) + 8:2, :],
                                           pm[0:GC, 2 + n % 2, :].rearrange("h (g k) -> h g k", g=4), ACT.Copy))
                with act.Fori(4, NW // WB) as j:
                    evac_ada(j)

            @block.tensor
            def _(pe):
                ps = Steps(pe, pe_s)
                pe.wait_ge(id_steps, 2)
                pe.wait_ge(act_s, 1)
                for k in range(KD):
                    last = pe.transpose(pm[:, 0, k * 9:(k + 1) * 9], sc9[:, k * P:(k + 1) * P], ident[0:9, 0:9])
                ps.did(last)
                pe.wait_ge(lam_in, 64)
                pe.transpose(pm[:, 1, 0:PAIRS], lam[:, 0, :], ident[0:PAIRS, 0:PAIRS])
                ps.did(pe.transpose(pm[:, 1, PAIRS:2 * PAIRS], lam[:, 1, :], ident[0:PAIRS, 0:PAIRS]))
                pe.wait_ge(chan, 3)

                def ada_chunk(j, b):
                    pe.wait_ge(w_s[b], 16 * j + 16)
                    if not isinstance(j, int):
                        pe.wait_ge(ada_free, WB * j + b + 1)
                    for k in range(KD):
                        last = pe.matmul(pa[0:9, b, :], cT[:, k, :], wada[:, b, k, :], start=k == 0, stop=k == KD - 1)
                    last.then_inc(ada_mm, 1)

                def ada_chunks(first, end):
                    with pe.Fori(first, end) as j:
                        for b in range(WB):
                            ada_chunk(j, b)

                for b in range(WB):
                    ada_chunk(0, b)
                pe.wait_ge(ssm_c_in, 16 * 32)
                for i in range(2):
                    for h in range(2):
                        last = pe.transpose(pm[:, i, 256 + h * P:256 + (h + 1) * P], c_in[:, i, h, :], ident[:, :])
                    ps.did(last)
                pe.wait_ge(small, 16 * N_SMALL)
                for h in range(HEADS):
                    last = pe.transpose(pm[:, 2, h * P:(h + 1) * P], ws_in[:, h, :], ident[:, :])
                ps.did(last)
                ada_chunks(1, 4)
                for n in range(8):
                    if n == 0:
                        pe.wait_ge(dve_s, 4)
                        pe.wait_ge(act_s, 8)
                    if n >= 2:
                        pe.wait_ge(act_s, 9 + n - 2)
                    for q in range(4):
                        last = pe.transpose(pm[:, n % 2, q * P:(q + 1) * P],
                                            v[q % 2][:, 2 * n + q // 2, :, :].rearrange("p s h -> p (s h)"), ident[:, :])
                    ps.did(last)
                pe.wait_ge(dve_s, 5)
                pe.wait_ge(pool_m, 4)
                for n in range(8):
                    if n >= 2:
                        pe.wait_ge(act_s, 15 + n)
                    for q in range(4):
                        g = 8 * (n // 2) + 2 * q + n % 2
                        r = slice((g % 2) * ST, (g % 2) * ST + ST)
                        for i, m in enumerate((S.m_re, S.m_im)):
                            last = pe.matmul(pm[0:GC, 2 + n % 2, q * P:(q + 1) * P], bb[r, i, g // 2, :],
                                             m[r, g // 2, 0:Q, :].rearrange("p k o -> p (k o)"),
                                             start=i == 0, stop=i == 1)
                    ps.did(last)
                ada_chunks(4, NW // WB)

            @block.vector
            def _(dve):
                ch = Steps(dve, chan)
                dv = Steps(dve, dve_s)

                def tt(out, x, y, op):
                    ch.link(dve.tensor_tensor(out, x, y, op))

                def cmul(o_re, o_im, x_re, x_im, y_re, y_im, t, shape=None):
                    ch.did(dve.tensor_tensor(o_re, x_re, y_re, ALU.mult))
                    ch.did(dve.tensor_tensor(o_im, x_re, y_im, ALU.mult))
                    tt(t, x_im, y_im, ALU.mult)
                    tt(o_re, o_re, t, ALU.subtract)
                    tt(t, x_im, y_re, ALU.mult)
                    tt(o_im, o_im, t, ALU.add)

                dve.wait_ge(pe_s, 1)
                ch.link(dve.tensor_copy(cT[:, :, :].rearrange("p k n -> p (k n)"), pm[:, 0, 0:9 * KD]))
                dve.wait_ge(pe_s, 2)
                ch.did(dve.tensor_copy(lr[:, :], pm[:, 1, 0:PAIRS]))
                ch.link(dve.tensor_copy(li[:, :], pm[:, 1, PAIRS:2 * PAIRS]))
                dve.wait_ge(act_s, 2)
                T = [t[:, :] for t in tmp]
                dv.did(dve.tensor_tensor(T[0], lr[:, :], T[7], ALU.mult))
                tt(T[1], li[:, :], T[7], ALU.mult)
                ch.link(dve.tensor_scalar(T[5], T[1], 1.0 / TWO_PI, MAGIC, ALU.mult, ALU.add))
                ch.link(dve.tensor_scalar(T[5], T[5], MAGIC, None, ALU.subtract))
                for part in (PI_HI, PI_MID):
                    ch.link(dve.scalar_tensor_tensor(out=T[1], in0=T[5], scalar=-part, in1=T[1], op0=ALU.mult, op1=ALU.add))
                dv.did(dve.scalar_tensor_tensor(out=T[1], in0=T[5], scalar=-PI_LO, in1=T[1], op0=ALU.mult, op1=ALU.add))
                dve.wait_ge(act_s, 6)
                tt(T[5], T[4], T[4], ALU.mult)
                ch.link(dve.tensor_scalar(T[5], T[5], -2.0, 1.0, ALU.mult, ALU.add))
                ch.did(dve.memset(pw_re[:, :, 0], 1.0))
                ch.did(dve.memset(pw_im[:, :, 0], 0.0))
                tt(pw_re[:, :, 1], T[2], T[5], ALU.mult)
                tt(pw_im[:, :, 1], T[2], T[3], ALU.mult)
                for k in range(2, 9):
                    cmul(pw_re[:, :, k], pw_im[:, :, k], pw_re[:, :, k - 1], pw_im[:, :, k - 1],
                         pw_re[:, :, 1], pw_im[:, :, 1], T[6])
                for s in range(Q):
                    ch.did(dve.tensor_copy(pr_re[:, :, s], pw_re[:, :, Q - 1 - s]))
                    ch.did(dve.tensor_copy(pr_im[:, :, s], pw_im[:, :, Q - 1 - s]))
                dve.sem_inc(powers_ok, 1)
                ch.did(dve.tensor_copy(S.a8_re[:, :], pw_re[:, :, 8]))
                ch.did(dve.tensor_copy(S.a8_im[:, :], pw_im[:, :, 8]))
                ch.link(dve.tensor_scalar(S.na8_im[:, :], pw_im[:, :, 8], -1.0, None, ALU.mult))
                ch.link(dve.tensor_scalar(T[0], pw_re[:, :, 1], -1.0, None, ALU.add))
                ch.did(dve.tensor_tensor(T[1], lr[:, :], lr[:, :], ALU.mult))
                tt(T[2], li[:, :], li[:, :], ALU.mult)
                tt(T[1], T[1], T[2], ALU.add)
                ch.link(dve.reciprocal(T[1], T[1]))
                ch.did(dve.tensor_tensor(T[2], T[0], lr[:, :], ALU.mult))
                tt(T[4], pw_im[:, :, 1], li[:, :], ALU.mult)
                tt(T[2], T[2], T[4], ALU.add)
                tt(T[2], T[2], T[1], ALU.mult)
                ch.did(dve.tensor_tensor(T[6], pw_im[:, :, 1], lr[:, :], ALU.mult))
                tt(T[4], T[0], li[:, :], ALU.mult)
                tt(T[6], T[6], T[4], ALU.subtract)
                tt(T[6], T[6], T[1], ALU.mult)
                s3 = [P, PAIRS, GC]
                t256 = big1[:, :, 0, :]
                dve.wait_ge(small, 16 * N_SMALL)
                cmul(bb[:, 0, :, :], bb[:, 1, :, :], fan(T[2], s3), fan(T[6], s3), b_in[:, 0, :, :], b_in[:, 1, :, :], t256)
                s4 = [P, PAIRS, Q, GC]
                pr, pi = fan(pr_re[:, :, :], s4), fan(pr_im[:, :, :], s4)
                b_re = bb[:, 0, :, :].unsqueeze(2).to_broadcast(s4)
                b_im = bb[:, 1, :, :].unsqueeze(2).to_broadcast(s4)
                t4 = big1[:, :, 0:Q, :]
                ch.did(dve.tensor_tensor(v[0], pr, b_re, ALU.mult))
                ch.did(dve.tensor_tensor(v[1], pr, b_im, ALU.mult))
                tt(t4, pi, b_im, ALU.mult)
                dv.did(dve.tensor_tensor(v[0], v[0], t4, ALU.subtract))
                dv.sync()
                tt(t4, pi, b_re, ALU.mult)
                dv.did(dve.tensor_tensor(v[1], v[1], t4, ALU.add))
                dv.sync()
                dve.wait_ge(act_s, 8)
                s9 = [P, PAIRS, 9, GC]
                q_re, q_im = fan(pw_re[:, :, :], s9), fan(pw_im[:, :, :], s9)
                c_re = cc[:, 0, :, :].unsqueeze(2).to_broadcast(s9)
                c_im = cc[:, 1, :, :].unsqueeze(2).to_broadcast(s9)
                m_re, t9 = S.m_re[:, :, :, :], big1[:, :, :, :]
                ch.did(dve.tensor_tensor(m_re, q_re, c_re, ALU.mult))
                tt(t9, q_im, c_im, ALU.mult)
                dv.did(dve.tensor_tensor(m_re, m_re, t9, ALU.subtract))
                ch.link(dve.tensor_tensor(dtmp[:, :, :], ident[0:GC, 0:GC].unsqueeze(1).to_broadcast([GC, G, GC]),
                                          fan(dd[:, :], [GC, G, GC]), ALU.mult))
                rc, rs = rot[:, :, 0, :], rot[:, :, 1, :]
                sq = [(T[5], T[3]), (T[0], T[1])]
                for i in range(3):
                    (x, y), (u, w) = sq[i % 2], sq[(i + 1) % 2]
                    cmul(u, w, x, y, x, y, T[2])
                ch.did(dve.memset(rc[:, :, 0:1], 1.0))
                ch.link(dve.memset(rs[:, :, 0:1], 0.0))
                n, i = 1, 1
                while n < NCH:
                    (x, y), (u, w) = sq[i % 2], sq[(i + 1) % 2]
                    sh = [P, PAIRS, n]
                    half = big1[:, :, :, :].rearrange("p a k o -> p a (k o)")[:, :, 0:n]
                    cmul(rc[:, :, n:2 * n], rs[:, :, n:2 * n], rc[:, :, 0:n], rs[:, :, 0:n], fan(x, sh), fan(y, sh), half)
                    cmul(u, w, x, y, x, y, T[2])
                    n, i = 2 * n, i + 1
                dve.sem_inc(rot_ok, 1)
                dve.wait_ge(act_s, 24)
                dve.tensor_tensor(k0[:, :, 0:GC], k0[:, :, 0:GC], dtmp[:, :, :], ALU.add).then_inc(k_ok, 1)



N_SMALL = 2 + 1 + 1 + 1 + NSEQ


def split_matmul(pe, out, left, right, n):
    for k in range(n):
        pe.matmul(out, left(0, k), right(0, k), start=k == 0, stop=False)
        pe.matmul(out, left(0, k), right(1, k), start=False, stop=False)
        last = pe.matmul(out, left(1, k), right(0, k), start=False, stop=k == n - 1)
    return last


def prompt_loop(eng, first, body, after=None):
    for b in range(2):
        body(first + b, (first + b) // 2, (first + b) % 2)
    with eng.Fori(1, 7) as j:
        if after is not None:
            after(j)
        for b in range(2):
            t = first + b
            body(2 * j + t, j + t // 2, t % 2)


def inv_sqrt(eng, c, y, total, share, x, t):
    c.link(eng.tensor_scalar(x, total, share, EPS, ALU.mult, ALU.add))
    c.link(eng.tensor_scalar(y.bitcast(I32), x.bitcast(I32), -0.5, float(0x5F3759DF), ALU.mult, ALU.add))
    for _ in range(3):
        c.link(eng.tensor_tensor(t, y, y, ALU.mult))
        c.link(eng.tensor_tensor(t, t, x, ALU.mult))
        c.link(eng.tensor_scalar(t, t, -0.5, 1.5, ALU.mult, ALU.add))
        c.link(eng.tensor_tensor(y, y, t, ALU.mult))


INV = 2 + 3 * 4


def mixin(nc, S, a, o):
    with ExitStack() as st:
        sb, sem = S.sb, S.sem
        RAW = 4
        win_hi = sb(st, "win_hi", [P, KD, 3 * DA], F32R)
        win_lo = sb(st, "win_lo", [P, KD, 3 * DA], F32R)
        raw = sb(st, "win_raw", [P, RAW, KD // RAW, DA])
        x = sb(st, "x", [P, 2, D])
        hT_hi = sb(st, "hT_hi", [P, 2, KD, P], F32R)
        hT_lo = sb(st, "hT_lo", [P, 2, KD, P], F32R)
        gain = sb(st, "gain1", [P, D])
        shift = sb(st, "shift1", [P, D])
        lng = sb(st, "lng", [P, DA])
        lnb = sb(st, "lnb", [P, DA])
        junk2 = sb(st, "junk2", [P, DA])
        ssq = sb(st, "ssq1", [P, 2])
        rstd = sb(st, "rstd1", [P, 2])
        v = sb(st, "v", [P, DA])
        u = sb(st, "u", [P, DA])
        a_row = sb(st, "a_row", [P, DA])
        s_row = sb(st, "s_row", [P, DA])
        mean = sb(st, "mean", [P, HEADS])
        var = sb(st, "var", [P, HEADS])
        newton = sb(st, "newton1", [P, 2, HEADS])
        pT = S.psum(st, "ps_hT", [P, 2, 512])
        pV = S.psum(st, "ps_v", [P, 512])
        pU = S.psum(st, "ps_u", [P, 512])
        pS = S.psum(st, "ps_s", [P, 512])
        pM = S.psum(st, "ps_mix", [P, 512])
        junk = S.psum(st, "ps_squares", [P, 2 * 512])
        ident = S.ident

        ln_in = sem("ln_loaded")
        mod_in, mod_samp, win_in = sem("mod1_loaded"), sem("mod1_sample_loaded"), [sem(f"win_loaded{i}") for i in range(RAW)]
        win_h, win_l = sem("win_hi_ready"), sem("win_lo_ready")
        x_in = [sem("x_loaded0"), sem("x_loaded1")]
        ssq_ok, ch, h_ok, hT_mm, hT_a, hT_d = sem("ssq1_ready"), sem("dve_chain1"), sem("h_ready"), sem("hT_transposed"), sem("hT_evac_act"), sem("hT_evac_dve")
        v_mm, v_ok, cen_ok, var_ok, vhat_ok, vn_ok = sem("v_mm"), sem("v_gelu"), sem("v_centred"), sem("v_var"), sem("v_scaled"), sem("v_normed")
        u_mm, u_ok, s_mm, s_ok, m_mm, a_ok = sem("u_mm"), sem("u_gelu"), sem("s_mm"), sem("s_copied"), sem("mix_mm"), sem("a_ready")
        xn_ok, s_out, a_out, v_out = sem("x_scaled"), sem("s_stored"), sem("a_stored"), sem("v_stored")
        w_view = a.w_in[0].rearrange("(k p) n -> p k n", p=P)
        x_rows = a.x_prompt[0]
        samp_rows = a.x_sample.rearrange("b t d -> (b t) d")

        def part_k(n):
            return slice(n % RAW * KD // RAW, (n % RAW + 1) * KD // RAW)

        def cols(n):
            c = (1, 0, 2)[n // RAW]
            return slice(c * DA, (c + 1) * DA)

        def rows_of(i):
            return NS if isinstance(i, int) and i == TP else P

        def dr(t, i):
            return t[TP * P:TOK, :] if isinstance(i, int) and i == TP else t[ds(i * P, P), :]

        with nc.Block() as block:
            @block.sync
            def _(sp):
                sp.dma_start(x[:, 0, :], x_rows[0:P, :]).then_inc(x_in[0], 16)
                sp.dma_start(gain[:, :], S.ada_d[0:1, D:2 * D].to_broadcast([P, D])).then_inc(mod_in, 16)
                sp.dma_start(shift[:, :], S.ada_d[0:1, 0:D].to_broadcast([P, D])).then_inc(mod_in, 16)
                for n in range(3 * RAW):
                    if n == RAW:
                        sp.dma_start(x[:, 1, :], x_rows[P:2 * P, :]).then_inc(x_in[1], 16)
                        sp.dma_start(lng[:, :], a.ln_g.rearrange("o h d -> o (h d)").to_broadcast([P, DA])).then_inc(ln_in, 16)
                        sp.dma_start(lnb[:, :], a.ln_b.rearrange("o h d -> o (h d)").to_broadcast([P, DA])).then_inc(ln_in, 16)
                    if n >= RAW:
                        sp.wait_ge(win_l, n - RAW + 1)
                    sp.dma_start(raw[:, n % RAW, :, :], w_view[:, part_k(n), cols(n)]).then_inc(win_in[n % RAW], 16)

                def stores(i, n, b):
                    r = rows_of(i)
                    sp.wait_ge(s_ok, i + 1)
                    sp.dma_start(dr(S.s_d, i), s_row[0:r, :]).then_inc(s_out, 16)
                    sp.wait_ge(a_ok, i + 1)
                    sp.dma_start(dr(S.a_d, i), a_row[0:r, :]).then_inc(a_out, 16)

                def step(i, n, b):
                    sp.wait_ge(hT_mm, i + 1)
                    sp.dma_start(x[:, b, :], x_rows[ds((i + 2) * P, P), :]).then_inc(x_in[b], 16)
                    stores(i, n, b)

                prompt_loop(sp, 0, step)
                sp.wait_ge(hT_mm, 15)
                sp.dma_start(x[0:NS, 0, :], samp_rows).then_inc(x_in[0], 16)
                sp.wait_ge(h_ok, TP)
                for k, t in enumerate((gain, shift)):
                    for q in range(NSEQ):
                        sp.dma_start(t[q * DSEQ:(q + 1) * DSEQ, :],
                                     S.ada_d[1 + q:2 + q, (1 - k) * D:(2 - k) * D].to_broadcast([DSEQ, D])).then_inc(mod_samp, 16)
                stores(14, 7, 0)
                stores(15, 7, 1)
                stores(16, 8, 0)
                sp.wait_ge(vn_ok, 2 * NT)
                sp.dma_start(o.v_sample[0].rearrange("b t d -> (b t) d"), v[0:NS, :]).then_inc(v_out, 16)
                sp.wait_ge(v_out, 16)
                sp.wait_ge(s_out, 16 * NT)
                sp.wait_ge(a_out, 16 * NT)

            @block.gpsimd
            def _(pool):

                def shift_h(i, n, b):
                    r = rows_of(i)
                    pool.wait_ge(xn_ok, i + 1)
                    pool.tensor_tensor(x[0:r, b, :], x[0:r, b, :], shift[0:r, :], ALU.add).then_inc(h_ok, 1)

                def affine_v(i):
                    r = rows_of(i)
                    pool.wait_ge(vhat_ok, i + 1)
                    pool.tensor_tensor(v[0:r, :], v[0:r, :], lng[0:r, :], ALU.mult).then_inc(vn_ok, 1)
                    pool.wait_ge(vn_ok, 2 * i + 1)
                    pool.tensor_tensor(v[0:r, :], v[0:r, :], lnb[0:r, :], ALU.add).then_inc(vn_ok, 1)

                pool.wait_ge(mod_in, 32)
                shift_h(0, 0, 0)
                shift_h(1, 0, 1)
                pool.wait_ge(ln_in, 32)

                def step(i, n, b):
                    affine_v(i)
                    if not (isinstance(i, int) and i + 2 > TP):
                        shift_h(i + 2, n + 1, b)

                prompt_loop(pool, 0, step)
                for i in (14, 15, 16):
                    step(i, i // 2, i % 2)

            @block.scalar
            def _(act):
                def square(i, n, b):
                    r = rows_of(i)
                    act.wait_ge(x_in[b], 16 * n + 16)
                    act.wait_ge(xn_ok, i)
                    act.activation(junk[0:r, :], x[0:r, b, :], ACT.Square, accum_out=ssq[0:r, b:b + 1]).then_inc(ssq_ok, 1)

                def evac(i, n, b):
                    r = rows_of(i)
                    act.wait_ge(hT_mm, i + 1)
                    for h in range(2):
                        act.activation(hT_hi[:, b, 4 * h:4 * h + 4, 0:r],
                                       pT[:, h, :].rearrange("p (k t) -> p k t", k=4)[:, :, 0:r], ACT.Copy).then_inc(hT_a, 1)

                def step(i, n, b):
                    r = rows_of(i)
                    last = isinstance(i, int) and i == TP
                    act.wait_ge(v_mm, i + 1)
                    act.activation(v[0:r, :], pV[0:r, :], ACT.Gelu_apprx_tanh).then_inc(v_ok, 1)
                    if not last:
                        evac(i + 1, n + b, 1 - b)
                    act.wait_ge(cen_ok, i + 1)
                    for h in range(HEADS):
                        s = act.activation(junk2[0:r, h * HD:(h + 1) * HD], v[0:r, h * HD:(h + 1) * HD], ACT.Square,
                                           accum_out=var[0:r, h:h + 1])
                    s.then_inc(var_ok, 1)
                    if not (isinstance(i, int) and i + 2 > TP):
                        square(i + 2, n + 1, b)
                    act.wait_ge(u_mm, i + 1)
                    act.wait_ge(a_ok, i)
                    act.activation(u[0:r, :], pU[0:r, :], ACT.Gelu_apprx_tanh).then_inc(u_ok, 1)
                    act.wait_ge(s_mm, i + 1)
                    act.wait_ge(s_out, 16 * i)
                    act.activation(s_row[0:r, :], pS[0:r, :], ACT.Copy).then_inc(s_ok, 1)

                square(0, 0, 0)
                for n in range(3 * RAW):
                    act.wait_ge(win_in[n % RAW], 16 * (n // RAW + 1))
                    act.activation(win_hi[:, part_k(n), cols(n)], raw[:, n % RAW, :, :], ACT.Copy).then_inc(win_h, 1)
                    if n == RAW - 1:
                        evac(0, 0, 0)
                    if n == RAW + 1:
                        square(1, 0, 1)
                prompt_loop(act, 0, step)
                for i in (14, 15, 16):
                    step(i, i // 2, i % 2)

            @block.tensor
            def _(pe):
                def transposes(i, n, b):
                    r = rows_of(i)
                    pe.wait_ge(h_ok, i + 1)
                    pe.wait_ge(hT_d, 2 * i)
                    for k in range(KD):
                        last = pe.transpose(pT[:, k // 4, k % 4 * P:k % 4 * P + r], x[0:r, b, k * P:(k + 1) * P],
                                            ident[0:r, 0:r])
                    last.then_inc(hT_mm, 1)

                def project(out, i, b, c, free, done):
                    r = rows_of(i)
                    pe.wait_ge(free, i)
                    last = split_matmul(pe, out[0:r, :], lambda t, k: (hT_hi, hT_lo)[t][:, b, k, 0:r],
                                        lambda t, k: (win_hi, win_lo)[t][:, k, c * DA:(c + 1) * DA], KD)
                    last.then_inc(done, 1)

                def step(i, n, b):
                    r = rows_of(i)
                    samp = isinstance(i, int) and i == TP
                    pe.wait_ge(hT_d, 2 * i + 2)
                    if isinstance(i, int) and i == 0:
                        pe.wait_ge(win_l, RAW)
                    project(pV, i, b, 1, v_ok, v_mm)
                    if not samp:
                        transposes(i + 1, n + b, 1 - b)
                    if isinstance(i, int) and i == 0:
                        pe.wait_ge(win_l, 2 * RAW)
                    project(pU, i, b, 0, u_ok, u_mm)
                    if isinstance(i, int) and i == 0:
                        pe.wait_ge(win_l, 3 * RAW)
                    project(pS, i, b, 2, s_ok, s_mm)
                    pe.wait_ge(vn_ok, 2 * i + 2)
                    pe.wait_ge(a_ok, i)
                    w = S.ws_samp if samp else S.ws
                    for h in range(HEADS):
                        last = pe.matmul(pM[0:r, h * HD:(h + 1) * HD], w[:, h, :], v[0:r, h * HD:(h + 1) * HD],
                                         start=True, stop=True)
                    last.then_inc(m_mm, 1)

                transposes(0, 0, 0)
                prompt_loop(pe, 0, step)
                for i in (14, 15, 16):
                    step(i, i // 2, i % 2)

            @block.vector
            def _(dve):
                c = Steps(dve, ch)

                def scale_x(i, n, b):
                    r = rows_of(i)
                    dve.wait_ge(ssq_ok, i + 1)
                    inv_sqrt(dve, c, rstd[0:r, 0:1], ssq[0:r, b:b + 1], 1.0 / D, newton[0:r, 0, 0:1], newton[0:r, 1, 0:1])
                    dve.scalar_tensor_tensor(out=x[0:r, b, :], in0=x[0:r, b, :], scalar=rstd[0:r, 0:1],
                                             in1=gain[0:r, :], op0=ALU.mult, op1=ALU.mult).then_inc(xn_ok, 1)

                def low_part(i, b):
                    r = rows_of(i)
                    for h in range(2):
                        dve.wait_ge(hT_a, 2 * i + h + 1)
                        ks = slice(4 * h, 4 * h + 4)
                        dve.tensor_tensor(hT_lo[:, b, ks, 0:r], pT[:, h, :].rearrange("p (k t) -> p k t", k=4)[:, :, 0:r],
                                          hT_hi[:, b, ks, 0:r].bitcast(F32), ALU.subtract).then_inc(hT_d, 1)

                def step(i, n, b):
                    r = rows_of(i)
                    samp = isinstance(i, int) and i == TP
                    v3 = v[0:r, :].rearrange("p (h d) -> p h d", h=HEADS)
                    s3 = [r, HEADS, HD]
                    dve.wait_ge(v_ok, i + 1)
                    c.link(dve.tensor_reduce(mean[0:r, :], v3, AX.X, ALU.add))
                    c.link(dve.tensor_scalar(mean[0:r, :], mean[0:r, :], 1.0 / HD, None, ALU.mult))
                    dve.tensor_tensor(v3, v3, fan(mean[0:r, :], s3), ALU.subtract).then_inc(cen_ok, 1)
                    if not samp:
                        low_part(i + 1, 1 - b)
                    dve.wait_ge(var_ok, i + 1)
                    inv_sqrt(dve, c, mean[0:r, :], var[0:r, :], 1.0 / HD, newton[0:r, 0, :], newton[0:r, 1, :])
                    dve.tensor_tensor(v3, v3, fan(mean[0:r, :], s3), ALU.mult).then_inc(vhat_ok, 1)
                    if not (isinstance(i, int) and i + 2 > TP):
                        if isinstance(i, int) and i + 2 == TP:
                            dve.wait_ge(mod_samp, 16 * 2 * NSEQ)
                        scale_x(i + 2, n + 1, b)
                    dve.wait_ge(m_mm, i + 1)
                    dve.wait_ge(u_ok, i + 1)
                    dve.wait_ge(a_out, 16 * i)
                    bs = S.bs_samp if samp else S.bs
                    for h in range(HEADS):
                        hs = slice(h * HD, (h + 1) * HD)
                        last = dve.scalar_tensor_tensor(out=a_row[0:r, hs], in0=pM[0:r, hs], scalar=bs[0:r, h:h + 1],
                                                        in1=u[0:r, hs], op0=ALU.add, op1=ALU.mult)
                    last.then_inc(a_ok, 1)

                dve.wait_ge(mod_in, 32)
                scale_x(0, 0, 0)
                for n in range(3 * RAW):
                    dve.wait_ge(win_h, n + 1)
                    dve.tensor_tensor(win_lo[:, part_k(n), cols(n)], raw[:, n % RAW, :, :],
                                      win_hi[:, part_k(n), cols(n)].bitcast(F32), ALU.subtract).then_inc(win_l, 1)
                    if n == RAW - 1:
                        low_part(0, 0)
                    if n == RAW + 1:
                        scale_x(1, 0, 1)
                prompt_loop(dve, 0, step, lambda j: c.at(2 * INV + CH1 * j))
                c.at(2 * INV + CH1 * 7)
                for i in (14, 15, 16):
                    step(i, i // 2, i % 2)


CH1 = 2 * (2 * INV + 2)


def s5(nc, S, a, o):
    with ExitStack() as st:
        sb, sem = S.sb, S.sem
        rows = sb(st, "chunk_rows", [P, 2, Q, DA])
        uT = sb(st, "uT", [P, G, CH])
        h_re = sb(st, "h_re", [P, PAIRS, CH + 1])
        h_im = sb(st, "h_im", [P, PAIRS, CH + 1])
        h0_in = sb(st, "h0_in", [P, 2, P])
        fin = sb(st, "fin", [P, 2, NSEQ, PAIRS])
        f1 = sb(st, "f1", [P, 2, NSEQ])
        rows_samp = sb(st, "samp_rows", [NSEQ, Q, DA])
        toep = sb(st, "toep", [P, G, P])
        turn = sb(st, "turn", [P, 4, 2, NCH])
        rot = sb(st, "rot", [P, 2, 4, NCH])
        scan = sb(st, "scan", [P, 2, 2, NCH])
        back = sb(st, "back", [P, 2, NCH])
        fo = sb(st, "fo", [P, 2, P])
        po = sb(st, "po", [PAIRS, 2, P])
        pX = S.psum(st, "ps_x", [P, 4, 512])
        pB = S.psum(st, "ps_b", [P, 4, 512])
        ident = S.ident

        rows_in, u_mm, u_a, u_d, h0_l, h0_mm, h0_ok = [sem(f"chunks_loaded{i}") for i in range(3)], sem("uT_mm"), sem("uT_evac_act"), sem("uT_evac_dve"), sem("h0_loaded"), sem("h0_mm"), sem("h0_ready")
        x_mm, x_free, scan_ok, h_ok, ch, ph = sem("state_mm"), sem("state_free"), sem("scan_ready"), sem("state_ready"), sem("dve_chain2"), sem("pool_chain2")
        y_mm, y_ok, y_out, f_mm, f_ok, f_out, fin_ok = sem("y_mm"), sem("y_gelu"), [sem("y_stored")], sem("final_mm"), sem("final_copied"), sem("final_stored"), sem("sample_state")
        h_free = sem("scan_free")
        WIDTH = (P, P, NSEQ)
        at = (0, P, NCH)
        s_rows = S.s_d.rearrange("(c s) n -> c s n", s=Q)
        y_rows = S.y_d.rearrange("(c s) n -> c s n", s=Q)

        by_group = [h[:, :, :].rearrange("p a c -> p (a c)")[:, 0:Q * DA] for h in (h_re, h_im, h_re)]
        toep_in, turn_in = sem("toep_loaded"), [sem(f"turn_loaded{i}") for i in range(4)]

        def row_tile(t):
            return rows_samp[:, :, :] if t == 2 else rows[:, t, :, :]

        perm_a, perm_d = sem("regrouped_act"), sem("regrouped_dve")

        def regroup(eng, t, half):
            w = WIDTH[t]
            gs = slice(half * G // 2, (half + 1) * G // 2)
            eng.wait_ge(rows_in[t], 16)
            if t == 2:
                eng.wait_ge(u_mm, 8)
            dst = by_group[t][0:w, :].rearrange("p (g s h) -> p g s h", g=G, s=Q)[:, gs, :, :]
            src = row_tile(t).rearrange("p s (g h) -> p g s h", g=G)[:, gs, :, :]
            if half == 0:
                eng.activation(dst, src, ACT.Copy).then_inc(perm_a, 1)
            else:
                eng.tensor_copy(dst, src).then_inc(perm_d, 1)

        with nc.Block() as block:
            @block.sync
            def _(sp):
                for t in range(2):
                    sp.dma_start(rows[:, t, :, :], s_rows[at[t]:at[t] + P, :, :]).then_inc(rows_in[t], 16)
                for i, x in enumerate((a.state_ssm_re, a.state_ssm_im)):
                    sp.dma_start(h0_in[:, i, :], x[0].rearrange("q (a g) p -> (q a) (g p)", g=2)).then_inc(h0_l, 16)
                sp.dma_start(rows_samp[:, :, :], s_rows[NCH:CH, :, :]).then_inc(rows_in[2], 16)
                for k in range(4):
                    sp.dma_start(turn[:, k, :, :], S.rot_d[:, k, :, :]).then_inc(turn_in[k], 16)
                for s in range(Q):
                    sp.dma_start(toep[s * GC:(s + 1) * GC, :, :], S.kpad_d[:, :, P - s * GC:2 * P - s * GC]).then_inc(toep_in, 16)
                for k in range(4, PAIRS):
                    sp.wait_ge(h_ok, 2 * (k - 3))
                    sp.dma_start(turn[:, k % 4, :, :], S.rot_d[:, k, :, :]).then_inc(turn_in[k % 4], 16)
                for t in range(3):
                    sp.wait_ge(y_ok, 20 + 2 * t)
                    sp.dma_start(y_rows[at[t]:at[t] + WIDTH[t], :, :], row_tile(t)).then_inc(y_out[0], 16)
                sp.wait_ge(f_ok, 4)
                for i, (x, y) in enumerate(((o.ssm_re_prompt, o.ssm_re_sample), (o.ssm_im_prompt, o.ssm_im_sample))):
                    sp.dma_start(x[0, 0].rearrange("(a g) p -> a (g p)", g=2), po[:, i, :]).then_inc(f_out, 16)
                    sp.dma_start(y[0].rearrange("q (a g) p -> (q a) (g p)", g=2), fo[:, i, :]).then_inc(f_out, 16)
                sp.wait_ge(f_out, 64)
                sp.wait_ge(y_out[0], 48)

            @block.tensor
            def _(pe):
                for n in range(24):
                    t, m = n // 8, n % 8
                    w = WIDTH[t]
                    if m % 4 == 0:
                        pe.wait_ge((perm_a, perm_d)[m // 4], t + 1)
                    if n >= 2:
                        pe.wait_ge((u_a, u_d)[n % 2], n // 2)
                    for q in range(4):
                        g = 4 * m + q
                        last = pe.transpose(pB[:, n % 2, q * P:q * P + w], by_group[t][0:w, g * P:(g + 1) * P],
                                            ident[0:w, 0:w])
                    last.then_inc(u_mm, 1)
                pe.wait_ge(h0_l, 32)
                for i in range(2):
                    last = pe.transpose(pB[:, 2, i * P:(i + 1) * P], h0_in[:, i, :], ident[:, :])
                last.then_inc(h0_mm, 1)
                pe.wait_ge(u_a, 12)
                pe.wait_ge(u_d, 12)
                def additions(k):
                    if k >= 2:
                        pe.wait_ge(x_free, k - 1)
                    for i in range(2):
                        for g in range(2):
                            r = slice(g * ST, (g + 1) * ST)
                            last = pe.matmul(pX[r, 2 * (k % 2) + i, 0:CH], S.wx[:, k, i, r], uT[:, 2 * k + g, :],
                                             start=True, stop=True)
                    last.then_inc(x_mm, 1)
                def outputs(n):
                    m, t, r2 = n // 6, n % 6 // 2, n % 2
                    w = WIDTH[t]
                    r = slice(r2 * ST, (r2 + 1) * ST)
                    if n == 0:
                        pe.wait_ge(toep_in, 16 * Q)
                    if n >= 4:
                        pe.wait_ge(y_ok, n - 3)
                    for q in range(4):
                        k = 4 * m + q
                        g = 2 * k + r2
                        if t == 0 and r2 == 0:
                            pe.wait_ge(h_ok, 2 * (k + 1))
                        c0 = at[t] + (1 if t == 2 else 0)
                        out = pB[0:w, n % 4, q * P:(q + 1) * P]
                        pe.matmul(out, uT[:, g, at[t]:at[t] + w], toep[:, g, :], start=True, stop=False)
                        pe.matmul(out, h_re[r, k, c0:c0 + w], S.m_re[r, k, 1:9, :].rearrange("p k o -> p (k o)"),
                                  start=False, stop=False)
                        last = pe.matmul(out, h_im[r, k, c0:c0 + w], S.m_im[r, k, 1:9, :].rearrange("p k o -> p (k o)"),
                                         start=False, stop=True)
                    last.then_inc(y_mm, 1)

                for k in range(4):
                    additions(k)
                pe.wait_ge(h0_ok, 2)
                for m in range(4):
                    for n in range(6 * m, 6 * m + 6):
                        if m < 3 and n % 6 < 4:
                            additions(4 * m + 4 + n % 6)
                        outputs(n)
                pe.wait_ge(y_ok, 24)
                pe.wait_ge(fin_ok, 2 * PAIRS)
                for i, h in enumerate((h_re, h_im)):
                    pe.transpose(pB[0:PAIRS, 3, i * P:(i + 1) * P], h[:, :, NCH], ident[:, :])
                for i in range(2):
                    last = pe.transpose(pB[:, 2, i * P:(i + 1) * P], fin[:, i, :, :].rearrange("p q a -> p (q a)"), ident[:, :])
                last.then_inc(f_mm, 1)

            @block.scalar
            def _(act):
                for n in range(0, 24, 2):
                    t, m = n // 8, n % 8
                    w = WIDTH[t]
                    if m == 0:
                        regroup(act, t, 0)
                    act.wait_ge(u_mm, n + 1)
                    act.activation(uT[:, 4 * m:4 * m + 4, at[t]:at[t] + w],
                                   pB[:, 0, :].rearrange("p (g c) -> p g c", g=4)[:, :, 0:w], ACT.Copy).then_inc(u_a, 1)
                for n in range(24):
                    m, t, r2 = n // 6, n % 6 // 2, n % 2
                    w = WIDTH[t]
                    act.wait_ge(y_mm, n + 1)
                    out = row_tile(t).rearrange("p s (m q r o) -> p m r q s o", m=4, q=4, r=2)[:, m, r2, :, :, :]
                    act.activation(out, pB[0:w, n % 4, :].rearrange("p (q s o) -> p q s o", q=4, s=Q),
                                   ACT.Gelu_apprx_tanh).then_inc(y_ok, 1)

            @block.vector
            def _(dve):
                c = Steps(dve, ch)
                for n in range(1, 24, 2):
                    t, m = n // 8, n % 8
                    w = WIDTH[t]
                    if m == 1:
                        regroup(dve, t, 1)
                    dve.wait_ge(u_mm, n + 1)
                    dve.tensor_copy(uT[:, 4 * m:4 * m + 4, at[t]:at[t] + w],
                                    pB[:, 1, :].rearrange("p (g c) -> p g c", g=4)[:, :, 0:w]).then_inc(u_d, 1)
                dve.wait_ge(h0_mm, 1)
                for i, h in enumerate((h_re, h_im)):
                    dve.tensor_copy(h[:, :, NCH + 1:CH + 1],
                                    pB[:, 2, i * P:(i + 1) * P].rearrange("p (q a) -> p a q", q=NSEQ)).then_inc(h0_ok, 1)
                dve.wait_ge(h0_ok, 2)

                def col(t, k):
                    return t[:, ds(k, 1)]

                def pair(k, b, q, j):
                    dve.wait_ge(turn_in[q], 16 * j + 16)
                    R, I = pX[:, 2 * b, :], pX[:, 2 * b + 1, :]
                    C, N = turn[:, q, 0, :], turn[:, q, 1, :]
                    dve.wait_ge(x_mm, k + 1)
                    dve.wait_ge(scan_ok, 2 * k + 2)
                    c.did(dve.tensor_tensor(rot[:, b, 0, :], R[:, 0:NCH], C, ALU.mult))
                    c.did(dve.tensor_tensor(rot[:, b, 1, :], I[:, 0:NCH], N, ALU.mult))
                    c.did(dve.tensor_tensor(rot[:, b, 2, :], I[:, 0:NCH], C, ALU.mult))
                    c.link(dve.tensor_tensor(rot[:, b, 3, :], R[:, 0:NCH], N, ALU.mult))
                    h0r = h_re[:, ds(k, 1), NCH + 1:CH + 1].rearrange("p o c -> p (o c)")
                    h0i = h_im[:, ds(k, 1), NCH + 1:CH + 1].rearrange("p o c -> p (o c)")
                    c.did(dve.scalar_tensor_tensor(out=f1[:, 0, :], in0=h0r, scalar=col(S.a8_re, k), in1=R[:, NCH:CH],
                                                   op0=ALU.mult, op1=ALU.add))
                    c.link(dve.scalar_tensor_tensor(out=f1[:, 1, :], in0=h0r, scalar=col(S.a8_im, k), in1=I[:, NCH:CH],
                                                    op0=ALU.mult, op1=ALU.add))
                    dve.scalar_tensor_tensor(out=fin[:, 0, :, ds(k, 1)].rearrange("p q o -> p (q o)"), in0=h0i,
                                             scalar=col(S.na8_im, k), in1=f1[:, 0, :], op0=ALU.mult, op1=ALU.add).then_inc(fin_ok, 1)
                    dve.scalar_tensor_tensor(out=fin[:, 1, :, ds(k, 1)].rearrange("p q o -> p (q o)"), in0=h0i,
                                             scalar=col(S.a8_re, k), in1=f1[:, 1, :], op0=ALU.mult, op1=ALU.add).then_inc(fin_ok, 1)
                    dve.wait_ge(fin_ok, 2 * k + 2)
                    c.did(dve.tensor_tensor(rot[:, b, 0, :], rot[:, b, 0, :], rot[:, b, 1, :], ALU.add))
                    c.link(dve.tensor_tensor(rot[:, b, 2, :], rot[:, b, 2, :], rot[:, b, 3, :], ALU.subtract))
                    dve.sem_inc(x_free, 1)
                    dve.wait_ge(h_free, k + 1)
                    for i in range(2):
                        dve.tensor_tensor_scan(scan[:, b, i, :], col(S.decay, k).to_broadcast([P, NCH]),
                                               rot[:, b, 2 * i, :], 0.0, ALU.mult, ALU.add).then_inc(scan_ok, 1)

                dve.sem_inc(scan_ok, 2)
                with dve.Fori(0, PAIRS // 4) as j:
                    c.at(8 * 4 * j)
                    for q in range(4):
                        pair(4 * j + q, q % 2, q, j)
                assert c.count == 8 * 4
                dve.wait_ge(f_mm, 1)
                for i in range(2):
                    dve.tensor_copy(po[:, i, :], pB[0:PAIRS, 3, i * P:(i + 1) * P]).then_inc(f_ok, 1)
                    dve.tensor_copy(fo[:, i, :], pB[:, 2, i * P:(i + 1) * P]).then_inc(f_ok, 1)

            @block.gpsimd
            def _(pool):
                p = Steps(pool, ph)
                pool.sem_clear(S.spent)
                pool.wait_ge(u_mm, 24)
                p.did(pool.memset(h_re[:, :, 0:1], 0.0))
                p.link(pool.memset(h_im[:, :, 0:1], 0.0))
                pool.sem_inc(h_free, 2)

                def pair(k, b, q):
                    C, N = turn[:, q, 0, :], turn[:, q, 1, :]
                    re = h_re[:, ds(k, 1), 1:NCH + 1].rearrange("p o c -> p (o c)")
                    im = h_im[:, ds(k, 1), 1:NCH + 1].rearrange("p o c -> p (o c)")
                    pool.wait_ge(scan_ok, 2 * k + 4)
                    p.did(pool.tensor_tensor(re, scan[:, b, 0, :], C, ALU.mult))
                    p.did(pool.tensor_tensor(im, scan[:, b, 0, :], N, ALU.mult))
                    p.did(pool.tensor_tensor(back[:, 0, :], scan[:, b, 1, :], N, ALU.mult))
                    p.link(pool.tensor_tensor(back[:, 1, :], scan[:, b, 1, :], C, ALU.mult))
                    pool.sem_inc(h_free, 1)
                    pool.tensor_tensor(re, re, back[:, 0, :], ALU.subtract).then_inc(h_ok, 1)
                    pool.tensor_tensor(im, im, back[:, 1, :], ALU.add).then_inc(h_ok, 1)
                    pool.wait_ge(h_ok, 2 * k + 2)

                with pool.Fori(0, PAIRS // 4) as j:
                    p.at(2 + 4 * 4 * j)
                    for q in range(4):
                        pair(4 * j + q, q % 2, q)
                assert p.count == 2 + 4 * 4


def mixout(nc, S, a):
    with ExitStack() as st:
        sb, sem = S.sb, S.sem
        RAW = 8
        raw = sb(st, "weights_raw", [P, RAW, D])
        wout_hi = sb(st, "wout_hi", [P, KD, D], F32R)
        wout_lo = sb(st, "wout_lo", [P, KD, D], F32R)
        wglu_hi = sb(st, "wglu_hi", [P, 4, DA], F32R)
        wglu_lo = sb(st, "wglu_lo", [P, 4, DA], F32R)
        wr = sb(st, "wr", [P, KD, NR])
        bglu = sb(st, "bglu", [P, DA])
        br = sb(st, "br", [P, NR])
        gate = sb(st, "gate1", [P, D])
        gain = sb(st, "gain2", [P, D])
        shift = sb(st, "shift2", [P, D])
        blank = sb(st, "blank", [P, D])
        cat = sb(st, "cat", [P, 2, D])
        x2 = sb(st, "x2", [P, 2, D])
        yT_hi = sb(st, "yT_hi", [P, 4, P], F32R)
        yT_lo = sb(st, "yT_lo", [P, 4, P], F32R)
        catT_hi = sb(st, "catT_hi", [P, KD, P], F32R)
        catT_lo = sb(st, "catT_lo", [P, KD, P], F32R)
        z = sb(st, "z", [P, DA])
        mixed = sb(st, "mixed", [P, 2, DA])
        h2 = sb(st, "h2", [P, D])
        h2T = sb(st, "h2T", [P, KD, P])
        junk = sb(st, "junk3", [P, D])
        ssq = sb(st, "ssq2", [P, 1])
        rstd = sb(st, "rstd2", [P, 1])
        newton = sb(st, "newton2", [P, 2])
        pY = S.psum(st, "ps_yT", [P, 512])
        pZ = S.psum(st, "ps_z", [P, 512])
        pC = S.psum(st, "ps_catT", [P, 2, 512])
        pM = S.psum(st, "ps_out", [P, 2, 512])
        pH = S.psum(st, "ps_h2T", [P, 2, 512])
        ident, lg = S.ident, S.logits

        mod_in, mod_s, w_in, w_h, w_l = sem("mod2_loaded"), sem("mod2_sample_loaded"), [sem(f"weights_loaded{i}") for i in range(RAW)], sem("weights_hi"), sem("weights_lo")
        a_in, x_in = [sem("cat_loaded0"), sem("cat_loaded1")], [sem("x2_in0"), sem("x2_in1")]
        yT_mm, yT_a, yT_d, z_mm, z_ok, sg_ok, b_ok = sem("yT_mm"), sem("yT_hi_ready"), sem("yT_lo_ready"), sem("z_mm"), sem("z_ok"), sem("sigmoid_ok"), sem("y_gated")
        c_mm, c_a, c_d, o_mm, mul_ok, x2_ok = sem("catT_mm"), sem("catT_hi_ready"), sem("catT_lo_ready"), sem("out_mm"), sem("gated"), sem("x2_ready")
        sq_ok, xs_ok, h2_ok, h_mm, h_a, h_d, l_mm, l_ok, h2_out, ch = (sem("ssq2_ready"), sem("x2_scaled"), sem("h2_ready"), sem("h2T_mm"), sem("h2T_act"), sem("h2T_dve"), sem("logit_mm"), sem("logits_ready"), sem("h2_stored"), sem("dve_chain3"))
        bglu_in = sem("bglu_loaded")
        x2_out, blank_ok, blank_out = sem("x2_stored"), sem("blank_ready"), sem("blank_stored")
        w_glu, w_out = a.w_glu[0].rearrange("(k p) n -> p k n", p=P), a.w_out[0].rearrange("(k p) n -> p k n", p=P)
        NPART = 2 + KD

        def part(t_glu, t_out, n):
            return t_glu[:, 2 * n:2 * n + 2, :] if n < 2 else t_out[:, n - 2, :]

        def raw_part(n):
            return raw[:, n % RAW, :].rearrange("p (k n) -> p k n", k=2) if n < 2 else raw[:, n % RAW, :]

        def rows_of(i):
            return NS if isinstance(i, int) and i == TP else P

        def dr(t, i):
            return t[TP * P:TOK, :] if isinstance(i, int) and i == TP else t[ds(i * P, P), :]

        def tiles(eng, step):
            step(0, 0, 0)
            prompt_loop(eng, 1, step)
            step(15, 7, 1)
            step(16, 8, 0)

        with nc.Block() as block:
            @block.sync
            def _(sp):
                def load_cat(i, b):
                    r = rows_of(i)
                    sp.dma_start(cat[0:r, b, DA:D], dr(S.y_d, i)).then_inc(a_in[b], 16)
                    sp.dma_start(cat[0:r, b, 0:DA], dr(S.a_d, i)).then_inc(a_in[b], 16)

                def load_x(i, b):
                    x = a.x_sample.rearrange("b t d -> (b t) d") if rows_of(i) == NS else a.x_prompt[0, ds(i * P, P), :]
                    sp.dma_start(x2[0:rows_of(i), b, :], x).then_inc(x_in[b], 16)

                load_cat(0, 0)
                for n in range(NPART):
                    if n >= RAW:
                        sp.wait_ge(w_l, n - RAW + 1)
                    sp.dma_start(raw_part(n), part(w_glu, w_out, n)).then_inc(w_in[n % RAW], 16)
                    if n == 1:
                        sp.dma_start(bglu[:, :], a.b_glu.to_broadcast([P, DA])).then_inc(bglu_in, 16)
                for t, c in ((gate, 2), (gain, 4), (shift, 3)):
                    sp.dma_start(t[:, :], S.ada_d[0:1, c * D:(c + 1) * D].to_broadcast([P, D])).then_inc(mod_in, 16)
                    if c == 2:
                        load_x(0, 0)
                load_cat(1, 1)
                sp.dma_start(wr[:, :, 0:EG], a.w_group[0].rearrange("(k p) n -> p k n", p=P)).then_inc(mod_in, 16)
                sp.dma_start(wr[:, :, EG:NR], a.w_expert[0].rearrange("(k p) n -> p k n", p=P)).then_inc(mod_in, 16)
                sp.dma_start(br[:, 0:EG], a.b_group.to_broadcast([P, EG])).then_inc(mod_in, 16)
                sp.dma_start(br[:, EG:NR], a.b_expert.to_broadcast([P, NE])).then_inc(mod_in, 16)
                load_x(1, 1)
                sp.wait_ge(blank_ok, 1)

                def step(i, n, b):
                    static = isinstance(i, int)
                    if not (static and i + 2 > TP):
                        sp.wait_ge(c_mm, i + 1)
                        load_cat(i + 2, b)
                    if static and i == TP:
                        for q in range(NSEQ):
                            sp.dma_start(gate[q * DSEQ:(q + 1) * DSEQ, :],
                                         S.ada_d[1 + q:2 + q, 2 * D:3 * D].to_broadcast([DSEQ, D])).then_inc(mod_s, 16)
                        for t, c in ((gain, 4), (shift, 3)):
                            for q in range(NSEQ):
                                sp.dma_start(t[q * DSEQ:(q + 1) * DSEQ, :],
                                             S.ada_d[1 + q:2 + q, c * D:(c + 1) * D].to_broadcast([DSEQ, D])).then_inc(mod_s, 16)
                    sp.wait_ge(x2_ok, 2 * i + 2)
                    sp.dma_start(dr(S.x2_d, i), x2[0:rows_of(i), b, :]).then_inc(x2_out, 16)
                    for k in range(2):
                        if not (static and 2 * i + k >= NBLK - FULL):
                            sp.dma_start(S.yb_d[ds((FULL + k + 2 * i) * P, P), :], blank[:, :]).then_inc(blank_out, 16)
                    sp.wait_ge(h2_ok, i + 1)
                    sp.dma_start(dr(S.h2_d, i), h2[0:rows_of(i), :]).then_inc(h2_out, 16)
                    if not (static and i + 2 > TP):
                        sp.wait_ge(x2_out, 16 * i + 16)
                        load_x(i + 2, b)

                prompt_loop(sp, 0, step)
                for i in (14, 15, 16):
                    step(i, i // 2, i % 2)
                sp.wait_ge(h2_out, 16 * NT)
                sp.wait_ge(x2_out, 16 * NT)
                sp.wait_ge(blank_out, 16 * (NBLK - FULL))

            @block.tensor
            def _(pe):
                def turn_y(i, n, b):
                    r = rows_of(i)
                    pe.wait_ge(a_in[b], 32 * n + 32)
                    pe.wait_ge(yT_d, i)
                    for k in range(4):
                        last = pe.transpose(pY[:, k * P:k * P + r], cat[0:r, b, DA + k * P:DA + (k + 1) * P], ident[0:r, 0:r])
                    last.then_inc(yT_mm, 1)

                def glu(i, n, b, logits_out):
                    r = rows_of(i)
                    pe.wait_ge(yT_d, i + 1)
                    pe.wait_ge(l_ok, logits_out)
                    split_matmul(pe, pZ[0:r, :], lambda t, k: (yT_hi, yT_lo)[t][:, k, 0:r],
                                 lambda t, k: (wglu_hi, wglu_lo)[t][:, k, :], 4).then_inc(z_mm, 1)

                def turn_cat(i, n, b):
                    r = rows_of(i)
                    pe.wait_ge(b_ok, i + 1)
                    pe.wait_ge(c_d, 2 * i)
                    for k in range(KD):
                        last = pe.transpose(pC[:, k // 4, k % 4 * P:k % 4 * P + r], cat[0:r, b, k * P:(k + 1) * P],
                                            ident[0:r, 0:r])
                    last.then_inc(c_mm, 1)

                def project(i, b, c):
                    r = rows_of(i)
                    pe.wait_ge(c_d, 2 * i + 2)
                    if not (isinstance(i, int) and i == 0):
                        pe.wait_ge(mul_ok, 2 * i - 1 + c)
                    cols = slice(c * DA, (c + 1) * DA)
                    split_matmul(pe, pM[0:r, c, :], lambda t, k: (catT_hi, catT_lo)[t][:, k, 0:r],
                                 lambda t, k: (wout_hi, wout_lo)[t][:, k, cols], KD).then_inc(o_mm, 1)

                def turn_h(i):
                    r = rows_of(i)
                    pe.wait_ge(h2_ok, i + 1)
                    pe.wait_ge(h_a, i)
                    pe.wait_ge(h_d, i)
                    for k in range(KD):
                        last = pe.transpose(pH[:, k // 4, k % 4 * P:k % 4 * P + r], h2[0:r, k * P:(k + 1) * P],
                                            ident[0:r, 0:r])
                    last.then_inc(h_mm, 1)

                def logits(i, z_done):
                    r = rows_of(i)
                    pe.wait_ge(h_a, i + 1)
                    pe.wait_ge(h_d, i + 1)
                    if isinstance(i, int) and i == 0:
                        pe.wait_ge(mod_in, 16 * 7)
                    pe.wait_ge(z_ok, z_done)
                    for k in range(KD):
                        last = pe.matmul(pZ[0:r, 0:NR], h2T[:, k, 0:r], wr[:, k, :], start=k == 0, stop=k == KD - 1)
                    last.then_inc(l_mm, 1)

                def step(i, n, b):
                    first, last = isinstance(i, int) and i == 0, isinstance(i, int) and i == TP
                    if not last:
                        turn_y(i + 1, n + b, 1 - b)
                    project(i, b, 0)
                    if not last:
                        glu(i + 1, n + b, 1 - b, 0 if first else i - 1)
                    project(i, b, 1)
                    if not first:
                        turn_h(i - 1)
                    if not last:
                        turn_cat(i + 1, n + b, 1 - b)
                    if not first:
                        logits(i - 1, NT if last else i + 2)

                turn_y(0, 0, 0)
                pe.wait_ge(w_l, 2)
                glu(0, 0, 0, 0)
                turn_cat(0, 0, 0)
                pe.wait_ge(w_l, NPART)
                tiles(pe, step)
                turn_h(TP)
                logits(TP, NT)

            @block.scalar
            def _(act):
                def evac_y(i, b):
                    r = rows_of(i)
                    act.wait_ge(yT_mm, i + 1)
                    act.activation(yT_hi[:, :, 0:r], pY[:, :].rearrange("p (k t) -> p k t", k=4)[:, :, 0:r], ACT.Copy).then_inc(yT_a, 1)

                def sigmoid(i, b):
                    r = rows_of(i)
                    act.wait_ge(z_ok, i + 1)
                    act.activation(z[0:r, :], z[0:r, :], ACT.Sigmoid).then_inc(sg_ok, 1)

                def evac(i, b):
                    r = rows_of(i)
                    act.wait_ge(c_mm, i + 1)
                    for h in range(2):
                        act.activation(catT_hi[:, 4 * h:4 * h + 4, 0:r],
                                       pC[:, h, :].rearrange("p (k t) -> p k t", k=4)[:, :, 0:r], ACT.Copy).then_inc(c_a, 1)

                def evac_h(i):
                    r = rows_of(i)
                    act.wait_ge(h_mm, i + 1)
                    act.wait_ge(l_mm, i)
                    act.activation(h2T[:, 0:4, 0:r], pH[:, 0, :].rearrange("p (k t) -> p k t", k=4)[:, :, 0:r],
                                   ACT.Copy).then_inc(h_a, 1)

                def step(i, n, b):
                    first, last = isinstance(i, int) and i == 0, isinstance(i, int) and i == TP
                    if not last:
                        evac_y(i + 1, 1 - b)
                        sigmoid(i + 1, 1 - b)
                    if not first:
                        evac_h(i - 1)
                    if not last:
                        evac(i + 1, 1 - b)
                    act.wait_ge(x2_ok, 2 * i + 2)
                    act.wait_ge(xs_ok, i)
                    act.activation(junk[0:rows_of(i), :], x2[0:rows_of(i), b, :], ACT.Square,
                                   accum_out=ssq[0:rows_of(i), :]).then_inc(sq_ok, 1)

                evac_y(0, 0)
                for n in range(NPART):
                    act.wait_ge(w_in[n % RAW], 16 * (n // RAW + 1))
                    act.activation(part(wglu_hi, wout_hi, n), raw_part(n), ACT.Copy).then_inc(w_h, 1)
                    if n == 6:
                        sigmoid(0, 0)
                evac(0, 0)
                tiles(act, step)
                evac_h(TP)

            @block.gpsimd
            def _(pool):
                def gate_y(i, n, b):
                    r = rows_of(i)
                    pool.wait_ge(sg_ok, i + 1)
                    pool.tensor_tensor(cat[0:r, b, DA:D], cat[0:r, b, DA:D], z[0:r, :], ALU.mult).then_inc(b_ok, 1)

                def residual(i, n, b, c):
                    r = rows_of(i)
                    if c == 0:
                        pool.wait_ge(x_in[b], 16 * n + 16)
                    pool.wait_ge(mul_ok, 2 * i + c + 1)
                    half = x2[0:r, b, c * DA:(c + 1) * DA]
                    pool.tensor_tensor(half, half, mixed[0:r, c, :], ALU.add).then_inc(x2_ok, 1)

                def step(i, n, b):
                    r = rows_of(i)
                    last = isinstance(i, int) and i == TP
                    residual(i, n, b, 0)
                    if not last:
                        gate_y(i + 1, n + b, 1 - b)
                    residual(i, n, b, 1)
                    pool.wait_ge(xs_ok, i + 1)
                    pool.tensor_tensor(h2[0:r, :], h2[0:r, :], shift[0:r, :], ALU.add).then_inc(h2_ok, 1)

                pool.memset(blank[:, :], 0.0).then_inc(blank_ok, 1)
                gate_y(0, 0, 0)
                tiles(pool, step)

            @block.vector
            def _(dve):
                c = Steps(dve, ch)

                def gated(i, h):
                    r = rows_of(i)
                    dve.wait_ge(o_mm, 2 * i + h + 1)
                    dve.wait_ge(x2_ok, 2 * i)
                    dve.tensor_tensor(mixed[0:r, h, :], pM[0:r, h, :], gate[0:r, h * DA:(h + 1) * DA], ALU.mult).then_inc(mul_ok, 1)

                def bias_z(i):
                    r = rows_of(i)
                    dve.wait_ge(z_mm, i + 1)
                    dve.wait_ge(b_ok, i)
                    dve.tensor_tensor(z[0:r, :], pZ[0:r, :], bglu[0:r, :], ALU.add).then_inc(z_ok, 1)

                def rest(lo, hi, ps, r):
                    return dve.tensor_tensor(lo, ps.rearrange("p (k t) -> p k t", k=4)[:, :, 0:r], hi.bitcast(F32), ALU.subtract)

                def low_y(i):
                    r = rows_of(i)
                    dve.wait_ge(yT_a, i + 1)
                    rest(yT_lo[:, :, 0:r], yT_hi[:, :, 0:r], pY[:, :], r).then_inc(yT_d, 1)

                def low_cat(i):
                    r = rows_of(i)
                    for h in range(2):
                        ks = slice(4 * h, 4 * h + 4)
                        dve.wait_ge(c_a, 2 * i + h + 1)
                        rest(catT_lo[:, ks, 0:r], catT_hi[:, ks, 0:r], pC[:, h, :], r).then_inc(c_d, 1)

                def evac_h(i):
                    r = rows_of(i)
                    dve.wait_ge(h_mm, i + 1)
                    dve.wait_ge(l_mm, i)
                    dve.tensor_copy(h2T[:, 4:8, 0:r],
                                    pH[:, 1, :].rearrange("p (k t) -> p k t", k=4)[:, :, 0:r]).then_inc(h_d, 1)

                def logits(i):
                    r = rows_of(i)
                    dve.wait_ge(l_mm, i + 1)
                    dve.tensor_tensor(lg[0:r, ds(i, 1), :].rearrange("p o n -> p (o n)"), pZ[0:r, 0:NR], br[0:r, :],
                                      ALU.add).then_inc(l_ok, 1)

                def step(i, n, b):
                    r = rows_of(i)
                    first, last = isinstance(i, int) and i == 0, isinstance(i, int) and i == TP
                    if last:
                        dve.wait_ge(mod_s, 16 * 3 * NSEQ)
                    if not last:
                        low_y(i + 1)
                    gated(i, 0)
                    if not last:
                        bias_z(i + 1)
                    gated(i, 1)
                    if not first:
                        evac_h(i - 1)
                    if not last:
                        low_cat(i + 1)
                    if not first:
                        logits(i - 1)
                    dve.wait_ge(sq_ok, i + 1)
                    inv_sqrt(dve, c, rstd[0:r, :], ssq[0:r, :], 1.0 / D, newton[0:r, 0:1], newton[0:r, 1:2])
                    dve.wait_ge(h_mm, i)
                    dve.wait_ge(h2_out, 16 * i)
                    dve.scalar_tensor_tensor(out=h2[0:r, :], in0=x2[0:r, b, :], scalar=rstd[0:r, :], in1=gain[0:r, :],
                                             op0=ALU.mult, op1=ALU.mult).then_inc(xs_ok, 1)

                low_y(0)
                for n in range(NPART):
                    dve.wait_ge(w_h, n + 1)
                    dve.tensor_tensor(part(wglu_lo, wout_lo, n), raw_part(n), part(wglu_hi, wout_hi, n).bitcast(F32),
                                      ALU.subtract).then_inc(w_l, 1)
                    if n == 5:
                        dve.wait_ge(bglu_in, 16)
                        bias_z(0)
                low_cat(0)
                dve.wait_ge(mod_in, 16 * 7)
                step(0, 0, 0)
                prompt_loop(dve, 1, step, lambda j: c.at(INV + 2 * INV * j))
                c.at(15 * INV)
                step(15, 7, 1)
                step(16, 8, 0)
                evac_h(TP)
                logits(TP)


AHEAD = 4
COLS = NBLK + AHEAD + 1


def expert_weights(a):
    return [(t[0].rearrange("e (k p) n -> e p k n", p=P), k) for t, k in ((a.w1, KD), (a.w3, KD), (a.w2, DE // P))]


def load_run(sp, S, weights, run, q, n):
    e = sp.value_load(S.run_expert[0:1, ds(run, 1)], min_val=0, max_val=NE - 1)
    view, k = weights[n]
    sp.dma_start(S.raw[:, q, n, :].rearrange("p (k n) -> p k n", k=k),
                 view[ds(e, 1), :, :, :].rearrange("o p k n -> p (o k) n")).then_inc(S.w_in[n][q], 16)


def route(nc, S, a):
    with ExitStack() as st:
        sb, sem = S.sb, S.sem
        N2 = 2 * NT
        iota = sb(st, "iota", [P, P])
        tok = sb(st, "tok", [P, N2])
        w4 = sb(st, "w4", [P, EG])
        w32 = sb(st, "w32", [P, NE])
        e32 = sb(st, "e32", [P, NE])
        k128 = sb(st, "k128", [P, NT])
        upper = sb(st, "upper", [P, P])
        ones = sb(st, "ones", [P, P])
        zeros = sb(st, "zeros", [P, 2 * COLS])
        s1 = [sb(st, f"r_one{i}", [P, NT]) for i in range(8)]
        g4 = [sb(st, f"r_four{i}", [P, NT, EG]) for i in range(3)]
        em = sb(st, "r_em", [P, NT, NE])
        oh = [sb(st, f"r_oh{i}", [P, NT, NE]) for i in range(2)]
        picked = sb(st, "r_picked", [P, NT, NE])
        cum = sb(st, "r_cum", [P, NT, NE])
        tot = sb(st, "r_tot", [P, NT, NE])
        cnt, nb, pend, pst, act, rix, t32 = (sb(st, f"r_{n}", [P, NE]) for n in ("cnt", "nb", "pend", "pst", "act", "rix", "t32"))
        cmp17 = sb(st, "r_cmp", [P, NE, NT])
        dest = sb(st, "r_dest", [P, N2])
        bi = sb(st, "r_bi", [P, N2], I32)
        ji = sb(st, "r_ji", [P, N2], I32)
        bf = sb(st, "r_bf", [P, N2])
        jf = sb(st, "r_jf", [P, N2])
        gates = sb(st, "r_gates", [P, N2])
        NOH = 4
        ohj = sb(st, "r_ohj", [P, NOH, P])
        ohb = sb(st, "r_ohb", [P, NOH, 2, COLS])
        cols = sb(st, "r_cols", [P, 2])
        part_no = sb(st, "r_part", [P, 1])
        row = sb(st, "r_row", [1, COLS])
        newrun = sb(st, "r_new", [1, COLS - 1])
        pre = S.psum(st, "ps_pre", [P, 2, 512])
        pt = S.psum(st, "ps_tot", [P, 2, 512])
        acc = S.psum(st, "ps_slots", [P, 512])
        const_ok, ch, diff_ok, exp_ok = sem("const_ready"), sem("dve_chain4"), sem("diff_ready"), sem("exp_ready")
        one_ok, pre_mm, ohs_ok, acc_mm = sem("onehot_ready"), sem("counts_mm"), sem("slot_onehots"), sem("slots_mm")
        tables_ok, cols_ok, rows_mm = sem("tables_ready"), sem("table_columns"), sem("table_rows")
        ident = S.ident
        CUT = (0, 9, NT)
        lg = S.logits

        def assignments(eng, step):
            with eng.Fori(0, N2 // NOH) as j:
                for b in range(NOH):
                    step(NOH * j + b, b)
            for n in range(N2 // NOH * NOH, N2):
                step(n, n % NOH)

        s4, s32 = [P, NT, EG], [P, NT, NE]

        with nc.Block() as block:
            @block.gpsimd
            def _(pool):
                c = Steps(pool, const_ok)

                def iota_f(t, pattern, base, mult):
                    c.did(pool.iota(t, pattern, base=base, channel_multiplier=mult, allow_small_or_imprecise_dtypes=True))

                iota_f(iota[:, :], [[1, P]], 0, 0)
                iota_f(tok[:, :].rearrange("p (k i) -> p k i", k=2), [[0, 2], [P, NT]], 0, 1)
                iota_f(w4[:, :], [[-1, EG]], EG, 0)
                iota_f(w32[:, :], [[-1, NE]], NE, 0)
                iota_f(e32[:, :], [[1, NE]], 0, 0)
                iota_f(part_no[:, :], [[0, 1]], 0, 1)
                iota_f(k128[:, :], [[P, NT]], 0, 0)
                c.did(pool.memset(ones[:, :], 1.0))
                c.did(pool.memset(zeros[:, :], 0.0))
                c.link(pool.memset(upper[:, :], 1.0))
                c.did(pool.affine_select(out=upper[:, :], in_=upper[:, :], compare_op=ALU.is_gt, fill=0.0, base=0,
                                         pattern=[[1, P]], channel_multiplier=-1))
            @block.sync
            def _(sp):
                weights = expert_weights(a)
                sp.wait_ge(tables_ok, 1)
                runs = sp.value_load(S.n_blocks[0:1, 1:2], min_val=1, max_val=NE)
                for n in range(3):
                    load_run(sp, S, weights, 0, 0, n)
                with sp.If(1 < runs):
                    for n in range(3):
                        load_run(sp, S, weights, 1, 1, n)

            @block.scalar
            def _(act_):
                act_.wait_ge(diff_ok, 1)
                act_.activation(g4[1][:, :, :], g4[0][:, :, :], ACT.Exp).then_inc(exp_ok, 1)
                act_.wait_ge(diff_ok, 2)
                act_.activation(s1[5][:, :], s1[4][:, :], ACT.Exp).then_inc(exp_ok, 1)

            @block.tensor
            def _(pe):
                pe.wait_ge(const_ok, 11)
                pe.wait_ge(one_ok, 1)
                for i in range(2):
                    w = (CUT[i + 1] - CUT[i]) * NE
                    rhs = picked[:, CUT[i]:CUT[i + 1], :].rearrange("p i e -> p (i e)")
                    pe.matmul(pre[:, i, 0:w], upper[:, :], rhs, start=True, stop=True).then_inc(pre_mm, 1)
                    pe.matmul(pt[:, i, 0:w], ones[:, :], rhs, start=True, stop=True).then_inc(pre_mm, 1)
                pe.wait_ge(cols_ok, 1)
                for i in range(2):
                    last = pe.matmul(pre[0:1, 0, i * P:(i + 1) * P], cols[:, i:i + 1], ident[:, :], start=True, stop=True)
                last.then_inc(rows_mm, 1)
                out = acc[:, 0:2 * COLS]
                pe.matmul(out, ones[:, :], zeros[:, :], start=True, stop=False)
                pe.sem_inc(acc_mm, NOH)

                def scatter(n, b):
                    pe.wait_ge(ohs_ok, n + 1)
                    pe.matmul(out, ohj[:, b, :], ohb[:, b, :, :].rearrange("p t c -> p (t c)"),
                              start=False, stop=False).then_inc(acc_mm, 1)

                assignments(pe, scatter)
                pe.matmul(out, ones[:, :], zeros[:, :], start=False, stop=True).then_inc(acc_mm, 1)

            @block.vector
            def _(dve):
                c = Steps(dve, ch)

                def tt(out, x, y, op):
                    c.link(dve.tensor_tensor(out, x, y, op))

                def ts(out, x, v1, v2, op1, op2=ALU.bypass):
                    c.link(dve.tensor_scalar(out, x, v1, v2, op1, op2) if v2 is not None
                           else dve.tensor_scalar(out, x, v1, None, op1))

                def red(out, x, op):
                    c.link(dve.tensor_reduce(out, x, AX.X, op))

                def first_max(hot, x, weights, best, shape):
                    red(best, x, ALU.max)
                    tt(hot, x, fan(best, shape), ALU.is_equal)
                    tt(hot, hot, weights.unsqueeze(1).to_broadcast(shape), ALU.mult)
                    red(s1[7][:, :], hot, ALU.max)
                    tt(hot, hot, fan(s1[7][:, :], shape), ALU.is_equal)

                gmax, gsum, gw, m1, diff, ex, m2 = (t[:, :] for t in s1[:7])
                dve.wait_ge(const_ok, 11)
                c.link(dve.memset(lg[NS:P, TP, :], 0.0))
                gl, el = lg[:, :, 0:EG], lg[:, :, EG:NR]
                ohg = g4[2][:, :, :]
                first_max(ohg, gl, w4[:, :], gmax, s4)
                dve.tensor_tensor(g4[0][:, :, :], gl, fan(gmax, s4), ALU.subtract).then_inc(diff_ok, 1)
                ts(ohg, ohg, BIG, BIG, ALU.mult, ALU.subtract)
                e4 = em[:, :, :].rearrange("p i (g e) -> p i g e", g=EG)
                tt(e4, el.rearrange("p i (g e) -> p i g e", g=EG),
                   ohg.unsqueeze(3).to_broadcast([P, NT, EG, EPG]), ALU.add)
                hot = [t[:, :, :] for t in oh]
                first_max(hot[0], em[:, :, :], w32[:, :], m1, s32)
                c.link(dve.scalar_tensor_tensor(out=em[:, :, :], in0=hot[0], scalar=-BIG, in1=em[:, :, :], op0=ALU.mult, op1=ALU.add))
                first_max(hot[1], em[:, :, :], w32[:, :], m2, s32)
                dve.tensor_tensor(diff, m2, m1, ALU.subtract).then_inc(diff_ok, 1)
                for t in oh:
                    c.link(dve.memset(t[NS:P, TP, :], 0.0))
                dve.tensor_tensor(picked[:, :, :], hot[0], hot[1], ALU.add).then_inc(one_ok, 1)
                dve.wait_ge(exp_ok, 2)
                red(gsum, g4[1][:, :, :], ALU.add)
                c.link(dve.reciprocal(gw, gsum))
                ts(m1, ex, 1.0, None, ALU.add)
                c.link(dve.reciprocal(m1, m1))
                tt(gates[:, 0:NT], gw, m1, ALU.mult)
                tt(gates[:, NT:N2], gates[:, 0:NT], ex, ALU.mult)
                for k in range(2):
                    at = k * NT + TP
                    c.did(dve.memset(gates[NS:P, at:at + 1], 0.0))
                    c.link(dve.memset(tok[NS:P, at:at + 1], 0.0))
                dve.wait_ge(pre_mm, 4)
                for i in range(2):
                    w = (CUT[i + 1] - CUT[i]) * NE
                    c.link(dve.tensor_copy(tot[:, CUT[i]:CUT[i + 1], :].rearrange("p i e -> p (i e)"), pt[:, i, 0:w]))
                c.link(dve.memset(cum[:, 0, :], 0.0))
                for i in range(1, NT):
                    tt(cum[:, i, :], cum[:, i - 1, :], tot[:, i - 1, :], ALU.add)
                tt(cnt[:, :], cum[:, TP, :], tot[:, TP, :], ALU.add)
                tt(cmp17[:, :, :], fan(cnt[:, :], [P, NE, NT]), k128[:, :].unsqueeze(1).to_broadcast([P, NE, NT]), ALU.is_gt)
                red(nb[:, :], cmp17[:, :, :], ALU.add)
                c.link(dve.tensor_tensor_scan(pend[:, :], ones[:, 0:NE], nb[:, :], 0.0, ALU.mult, ALU.add))
                tt(pst[:, :], pend[:, :], nb[:, :], ALU.subtract)
                ts(t32[:, :], pst[:, :], float(P), None, ALU.mult)
                tt(cum[:, :, :], cum[:, :, :], t32[:, :].unsqueeze(1).to_broadcast(s32), ALU.add)
                for i in range(2):
                    w = (CUT[i + 1] - CUT[i]) * NE
                    part = cum[:, CUT[i]:CUT[i + 1], :].rearrange("p i e -> p (i e)")
                    tt(part, part, pre[:, i, 0:w], ALU.add)
                for k in range(2):
                    tt(picked[:, :, :], hot[k], cum[:, :, :], ALU.mult)
                    red(dest[:, k * NT:(k + 1) * NT], picked[:, :, :], ALU.add)
                c.link(dve.tensor_copy(S.dest[:, :], dest[:, :]))
                ts(bi[:, :], S.dest[:, :], 7, None, ALU.arith_shift_right)
                ts(ji[:, :], S.dest[:, :], P - 1, None, ALU.bitwise_and)
                c.link(dve.tensor_copy(bf[:, :], bi[:, :]))
                c.link(dve.tensor_copy(jf[:, :], ji[:, :]))
                ts(act[:, :], cnt[:, :], 0.0, None, ALU.is_gt)
                c.link(dve.tensor_tensor_scan(rix[:, :], ones[:, 0:NE], act[:, :], 0.0, ALU.mult, ALU.add))
                c.link(dve.tensor_copy(S.n_blocks[:, 0:1], pend[0:1, NE - 1:NE]))
                c.link(dve.tensor_copy(S.n_blocks[:, 1:2], rix[0:1, NE - 1:NE]))
                tt(t32[:, :], part_no[:, :].to_broadcast([P, NE]), pst[:, :], ALU.is_ge)
                tt(t32[:, :], t32[:, :], act[:, :], ALU.mult)
                red(cols[:, 0:1], t32[:, :], ALU.add)
                ts(t32[:, :], rix[:, :], -1.0, None, ALU.add)
                tt(t32[:, :], part_no[:, :].to_broadcast([P, NE]), t32[:, :], ALU.is_equal)
                tt(t32[:, :], t32[:, :], act[:, :], ALU.mult)
                tt(t32[:, :], t32[:, :], e32[:, :], ALU.mult)
                red(cols[:, 1:2], t32[:, :], ALU.add)
                dve.sem_inc(cols_ok, 1)
                dve.wait_ge(rows_mm, 1)
                ts(row[:, :], pre[0:1, 0, 0:COLS], -1.0, None, ALU.add)
                c.link(dve.tensor_copy(S.block_run[:, :], row[:, :]))
                new = newrun[:, :]
                tt(new, row[:, 1:COLS], row[:, 0:COLS - 1], ALU.subtract)
                ts(row[:, :], row[:, :], 1.0, None, ALU.add)
                tt(new, new, row[:, 1:COLS], ALU.mult)
                ts(row[:, 1:COLS], row[:, 1:COLS], rix[0:1, NE - 1:NE], None, ALU.is_lt)
                tt(new, new, row[:, 1:COLS], ALU.mult)
                c.link(dve.tensor_copy(S.block_split[:, 1:COLS], new))
                ts(row[:, 1:COLS], new, 2.0, None, ALU.add)
                ts(row[:, 1:COLS], row[:, 1:COLS], rix[0:1, NE - 1:NE], None, ALU.is_lt)
                tt(new, new, row[:, 1:COLS], ALU.mult)
                c.link(dve.tensor_copy(S.block_next[:, 1:COLS], new))
                c.link(dve.tensor_copy(S.run_expert[:, :], pre[0:1, 0, P:P + NE]))
                dve.sem_inc(tables_ok, 1)
                def one_hots(n, b):
                    dve.wait_ge(acc_mm, n + 1)
                    dve.tensor_scalar(ohj[:, b, :], iota[:, :], jf[:, ds(n, 1)], None, ALU.is_equal)
                    dve.tensor_scalar(ohb[:, b, 0, :], iota[:, 0:COLS], bf[:, ds(n, 1)], tok[:, ds(n, 1)],
                                      ALU.is_equal, ALU.mult)
                    dve.tensor_scalar(ohb[:, b, 1, :], iota[:, 0:COLS], bf[:, ds(n, 1)], gates[:, ds(n, 1)],
                                      ALU.is_equal, ALU.mult).then_inc(ohs_ok, 1)

                assignments(dve, one_hots)
                dve.wait_ge(acc_mm, NOH + N2 + 1)
                c.did(dve.tensor_copy(S.slot_tok[:, :], acc[:, 0:COLS]))
                c.link(dve.tensor_copy(S.slot_gate[:, :], acc[:, COLS:2 * COLS]))


def experts(nc, S, a):
    with ExitStack() as st:
        sb, sem = S.sb, S.sem
        KH = DE // P
        up_hi = sb(st, "up_hi", [P, 2, KD, 2, DE], F32R)
        up_lo = sb(st, "up_lo", [P, 2, KD, 2, DE], F32R)
        down_hi = sb(st, "down_hi", [P, 2, KH, D], F32R)
        down_lo = sb(st, "down_lo", [P, 2, KH, D], F32R)
        xg = sb(st, "xg", [P, AHEAD, D])
        xT_hi = sb(st, "xT_hi", [P, 2, KD, P], F32R)
        xT_lo = sb(st, "xT_lo", [P, 2, KD, P], F32R)
        idx = sb(st, "idx", [P, AHEAD], I32)
        gcol = sb(st, "gcol", [P, 2])
        act_v = sb(st, "silu", [P, DE])
        hid = sb(st, "hid", [P, DE])
        hT_hi = sb(st, "hidT_hi", [P, KH, P], F32R)
        hT_lo = sb(st, "hidT_lo", [P, KH, P], F32R)
        yo = sb(st, "yo", [P, 2, D])
        pX = S.psum(st, "ps_xT", [P, 2, 512])
        pU = S.psum(st, "ps_up", [P, 512])
        pT = S.psum(st, "ps_hidT", [P, 512])
        pY = S.psum(st, "ps_y", [P, 2, 512])
        ident = S.ident

        raw, w_in, weights = S.raw, S.w_in, expert_weights(a)
        g_in, y_out = [sem(f"gathered{i}") for i in range(AHEAD)], [sem("y_row_stored0"), sem("y_row_stored1")]
        up_h, up_l, down_h, down_l = sem("up_hi_ready"), sem("up_lo_ready"), sem("down_hi_ready"), sem("down_lo_ready")
        idx_ok, x_mm, x_a, x_d, u_mm, s_ok, h_ok, t_mm, t_a, t_d, y_mm, y_a, y_d, gc_ok = (sem(n) for n in (
            "idx_ready", "x_mm", "x_hi_ready", "x_lo_ready", "up_mm", "silu_ok", "hid_ok", "hid_mm", "hidT_hi_ready",
            "hidT_lo_ready", "down_mm", "y_act", "y_dve", "gate_col"))
        tail, gathers_end, seen = sem("experts_end"), sem("gathers_end"), sem("sync_waits")
        idx_seen = sem("idx_seen")

        def blocks(eng, step):
            n = eng.value_load(S.n_blocks[0:1, 0:1], min_val=FULL, max_val=NBLK)
            for t in range(1, AHEAD + 1):
                step(t, 0, t)
            with eng.Fori(1, NBLK // AHEAD) as j:
                for t in range(1, AHEAD + 1):
                    with eng.If(AHEAD * j + t <= n):
                        step(AHEAD * j + t, j, t)
            return n

        def up_piece(t, run, m):
            ks, n = slice(m % 2 * KD // 2, (m % 2 + 1) * KD // 2), m // 2
            if isinstance(run, int):
                return t[:, run % 2, ks, n, :]
            return t[:, ds(run % 2, 1), ks, n, :].rearrange("p o k n -> p (o k) n")

        def down_piece(t, run, m):
            if isinstance(run, int):
                return t[:, run % 2, m, :]
            return t[:, ds(run % 2, 1), m, :].rearrange("p o n -> p (o n)")

        def raw_piece(run, n, m, k):
            cols = slice(m * KD * DE // 2, (m + 1) * KD * DE // 2)
            r = raw[:, run % 2, n, cols] if isinstance(run, int) else raw[:, ds(run % 2, 1), n, cols].rearrange("p o n -> p (o n)")
            return r if k == 1 else r.rearrange("p (k n) -> p k n", k=k)

        def wait_raw(eng, n, run):
            for q in range(2):
                if not isinstance(run, int):
                    eng.wait_ge(w_in[n][q], 16 * ((run + (2 - q)) // 2))
                elif run >= q:
                    eng.wait_ge(w_in[n][q], 16 * ((run + 2 - q) // 2))

        def split_next(eng, b, body):
            run = eng.value_load(S.block_split[0:1, ds(b, 1)], min_val=0, max_val=NE - 1)
            with eng.If(run > 0):
                body(run)

        def split_down_next(eng, b, body):
            if not (isinstance(b, int) and b == 1):
                split_next(eng, b - 1, body)

        with nc.Block() as block:
            @block.sync
            def _(sp):
                runs = sp.value_load(S.n_blocks[0:1, 1:2], min_val=1, max_val=NE)

                def load(run, ns, gone):
                    for n in ns:
                        sp.wait_ge((up_l, up_l, down_l)[n], (4, 4, KH)[n] * gone + (2, 4, KH)[n])
                        sp.sem_inc(seen, 1)
                        if isinstance(run, int):
                            load_run(sp, S, weights, run, run % 2, n)
                        else:
                            for q in range(2):
                                with sp.If(gone % 2 == q):
                                    load_run(sp, S, weights, run, q, n)

                def load_next(b, ns):
                    gone = sp.value_load(S.block_next[0:1, ds(b, 1)], min_val=0, max_val=NE - 3)
                    with sp.If(gone > 0):
                        load(gone + 2, ns, gone)

                def step(b, j, t):
                    load_next(b, (0, 1))
                    sp.wait_ge(y_a, b)
                    sp.wait_ge(y_d, b)
                    sp.sem_inc(seen, 1)
                    sp.dma_start(S.yb_d[ds(b * P - P, P), :], yo[:, (t + 1) % 2, :]).then_inc(y_out[(t + 1) % 2], 16)
                    if not (isinstance(b, int) and b == 1):
                        load_next(b - 1, (2,))

                for run in (2, 3):
                    with sp.If(run < runs):
                        load(run, range(3), run - 2)
                n = blocks(sp, step)
                for q in range(2):
                    sp.wait_ge(y_out[q], 16 * ((n + (1 - q)) // 2))
                    sp.sem_inc(tail, 1)

            @block.gpsimd
            def _(pool):
                def gather(b, par):
                    pool.tensor_copy(idx[:, par:par + 1], S.slot_tok[:, ds(b, 1)]).then_inc(idx_ok, 1)
                    pool.wait_ge(idx_ok, b + 1)
                    pool.sem_inc(idx_seen, 1)
                    pool.indirect_dma_start(out=xg[:, par, :], out_offset=None, in_=S.h2_d,
                                            in_offset=bass.IndirectOffsetOnAxis(ap=idx[:, par:par + 1], axis=0)).then_inc(g_in[par], 16)

                def split_down(run):
                    for m in range(KH):
                        pool.wait_ge(down_h, KH * run + m + 1)
                        pool.tensor_tensor(down_piece(down_lo, run, m), raw_piece(run, 2, m, 1),
                                           down_piece(down_hi, run, m).bitcast(F32), ALU.subtract).then_inc(down_l, 1)

                def step(b, j, t):
                    pool.wait_ge(x_mm, b + 1)
                    gather(b + AHEAD, t % AHEAD)
                    split_down_next(pool, b, split_down)

                for b in range(AHEAD):
                    gather(b, b)
                split_down(0)
                pool.wait_ge(x_mm, 1)
                gather(AHEAD, 0)
                runs = pool.value_load(S.n_blocks[0:1, 1:2], min_val=1, max_val=NE)
                with pool.If(1 < runs):
                    split_down(1)
                n = blocks(pool, step)
                for q in range(AHEAD):
                    pool.wait_ge(g_in[q], 16 * ((n + (2 * AHEAD - q)) // AHEAD))
                    pool.sem_inc(gathers_end, 1)

            @block.tensor
            def _(pe):
                def turn_x(b, n, q):
                    pe.wait_ge(g_in[q], 16 * n + 16)
                    if not (isinstance(b, int) and b == 0):
                        pe.wait_ge(x_d, 2 * b)
                    for k in range(KD):
                        last = pe.transpose(pX[:, k // 4, k % 4 * P:(k % 4 + 1) * P], xg[:, q, k * P:(k + 1) * P], ident[:, :])
                    last.then_inc(x_mm, 1)

                def run_of(b):
                    return pe.value_load(S.block_run[0:1, ds(b, 1)], min_val=0, max_val=NE - 1)

                def up_mm(b, par, run):
                    pe.wait_ge(up_l, 4 * run + 4)
                    pe.wait_ge(x_d, 2 * b + 2)
                    if not (isinstance(b, int) and b == 0):
                        pe.wait_ge(h_ok, b)
                    half = pe.snap(run % 2)
                    split_matmul(pe, pU[:, :], lambda t, k: (xT_hi, xT_lo)[t][:, par, k, :],
                                 lambda t, k: (up_hi, up_lo)[t][:, ds(half, 1), k, :, :].rearrange("p o t n -> p (o t n)"),
                                 KD).then_inc(u_mm, 1)

                def down_mm(b, run):
                    pe.wait_ge(down_l, KH * run + KH)
                    pe.wait_ge(t_d, b + 1)
                    if not (isinstance(b, int) and b == 0):
                        pe.wait_ge(y_a, b)
                        pe.wait_ge(y_d, b)
                    half = pe.snap(run % 2)
                    for c in range(2):
                        last = split_matmul(pe, pY[:, c, :], lambda t, k: (hT_hi, hT_lo)[t][:, k, :],
                                            lambda t, k: (down_hi, down_lo)[t][:, ds(half, 1), k, c * 512:(c + 1) * 512].rearrange(
                                                "p o n -> p (o n)"), KH)
                    last.then_inc(y_mm, 1)

                def turn_hid(b):
                    pe.wait_ge(h_ok, b + 1)
                    for k in range(KH):
                        last = pe.transpose(pT[:, k * P:(k + 1) * P], hid[:, k * P:(k + 1) * P], ident[:, :])
                    last.then_inc(t_mm, 1)

                def step(b, j, t):
                    turn_x(b + 1, j + (t + 1) // AHEAD, (t + 1) % AHEAD)
                    up_mm(b, t % 2, run_of(b))
                    down_mm(b - 1, run_of(b - 1))
                    turn_hid(b)

                turn_x(0, 0, 0)
                turn_x(1, 0, 1)
                up_mm(0, 0, run_of(0))
                turn_hid(0)
                blocks(pe, step)

            @block.scalar
            def _(act):
                def evac_x(b, par):
                    act.wait_ge(x_mm, b + 1)
                    for h in range(2):
                        act.activation(xT_hi[:, par, 4 * h:4 * h + 4, :], pX[:, h, :].rearrange("p (k t) -> p k t", k=4),
                                       ACT.Copy).then_inc(x_a, 1)

                def split_up(run):
                    for m in range(4):
                        if m % 2 == 0:
                            wait_raw(act, m // 2, run)
                        act.activation(up_piece(up_hi, run, m), raw_piece(run, m // 2, m % 2, KD // 2), ACT.Copy).then_inc(up_h, 1)

                def split_down(run):
                    wait_raw(act, 2, run)
                    for m in range(KH):
                        act.activation(down_piece(down_hi, run, m), raw_piece(run, 2, m, 1), ACT.Copy).then_inc(down_h, 1)

                def silu(b):
                    act.wait_ge(u_mm, b + 1)
                    act.activation(act_v[:, :], pU[:, 0:DE], ACT.Silu).then_inc(s_ok, 1)

                def evac_hid(b):
                    act.wait_ge(t_mm, b + 1)
                    act.activation(hT_hi[:, :, :], pT[:, 0:DE].rearrange("p (k t) -> p k t", k=KH), ACT.Copy).then_inc(t_a, 1)

                def out(b, n, par):
                    act.wait_ge(y_mm, b + 1)
                    act.wait_ge(gc_ok, b + 1)
                    if not (isinstance(n, int) and n == 0):
                        act.wait_ge(y_out[par], 16 * n)
                    act.activation(yo[:, par, 0:512], pY[:, 0, :], ACT.Copy, scale=gcol[:, par:par + 1]).then_inc(y_a, 1)

                def step(b, j, t):
                    evac_x(b + 1, (t + 1) % 2)
                    split_next(act, b, split_up)
                    silu(b)
                    split_down_next(act, b, split_down)
                    out(b - 1, AHEAD // 2 * j + (t - 1) // 2, (t + 1) % 2)
                    evac_hid(b)

                evac_x(0, 0)
                split_up(0)
                evac_x(1, 1)
                split_down(0)
                silu(0)
                evac_hid(0)
                runs = act.value_load(S.n_blocks[0:1, 1:2], min_val=1, max_val=NE)
                with act.If(1 < runs):
                    split_up(1)
                    split_down(1)
                blocks(act, step)

            @block.vector
            def _(dve):
                def evac_x(b, par):
                    for h in range(2):
                        dve.wait_ge(x_a, 2 * b + h + 1)
                        ks = slice(4 * h, 4 * h + 4)
                        dve.tensor_tensor(xT_lo[:, par, ks, :], pX[:, h, :].rearrange("p (k t) -> p k t", k=4),
                                          xT_hi[:, par, ks, :].bitcast(F32), ALU.subtract).then_inc(x_d, 1)

                def split_up(run):
                    for m in range(4):
                        dve.wait_ge(up_h, 4 * run + m + 1)
                        dve.tensor_tensor(up_piece(up_lo, run, m), raw_piece(run, m // 2, m % 2, KD // 2),
                                          up_piece(up_hi, run, m).bitcast(F32), ALU.subtract).then_inc(up_l, 1)

                def hidden(b):
                    dve.wait_ge(s_ok, b + 1)
                    dve.tensor_tensor(hid[:, :], act_v[:, :], pU[:, DE:2 * DE], ALU.mult).then_inc(h_ok, 1)

                def evac_hid(b):
                    dve.wait_ge(t_a, b + 1)
                    dve.tensor_tensor(hT_lo[:, :, :], pT[:, 0:DE].rearrange("p (k t) -> p k t", k=KH),
                                      hT_hi[:, :, :].bitcast(F32), ALU.subtract).then_inc(t_d, 1)

                def out(b, n, par):
                    dve.wait_ge(gc_ok, b + 1)
                    dve.wait_ge(y_mm, b + 1)
                    if not (isinstance(n, int) and n == 0):
                        dve.wait_ge(y_out[par], 16 * n)
                    dve.tensor_scalar(yo[:, par, 512:D], pY[:, 1, :], gcol[:, par:par + 1], None, ALU.mult).then_inc(y_d, 1)

                def step(b, j, t):
                    prev = (t + 1) % 2
                    dve.tensor_copy(gcol[:, prev:prev + 1], S.slot_gate[:, ds(b - 1, 1)]).then_inc(gc_ok, 1)
                    evac_x(b + 1, prev)
                    split_next(dve, b, split_up)
                    hidden(b)
                    out(b - 1, AHEAD // 2 * j + (t - 1) // 2, prev)
                    evac_hid(b)

                evac_x(0, 0)
                split_up(0)
                evac_x(1, 1)
                hidden(0)
                evac_hid(0)
                runs = dve.value_load(S.n_blocks[0:1, 1:2], min_val=1, max_val=NE)
                with dve.If(1 < runs):
                    split_up(1)
                blocks(dve, step)


def final(nc, S, a, o):
    with ExitStack() as st:
        sb, sem = S.sb, S.sem
        NB = 4
        gate = sb(st, "gate2", [P, D])
        gf = sb(st, "gf", [P, D])
        yg = sb(st, "yg", [P, NB, 2, D])
        idx = sb(st, "idx2", [P, NB, 2], I32)
        x3 = sb(st, "x3", [P, NB, D])
        junk = sb(st, "junk4", [P, D])
        out = sb(st, "out_rows", [P, NB, D])
        ssq = sb(st, "ssq3", [P, NB])
        rstd = sb(st, "rstd3", [P, 1])
        newton = sb(st, "newton3", [P, 2])
        mod_in, mod_s, idx_ok, mul_ok, x_ok, sq_ok, o_ok, ch = (sem(n) for n in (
            "mod3_loaded", "mod3_sample_loaded", "idx2_ready", "rows_gated", "x3_ready", "ssq3_ready",
            "out_ready", "dve_chain5"))
        s1_ok, idx_seen = sem("rows_added"), sem("idx2_seen")
        x_in, y_in, o_out = ([sem(f"{n}{i}") for i in range(NB)] for n in ("x2_loaded", "rows_gathered", "out_stored"))

        def rows_of(i):
            return NS if isinstance(i, int) and i == TP else P

        def tiles(eng, step, at=None):
            for i in range(NB):
                step(i, 0, i)
            with eng.Fori(1, TP // NB - 1) as j:
                if at is not None:
                    at(NB * j)
                for b in range(NB):
                    step(NB * j + b, j, b)
            if at is not None:
                at(TP - NB)
            for i in range(TP - NB, NT):
                step(i, i // NB, i % NB)

        with nc.Block() as block:
            @block.sync
            def _(sp):
                def load(i, b):
                    rows = S.x2_d[TP * P:TOK, :] if rows_of(i) == NS else S.x2_d[ds(i * P, P), :]
                    sp.dma_start(x3[0:rows_of(i), b, :], rows).then_inc(x_in[b], 16)

                load(0, 0)
                sp.dma_start(gate[:, :], S.ada_d[0:1, 5 * D:6 * D].to_broadcast([P, D])).then_inc(mod_in, 16)
                sp.dma_start(gf[:, :], a.g_final.to_broadcast([P, D])).then_inc(mod_in, 16)
                for i in range(1, NB):
                    load(i, i)

                def step(i, n, b):
                    if isinstance(i, int) and i == TP - 1:
                        sp.wait_ge(mul_ok, TP)
                        for q in range(NSEQ):
                            sp.dma_start(gate[q * DSEQ:(q + 1) * DSEQ, :],
                                         S.ada_d[1 + q:2 + q, 5 * D:6 * D].to_broadcast([DSEQ, D])).then_inc(mod_s, 16)
                    sp.wait_ge(o_ok, i + 1)
                    if rows_of(i) == NS:
                        sp.dma_start(o.y_sample.rearrange("b t d -> (b t) d"), out[0:NS, b, :]).then_inc(o_out[b], 16)
                    else:
                        sp.dma_start(o.y_prompt[0, ds(i * P, P), :], out[:, b, :]).then_inc(o_out[b], 16)
                    if not isinstance(i, int) or i + NB < NT:
                        load(i + NB, b)

                tiles(sp, step)
                for b in range(NB):
                    sp.wait_ge(o_out[b], 16 * ((NT - 1 - b) // NB + 1))

            @block.gpsimd
            def _(pool):
                def gather(i, b):
                    r = rows_of(i)
                    for k in range(2):
                        pool.tensor_copy(idx[0:r, b, k:k + 1], S.dest[0:r, ds(i + k * NT, 1)]).then_inc(idx_ok, 1)
                    pool.wait_ge(idx_ok, 2 * i + 2)
                    pool.sem_inc(idx_seen, 1)
                    for k in range(2):
                        pool.indirect_dma_start(out=yg[0:r, b, k, :], out_offset=None, in_=S.yb_d,
                                                in_offset=bass.IndirectOffsetOnAxis(ap=idx[0:r, b, k:k + 1], axis=0)).then_inc(y_in[b], 16)

                def step(i, n, b):
                    r = rows_of(i)
                    if not isinstance(i, int) or i + NB - 1 < NT:
                        if not (isinstance(i, int) and i == 0):
                            pool.wait_ge(x_ok, i)
                        gather(i + NB - 1, (b + NB - 1) % NB)
                    pool.wait_ge(mul_ok, i + 1)
                    pool.wait_ge(x_in[b], 16 * n + 16)
                    pool.tensor_tensor(x3[0:r, b, :], x3[0:r, b, :], yg[0:r, b, 0, :], ALU.add).then_inc(x_ok, 1)

                for i in range(NB - 1):
                    gather(i, i)
                tiles(pool, step)

            @block.scalar
            def _(act):
                def step(i, n, b):
                    r = rows_of(i)
                    act.wait_ge(sq_ok, i)
                    act.wait_ge(x_ok, i + 1)
                    act.activation(junk[0:r, :], x3[0:r, b, :], ACT.Square, accum_out=ssq[0:r, b:b + 1]).then_inc(sq_ok, 1)

                tiles(act, step)

            @block.vector
            def _(dve):
                c = Steps(dve, ch)

                def rows_in(i, n, b):
                    r = rows_of(i)
                    if isinstance(i, int) and i == TP:
                        dve.wait_ge(mod_s, 16 * NSEQ)
                    dve.wait_ge(y_in[b], 32 * n + 32)
                    y0, y1 = yg[0:r, b, 0, :], yg[0:r, b, 1, :]
                    dve.tensor_tensor(y1, y0, y1, ALU.add).then_inc(s1_ok, 1)
                    dve.wait_ge(s1_ok, i + 1)
                    dve.tensor_tensor(y0, y1, gate[0:r, :], ALU.mult).then_inc(mul_ok, 1)

                def norm(i, n, b):
                    r = rows_of(i)
                    dve.wait_ge(sq_ok, i + 1)
                    inv_sqrt(dve, c, rstd[0:r, :], ssq[0:r, b:b + 1], 1.0 / D, newton[0:r, 0:1], newton[0:r, 1:2])
                    if not (isinstance(n, int) and n == 0):
                        dve.wait_ge(o_out[b], 16 * n)
                    dve.scalar_tensor_tensor(out=out[0:r, b, :], in0=x3[0:r, b, :], scalar=rstd[0:r, :], in1=gf[0:r, :],
                                             op0=ALU.mult, op1=ALU.mult).then_inc(o_ok, 1)

                def step(i, n, b):
                    if not (isinstance(i, int) and i == TP):
                        rows_in(i + 1, n + (b + 1) // NB, (b + 1) % NB)
                    norm(i, n, b)

                dve.wait_ge(mod_in, 32)
                rows_in(0, 0, 0)
                tiles(dve, step, lambda i: c.at(INV * i))


_INS = ['x_prompt', 'x_sample', 'state_ssm_re', 'state_ssm_im', 'c_prompt', 'c_sample', 'w_ada', 'b_ada',
        'g_norm1', 'g_norm2', 'w_in', 'ln_g', 'ln_b', 'w_s', 'b_s', 'lam_re', 'lam_im', 'log_dt',
        'ssm_b_re', 'ssm_b_im', 'ssm_c_re', 'ssm_c_im', 'ssm_d', 'w_glu', 'b_glu', 'w_out',
        'w_group', 'b_group', 'w_expert', 'b_expert', 'w1', 'w3', 'w2', 'g_final']
_OUTS = [('y_prompt', (1, SEQ, D)), ('y_sample', (NSEQ, DSEQ, D)),
         ('ssm_re_prompt', (1, 1, G, ST)), ('ssm_im_prompt', (1, 1, G, ST)),
         ('ssm_re_sample', (1, NSEQ, G, ST)), ('ssm_im_sample', (1, NSEQ, G, ST)),
         ('v_sample', (1, NSEQ, DSEQ, DA))]


def kernel(**inputs):
    import concourse.bacc as _bacc
    from concourse.bass_utils import run_bass_kernel_spmd as _run

    nc = _bacc.Bacc("TRN2", target_bir_lowering=False, num_devices=1)
    arrays, ins, outs = {}, {}, {}
    for name in _INS:
        x = np.ascontiguousarray(inputs[name])
        if x.ndim == 1:
            x = x.reshape(1, -1)
        arrays[f"in_{name}"] = x
        ins[name] = nc.dram_tensor(f"in_{name}", x.shape, mybir.dt.from_np(x.dtype), kind="ExternalInput").ap()
    for name, shape in _OUTS:
        outs[name] = nc.dram_tensor(f"out_{name}", shape, F32, kind="ExternalOutput").ap()
    build(nc, Inputs(ins), Outputs(outs))
    r = _run(nc, [arrays], core_ids=[0])
    return tuple(r.results[0][f"out_{name}"] for name, _ in _OUTS)
```
